# Optimizing a Trainium2 kernel written in Bass

```python
import math
import jax
import jax.numpy as jnp
from jax import lax
import numpy as np

D_MODEL = 1024
BATCH = 1
SEQ = 256
DEPTH = 2
DEC_BATCH = 1
DEC_SEQ = 1024
PAST_LEN = 256

GRID_W = 64
HEAD_DIM = 64
A_HEADS = 8
A_KV_HEADS = 2
A_GROUP = A_HEADS // A_KV_HEADS
A_WIDTH = A_HEADS * HEAD_DIM
B_HEADS = 4
B_QK_DIM = 32
B_V_DIM = 64
B_WIDTH = B_HEADS * B_V_DIM
C_HEADS = 4
C_DK = 32
C_DV = 64
C_WIDTH = C_HEADS * C_DV
GATE_RANK = 16
GLA_TAU = 16.0
CHUNK = 64
D_MIX = A_WIDTH + B_WIDTH + C_WIDTH
Q_BLOCK = 128
ROPE_THETA = 10000.0
EPS = 1e-6
IN_SIZES = (A_WIDTH, A_KV_HEADS * HEAD_DIM, A_KV_HEADS * HEAD_DIM,
            B_HEADS * 2 * B_QK_DIM, B_HEADS * 2 * B_QK_DIM, B_WIDTH,
            C_HEADS * C_DK, C_HEADS * C_DK, C_WIDTH, 2 * GATE_RANK, D_MIX)
IN_WIDTH = sum(IN_SIZES)

kernel_name = 'hybrid_diffusion_parallel_heads_step'

def rms_norm(x, g):
    xf = x.astype(jnp.float32)
    y = xf * lax.rsqrt(jnp.mean(xf * xf, axis=-1, keepdims=True) + EPS)
    return (y * g.astype(jnp.float32)).astype(x.dtype)

def split_heads(t, n_heads):
    b, l, _ = t.shape
    return t.reshape(b, l, n_heads, -1).transpose(0, 2, 1, 3)

def merge_heads(t):
    b, n, l, d = t.shape
    return t.transpose(0, 2, 1, 3).reshape(b, l, n * d)

def rope_1d(x, pos):
    half = x.shape[-1] // 2
    freq = ROPE_THETA ** (-jnp.arange(half, dtype=jnp.float32) / half)
    ang = pos.astype(jnp.float32)[:, None] * freq[None, :]
    cos, sin = jnp.cos(ang), jnp.sin(ang)
    xf = x.astype(jnp.float32)
    x1, x2 = xf[..., :half], xf[..., half:]
    return jnp.concatenate([x1 * cos - x2 * sin, x2 * cos + x1 * sin], axis=-1)

def rope_2d(x, pos_row, pos_col):
    d = x.shape[-1] // 2
    return jnp.concatenate([rope_1d(x[..., :d], pos_row), rope_1d(x[..., d:], pos_col)], axis=-1).astype(x.dtype)

def sweep_query_blocks(attend, q):
    lead = q.shape[:-2]
    lq, d = q.shape[-2], q.shape[-1]
    nb = lq // Q_BLOCK
    qb = jnp.moveaxis(q.reshape(*lead, nb, Q_BLOCK, d), -3, 0)
    ob = lax.map(attend, qb)
    return jnp.moveaxis(ob, 0, -3).reshape(*lead, lq, ob.shape[-1])

def gqa_attention(q, k, v):
    scale = q.shape[-1] ** -0.5

    def attend(qb):
        s = jnp.einsum('bkgqd,bksd->bkgqs', qb, k).astype(jnp.float32) * scale
        p = jax.nn.softmax(s, axis=-1).astype(v.dtype)
        return jnp.einsum('bkgqs,bksd->bkgqd', p, v)

    return sweep_query_blocks(attend, q)

def diff_attention(q, k, v, lam):
    scale = B_QK_DIM ** -0.5
    k1, k2 = k[..., :B_QK_DIM], k[..., B_QK_DIM:]
    lam32 = lam.astype(jnp.float32)

    def attend(qb):
        s1 = jnp.einsum('bhqd,bhsd->bhqs', qb[..., :B_QK_DIM], k1).astype(jnp.float32) * scale
        s2 = jnp.einsum('bhqd,bhsd->bhqs', qb[..., B_QK_DIM:], k2).astype(jnp.float32) * scale
        a = jax.nn.softmax(s1, axis=-1) - lam32 * jax.nn.softmax(s2, axis=-1)
        return jnp.einsum('bhqs,bhsd->bhqd', a.astype(v.dtype), v)

    return sweep_query_blocks(attend, q)

def gla_scan(q, k, v, g, s0):
    b, h, l, _ = q.shape
    n = l // CHUNK

    def to_chunks(t):
        return jnp.moveaxis(t.reshape(b, h, n, CHUNK, t.shape[-1]), 2, 0)

    mask = jnp.tril(jnp.ones((CHUNK, CHUNK), dtype=bool))

    def step(s, inp):
        qc, kc, vc, gc = inp
        cum = jnp.cumsum(gc, axis=-2)
        q_t = qc * jnp.exp(cum)
        k_t = kc * jnp.exp(-cum)
        a = jnp.where(mask, jnp.einsum('bhid,bhjd->bhij', q_t, k_t), 0.0)
        o = jnp.einsum('bhid,bhde->bhie', q_t, s) + jnp.einsum('bhij,bhje->bhie', a, vc)
        last = cum[..., -1:, :]
        s_new = jnp.exp(last)[..., 0, :, None] * s + jnp.einsum('bhjd,bhje->bhde', kc * jnp.exp(last - cum), vc)
        return s_new, o

    s_fin, o = lax.scan(step, s0, (to_chunks(q), to_chunks(k), to_chunks(v), to_chunks(g)))
    o = jnp.moveaxis(o, 0, 2).reshape(b, h, l, v.shape[-1])
    return o, s_fin

def gla_bidirectional(q, k, v, g_f, g_b, s_f0, s_b0):
    o_f, s_f = gla_scan(q, k, v, g_f, s_f0)
    flip = lambda t: jnp.flip(t, axis=2)
    o_b, s_b = gla_scan(flip(q), flip(k), flip(v), flip(g_b), s_b0)
    return o_f + flip(o_b), s_f, s_b

def trunk_layer(x, mod, lp, lam, lam_init, pos, ctx):
    (g_pre, g_post, w_in, w_out, a_q_gain, a_k_gain, b_out_gain,
     c_w_f, c_b_f, c_w_b, c_b_b, c_out_gain) = lp
    bsz, l, _ = x.shape
    f32 = jnp.float32
    shift, scale, gate = jnp.split(mod, 3, axis=-1)
    h = rms_norm(x, g_pre) * (1.0 + scale[:, None, :]) + shift[:, None, :]
    z = h @ w_in
    (a_q, a_k, a_v, b_q, b_k, b_v, c_q, c_k, c_v, c_lr, u) = jnp.split(
        z, np.cumsum(IN_SIZES)[:-1].tolist(), axis=-1)

    a_q = rms_norm(split_heads(a_q, A_HEADS), a_q_gain)
    a_k = rms_norm(split_heads(a_k, A_KV_HEADS), a_k_gain)
    a_v = split_heads(a_v, A_KV_HEADS)
    b_q = split_heads(b_q, B_HEADS)
    b_k = split_heads(b_k, B_HEADS)
    b_v = split_heads(b_v, B_HEADS)
    c_q = split_heads(c_q, C_HEADS).astype(f32) * (C_DK ** -0.5)
    c_k = split_heads(c_k, C_HEADS).astype(f32)
    c_v = split_heads(c_v, C_HEADS).astype(f32)
    g_f = split_heads(jax.nn.log_sigmoid((c_lr[..., :GATE_RANK] @ c_w_f + c_b_f).astype(f32)) / GLA_TAU, C_HEADS)
    g_b = split_heads(jax.nn.log_sigmoid((c_lr[..., GATE_RANK:] @ c_w_b + c_b_b).astype(f32)) / GLA_TAU, C_HEADS)

    if ctx is None:
        a_k_all, a_v_all, b_k_all, b_v_all = a_k, a_v, b_k, b_v
        s_f0 = jnp.zeros((bsz, C_HEADS, C_DK, C_DV), f32)
        s_b0 = jnp.zeros((bsz, C_HEADS, C_DK, C_DV), f32)
    else:
        pos_row, pos_col = pos
        ck_a, cv_a, ck_b, cv_b, cs_f, cs_b = ctx
        a_q = rope_2d(a_q, pos_row, pos_col)
        a_k = rope_2d(a_k, pos_row, pos_col)
        b_q = jnp.concatenate([rope_2d(b_q[..., :B_QK_DIM], pos_row, pos_col),
                               rope_2d(b_q[..., B_QK_DIM:], pos_row, pos_col)], axis=-1)
        b_k = jnp.concatenate([rope_2d(b_k[..., :B_QK_DIM], pos_row, pos_col),
                               rope_2d(b_k[..., B_QK_DIM:], pos_row, pos_col)], axis=-1)
        a_k_all = jnp.concatenate([ck_a.astype(a_k.dtype), a_k], axis=2)
        a_v_all = jnp.concatenate([cv_a.astype(a_v.dtype), a_v], axis=2)
        b_k_all = jnp.concatenate([ck_b.astype(b_k.dtype), b_k], axis=2)
        b_v_all = jnp.concatenate([cv_b.astype(b_v.dtype), b_v], axis=2)
        s_f0 = cs_f.astype(f32)
        s_b0 = cs_b.astype(f32)

    o_a = gqa_attention(a_q.reshape(bsz, A_KV_HEADS, A_GROUP, l, HEAD_DIM), a_k_all, a_v_all)
    o_a = o_a.reshape(bsz, A_HEADS, l, HEAD_DIM)
    o_b = rms_norm(diff_attention(b_q, b_k_all, b_v_all, lam), b_out_gain) * (1.0 - lam_init)
    o_c, s_f, s_b = gla_bidirectional(c_q, c_k, c_v, g_f, g_b, s_f0, s_b0)
    o_c = rms_norm(o_c.astype(x.dtype), c_out_gain)

    mixed = jnp.concatenate([merge_heads(o_a), merge_heads(o_b), merge_heads(o_c)], axis=-1) * jax.nn.silu(u)
    y = mixed @ w_out
    x_new = x + gate[:, None, :] * rms_norm(y, g_post)
    if ctx is None:
        return x_new, (a_k, a_v, b_k, b_v, s_f.astype(x.dtype), s_b.astype(x.dtype))
    return x_new, None

def setup_inputs(seed: int = 0) -> dict:
    key = jax.random.key(seed)
    ks = jax.random.split(key, 28)
    f32 = jnp.float32

    def nrm(k, shape, s):
        return jax.random.normal(k, shape, f32) * s

    return {
        'x_prompt': nrm(ks[0], (BATCH, SEQ, D_MODEL), 1.0),
        'x_sample': nrm(ks[1], (DEC_BATCH, DEC_SEQ, D_MODEL), 1.0),
        'c': nrm(ks[2], (DEC_BATCH, D_MODEL), 1.0),
        'cache_a_k': nrm(ks[3], (DEC_BATCH, DEPTH, A_KV_HEADS, PAST_LEN, HEAD_DIM), 1.0),
        'cache_a_v': nrm(ks[4], (DEC_BATCH, DEPTH, A_KV_HEADS, PAST_LEN, HEAD_DIM), 1.0),
        'cache_b_k': nrm(ks[5], (DEC_BATCH, DEPTH, B_HEADS, PAST_LEN, 2 * B_QK_DIM), 1.0),
        'cache_b_v': nrm(ks[6], (DEC_BATCH, DEPTH, B_HEADS, PAST_LEN, B_V_DIM), 1.0),
        'state_c_fwd': nrm(ks[7], (DEC_BATCH, DEPTH, C_HEADS, C_DK, C_DV), 1.0),
        'state_c_bwd': nrm(ks[8], (DEC_BATCH, DEPTH, C_HEADS, C_DK, C_DV), 1.0),
        'c_ctx': nrm(ks[9], (D_MODEL,), 1.0),
        'w_mod': nrm(ks[10], (DEPTH, D_MODEL, 3 * D_MODEL), D_MODEL ** -0.5),
        'b_mod': nrm(ks[11], (DEPTH, 3 * D_MODEL), 0.02),
        'g_pre': 1.0 + nrm(ks[12], (DEPTH, D_MODEL), 0.02),
        'g_post': 1.0 + nrm(ks[13], (DEPTH, D_MODEL), 0.02),
        'w_in': nrm(ks[14], (DEPTH, D_MODEL, IN_WIDTH), D_MODEL ** -0.5),
        'w_out': nrm(ks[15], (DEPTH, D_MIX, D_MODEL), D_MIX ** -0.5),
        'a_q_gain': 1.0 + nrm(ks[16], (DEPTH, HEAD_DIM), 0.02),
        'a_k_gain': 1.0 + nrm(ks[17], (DEPTH, HEAD_DIM), 0.02),
        'b_lambda_q1': nrm(ks[18], (DEPTH, B_QK_DIM), 0.1),
        'b_lambda_k1': nrm(ks[19], (DEPTH, B_QK_DIM), 0.1),
        'b_lambda_q2': nrm(ks[20], (DEPTH, B_QK_DIM), 0.1),
        'b_lambda_k2': nrm(ks[21], (DEPTH, B_QK_DIM), 0.1),
        'b_out_gain': 1.0 + nrm(ks[22], (DEPTH, B_V_DIM), 0.02),
        'c_gate_w_fwd': nrm(ks[23], (DEPTH, GATE_RANK, C_HEADS * C_DK), GATE_RANK ** -0.5),
        'c_gate_b_fwd': nrm(ks[24], (DEPTH, C_HEADS * C_DK), 0.02),
        'c_gate_w_bwd': nrm(ks[25], (DEPTH, GATE_RANK, C_HEADS * C_DK), GATE_RANK ** -0.5),
        'c_gate_b_bwd': nrm(ks[26], (DEPTH, C_HEADS * C_DK), 0.02),
        'c_out_gain': 1.0 + nrm(ks[27], (DEPTH, C_DV), 0.02),
    }

def reference(x_prompt, x_sample, c, cache_a_k, cache_a_v, cache_b_k, cache_b_v, state_c_fwd, state_c_bwd,
              c_ctx, w_mod, b_mod, g_pre, g_post, w_in, w_out, a_q_gain, a_k_gain,
              b_lambda_q1, b_lambda_k1, b_lambda_q2, b_lambda_k2, b_out_gain,
              c_gate_w_fwd, c_gate_b_fwd, c_gate_w_bwd, c_gate_b_bwd, c_out_gain):
    rows = x_sample.shape[1] // GRID_W
    t = jnp.arange(rows * GRID_W)
    pos = (t // GRID_W, t % GRID_W)
    lam_base = (jnp.exp(jnp.sum(b_lambda_q1.astype(jnp.float32) * b_lambda_k1.astype(jnp.float32), axis=-1))
                - jnp.exp(jnp.sum(b_lambda_q2.astype(jnp.float32) * b_lambda_k2.astype(jnp.float32), axis=-1)))

    y_p, y_s = x_prompt, x_sample
    ctx_layers = []
    for l in range(DEPTH):
        lam_init = 0.8 - 0.6 * math.exp(-0.3 * l)
        lam = lam_base[l] + lam_init
        lp = (g_pre[l], g_post[l], w_in[l], w_out[l], a_q_gain[l], a_k_gain[l], b_out_gain[l],
              c_gate_w_fwd[l], c_gate_b_fwd[l], c_gate_w_bwd[l], c_gate_b_bwd[l], c_out_gain[l])
        mod_ctx = (jax.nn.silu(c_ctx) @ w_mod[l] + b_mod[l])[None, :]
        mod_lat = jax.nn.silu(c) @ w_mod[l] + b_mod[l]
        y_p, ctx_l = trunk_layer(y_p, mod_ctx, lp, lam, lam_init, None, None)
        ctx_cache = (cache_a_k[:, l], cache_a_v[:, l], cache_b_k[:, l], cache_b_v[:, l],
                     state_c_fwd[:, l], state_c_bwd[:, l])
        y_s, _ = trunk_layer(y_s, mod_lat, lp, lam, lam_init, pos, ctx_cache)
        ctx_layers.append(ctx_l)

    new_a_k, new_a_v, new_b_k, new_b_v, new_state_c_fwd, new_state_c_bwd = [
        jnp.stack(ts, axis=1) for ts in zip(*ctx_layers)]
    return (y_p, y_s, new_a_k, new_a_v, new_b_k, new_b_v, new_state_c_fwd, new_state_c_bwd)


_drawn_inputs = setup_inputs


def setup_inputs(seed=0):
    import zlib

    import numpy as np

    out = dict(_drawn_inputs(seed))
    spreads = {}
    factors = {'cache_a_k': 3.579,
     'cache_a_v': 3.151,
     'state_c_fwd': 8.0,
     'state_c_bwd': 8.0,
     'g_post': 3.526,
     'a_q_gain': 8.0,
     'a_k_gain': 2.898,
     'b_lambda_q2': 3.294,
     'b_lambda_k2': 7.119,
     'b_out_gain': 6.753,
     'c_gate_b_fwd': 4.521,
     'c_gate_b_bwd': 5.058,
     'c_out_gain': 6.157}
    for name, (base, spread) in spreads.items():
        noise = np.random.default_rng([zlib.crc32(name.encode()), seed]).standard_normal(out[name].shape)
        drawn = base * np.exp(spread * noise) if base else spread * noise
        out[name] = jnp.asarray(drawn.astype(out[name].dtype))
    for name, factor in factors.items():
        out[name] = (out[name] * factor).astype(out[name].dtype)
    return out
```

```python
from contextlib import ExitStack

import concourse.bass as bass
from concourse import mybir

F32 = mybir.dt.float32
F32R = mybir.dt.float32r
ACT = mybir.ActivationFunctionType
ALU = mybir.AluOpType
AX_X = mybir.AxisListType.X

P = 128
D_MODEL = 1024
DEPTH = 2
SEQ, DEC_SEQ, PAST = 256, 1024, 256
GRID_W = 64
HEAD_DIM = 64
A_HEADS, A_KV = 8, 2
B_HEADS, B_QK, B_V = 4, 32, 64
C_HEADS, C_DK, C_DV = 4, 32, 64
RANK, TAU = 16, 16.0
EPS = 1e-6
ROPE_THETA = 10000.0

KD = D_MODEL // P
TS = DEC_SEQ // P
TP = SEQ // P
T = TS + TP
TOK = T * P
NB = 512
Z_COLS = 3 * NB
C_COL0 = Z_COLS
LR_COL0 = C_COL0 + NB
U_COL0 = LR_COL0 + 2 * RANK
IN_WIDTH = U_COL0 + D_MODEL

BLOCKS = [("z", 2 * NB, NB), ("z", 0, NB), ("z", NB, NB), ("c", C_COL0, NB), ("lr", LR_COL0, P),
          ("u", U_COL0, NB), ("u", U_COL0 + NB, NB)]
Z_BLOCKS = 3
RING = 12
STAGES = 3


def tile_rows(t):
    return slice(t * P, (t + 1) * P)


class Chain:

    def __init__(self, eng, sem):
        self.eng, self.sem, self.n = eng, sem, 0

    def __call__(self, ins):
        self.n += 1
        ins.then_inc(self.sem, 1)
        self.eng.wait_ge(self.sem, self.n)


def modulation_block(nc, l, io, per, s):
    NT = 3 * KD
    WST = 3
    with ExitStack() as ctx:
        def sb(name, shape, dt=F32):
            return ctx.enter_context(nc.sbuf_tensor(name, shape, dt))

        wst = sb("mod_w", [P, WST, 3 * D_MODEL])
        rows = sb("mod_rows", [NT + 2 * KD, P])
        lams = sb("mod_lams", [P, 4, B_QK])
        prod = sb("mod_prod", [P, 2, B_QK])
        dots = sb("mod_dots", [P, 2])
        lam_c = sb("mod_lam_c", [P, 2])
        mod = sb("mod_cols", [P, 2, NT])
        one_scale = sb("mod_one_scale", [P, 2, KD])
        bcols = sb("mod_bcols", [P, NT + 2 * KD])
        acc = ctx.enter_context(nc.psum_tensor("mod_acc", [P, NB], F32))
        tr = ctx.enter_context(nc.psum_tensor("mod_tr", [P, NB], F32))
        accv = acc[:, 0:2 * NT].rearrange("p (m s) -> p m s", s=2)
        block = ctx.enter_context(nc.Block())

        def layer(ap):
            return ap[bass.ds(l, 1)]

        @block.sync
        def _(sp):
            sp.dma_start(rows[0:NT, :], layer(io["b_mod"]).rearrange("a (m p) -> (a m) p", p=P)).then_inc(s["m_small"], 16)
            sp.dma_start(rows[NT:NT + KD, :], layer(io["g_pre"]).rearrange("a (m p) -> (a m) p", p=P)).then_inc(s["m_small"], 16)
            sp.dma_start(rows[NT + KD:, :], layer(io["g_post"]).rearrange("a (m p) -> (a m) p", p=P)).then_inc(s["m_small"], 16)
            for i, name in enumerate(("b_lambda_q1", "b_lambda_k1", "b_lambda_q2", "b_lambda_k2")):
                sp.dma_start(lams[:, i, :], layer(io[name]).broadcast_to([P, B_QK])).then_inc(s["m_small"], 16)
            for i, name in enumerate(("a_q_gain", "a_k_gain", "b_out_gain", "c_out_gain")):
                sp.dma_start(per["gains"][:, i, :], layer(io[name]).broadcast_to([P, HEAD_DIM])).then_inc(s["m_small"], 16)
            sp.dma_start(lam_c[:, :], layer(io["lam_consts"]).broadcast_to([P, 2])).then_inc(s["m_small"], 16)
            C = C_HEADS * C_DK
            gw = per["gate_w"]
            sp.dma_start(gw[0:RANK, 0:C], layer(io["c_gate_w_fwd"]).rearrange("a r c -> (a r) c")).then_inc(s["m_small"], 16)
            sp.dma_start(gw[RANK:2 * RANK, C:2 * C], layer(io["c_gate_w_bwd"]).rearrange("a r c -> (a r) c")).then_inc(s["m_small"], 16)
            sp.dma_start(gw[2 * RANK:2 * RANK + 1, 0:C], layer(io["c_gate_b_fwd"])).then_inc(s["m_small"], 16)
            sp.dma_start(gw[2 * RANK:2 * RANK + 1, C:2 * C], layer(io["c_gate_b_bwd"])).then_inc(s["m_small"], 16)
            for k in range(KD):
                if k >= WST:
                    sp.wait_ge(s["m_used"], k - WST + 1)
                sp.dma_start(wst[:, k % WST, :], layer(io["w_mod"])[:, k * P:(k + 1) * P, :].rearrange("a p n -> (a p) n")
                             ).then_inc(s[f"m_w{k % WST}"], 16)

        @block.tensor
        def _(pe):
            pe.wait_ge(s["m_small"], 16 * 16)
            pe.transpose(tr[:, 0:NT + 2 * KD], rows[:, :], per["ident"][0:NT + 2 * KD, 0:NT + 2 * KD]).then_inc(s["m_tr"], 1)
            for k in range(KD):
                pe.wait_ge(s[f"m_w{k % WST}"], 16 * (k // WST + 1))
                for m in range(NT):
                    mm = pe.matmul(accv[:, m, :], wst[:, k % WST, m * P:(m + 1) * P], per["cond"][:, k, :],
                                   start=(k == 0 and m == 0), stop=(k == KD - 1), skip_group_check=True)
                mm.then_inc(s["m_used"], 1)

        @block.scalar
        def _(act):
            act.wait_ge(s["m_dot"], 2)
            act.activation(dots[:, :], dots[:, :], ACT.Exp).then_inc(s["m_exp"], 1)

        @block.vector
        def _(dve):
            do = Chain(dve, s["m_dve"])
            dve.wait_ge(s["m_small"], 16 * 16)
            do(dve.tensor_tensor(prod[:, :, :], lams[:, 0:4:2, :], lams[:, 1:4:2, :], ALU.mult))
            dve.tensor_reduce(dots[:, :], prod[:, :, :], AX_X, ALU.add).then_inc(s["m_dot"], 2)
            dve.wait_ge(s["m_exp"], 1)
            do(dve.tensor_tensor(per["neg_lam"][:, :], dots[:, 1:2], dots[:, 0:1], ALU.subtract))
            do(dve.tensor_tensor(per["neg_lam"][:, :], per["neg_lam"][:, :], lam_c[:, 0:1], ALU.subtract))
            do(dve.tensor_scalar(per["gains"][:, 2, :], per["gains"][:, 2, :], lam_c[:, 1:2], None, ALU.mult))
            dve.wait_ge(s["m_tr"], 1)
            do(dve.tensor_copy(bcols[:, :], tr[:, 0:NT + 2 * KD]))
            dve.wait_ge(s["m_used"], KD)
            for g in range(2):
                do(dve.tensor_tensor(mod[:, g, :], accv[:, :, g], bcols[:, 0:NT], ALU.add))
                do(dve.tensor_copy(per["h_shift"][:, g, :], mod[:, g, 0:KD]))
                do(dve.tensor_scalar(one_scale[:, g, :], mod[:, g, KD:2 * KD], 1.0, None, ALU.add))
                do(dve.tensor_tensor(per["h_scale"][:, g, :], one_scale[:, g, :], bcols[:, NT:NT + KD], ALU.mult))
                do(dve.tensor_tensor(per["post"][:, g, :], mod[:, g, 2 * KD:], bcols[:, NT + KD:], ALU.mult))


def projection_block(nc, l, io, per, s):
    with ExitStack() as ctx:
        def sb(name, shape, dt=F32):
            return ctx.enter_context(nc.sbuf_tensor(name, shape, dt))

        h_hi = sb("h_hi", [P, KD, TOK], F32R)
        h_lo = sb("h_lo", [P, KD, TOK], F32R)
        w_hi = sb("w_hi", [P, RING, NB], F32R)
        w_lo = sb("w_lo", [P, RING, NB], F32R)
        stage = sb("w_stage", [P, STAGES, NB])
        xs = sb("x_tiles", [P, 2, D_MODEL])
        xn = sb("x_normed", [P, D_MODEL])
        h32 = sb("h32", [P, KD, P])
        ss = sb("x_stats", [P, 3, T])
        zt = sb("z_raw", [P, 3, NB])
        zo = sb("z_out", [P, 3, NB])
        tm = sb("z_tmp", [P, 3, NB])
        hst = sb("head_stats", [P, 2, 3, A_HEADS])
        tp = [ctx.enter_context(nc.psum_tensor(f"h_tr{i}", [P, KD, P], F32)) for i in range(2)]
        zp = [ctx.enter_context(nc.psum_tensor(f"z_acc{i}", [P, NB], F32)) for i in range(4)]
        block = ctx.enter_context(nc.Block())
        w_in, Zs, Us = io["w_in"], io["Zs"], io["Us"]
        NW = KD * len(BLOCKS)

        def group(t):
            return 0 if t < TS else 1

        uses = []
        for b, (kind, _, _) in enumerate(BLOCKS):
            if kind in ("z", "u"):
                uses += [(b, kind, t) for t in range(T)]
            elif kind == "c":
                uses += [(b, f"cT{m}", tb) for m in range(2) for tb in range(3)] + [(b, "cv", t) for t in range(T)]
            else:
                uses += [(b, "lr", tb) for tb in range(3)]
        first_use = {b: min(i for i, u in enumerate(uses) if u[0] == b) for b in range(len(BLOCKS))}
        last_use = {b: max(i for i, u in enumerate(uses) if u[0] == b) for b in range(len(BLOCKS))}
        U_USE0 = first_use[len(BLOCKS) - 2]

        def new_stores(slot, i):
            return sum(2 for j in range(slot, i, 3) if j % T >= TS and BLOCKS[j // T][1] > 0)

        def tok_block(tb):
            return slice(tb * NB, min((tb + 1) * NB, TOK))

        def free_ring(eng, n):
            b, k = divmod(n - RING, KD)
            if k < KD - 1:
                eng.wait_ge(s["p_wfree"], b * (KD - 1) + k + 1)
            else:
                eng.wait_ge(s["p_acc"], last_use[b] + 1)

        @block.sync
        def _(sp):
            def load_x(t):
                if t >= 2:
                    sp.wait_ge(s["p_xn"], t - 1)
                src_new = (io["y_sample"], t * P) if t < TS else (io["y_prompt"], (t - TS) * P)
                src_in = (io["x_sample"], t * P) if t < TS else (io["x_prompt"], (t - TS) * P)
                with sp.If(l < 1):
                    sp.dma_start(xs[:, t % 2, :], src_in[0][src_in[1]:src_in[1] + P, :]).then_inc(s[f"p_x{t % 2}"], 16)
                with sp.Else():
                    sp.dma_start(xs[:, t % 2, :], src_new[0][src_new[1]:src_new[1] + P, :]).then_inc(s[f"p_x{t % 2}"], 16)

            def load_w(first, end):
                for n in range(first, min(end, NW)):
                    (_, c0, cols), k = BLOCKS[n // KD], n % KD
                    if n >= STAGES:
                        sp.wait_ge(s["p_wlo"], n - STAGES + 1)
                    sp.dma_start(stage[:, n % STAGES, 0:cols],
                                 w_in[bass.ds(l, 1), k * P:(k + 1) * P, c0:c0 + cols].rearrange("a p n -> (a p) n")
                                 ).then_inc(s[f"p_w{n % STAGES}"], 16)

            def store_z(b, t):
                i = b * T + t
                sp.wait_ge(s["p_zo"], i + 1)
                c0 = BLOCKS[b][1]
                sp.dma_start(Zs[tile_rows(t), c0:c0 + NB], zo[:, i % 3, :]).then_inc(s[f"p_out{i % 3}"], 16)
                if t >= TS:
                    rows = slice((t - TS) * P, (t - TS + 1) * P)
                    outs = {0: (), NB: (("new_a_k", 0, A_KV), ("new_a_v", A_KV * HEAD_DIM, A_KV)),
                            2 * NB: (("new_b_k", 0, B_HEADS), ("new_b_v", B_HEADS * B_V, B_HEADS))}[c0]
                    for name, c, heads in outs:
                        dst = io[name][bass.ds(l, 1), :, rows, :].rearrange("a h t d -> t (a h) d")
                        sp.dma_start(dst, zo[:, i % 3, c:c + heads * HEAD_DIM].rearrange("t (h d) -> t h d", h=heads)
                                     ).then_inc(s[f"p_new{i % 3}"], 16)

            def store_u(b, t):
                j = (b - len(BLOCKS) + 2) * T + t
                i = Z_BLOCKS * T + j
                sp.wait_ge(s["p_ev"], U_USE0 + j + 1)
                c0 = BLOCKS[b][1] - U_COL0
                sp.dma_start(Us[tile_rows(t), c0:c0 + NB], zo[:, i % 3, :]).then_inc(s[f"p_out{i % 3}"], 16)

            ahead = 4 + STAGES
            load_x(0)
            load_x(1)
            load_w(0, KD)
            load_x(2)
            load_x(3)
            for b, (kind, _, _) in enumerate(BLOCKS):
                load_w((b + 1) * KD, (b + 1) * KD + ahead)
                for t in range(T):
                    if b == 0 and t + 4 < T:
                        load_x(t + 4)
                    if t == T - 2:
                        load_w((b + 1) * KD + ahead, (b + 2) * KD)
                    if kind == "z":
                        store_z(b, t)
                    elif kind == "u":
                        store_u(b, t)
            n = Z_BLOCKS * T + 2 * T
            for i in range(3):
                sp.wait_ge(s[f"p_out{i}"], 16 * len(range(i, n, 3)))
                sp.wait_ge(s[f"p_new{i}"], 16 * new_stores(i, Z_BLOCKS * T))

        @block.tensor
        def _(pe):
            def turn(t):
                pe.wait_ge(s["p_xn"], t + 1)
                if t >= 2:
                    pe.wait_ge(s["p_h32"], t - 1)
                for k in range(KD):
                    mm = pe.transpose(tp[t % 2][:, k, :], xn[:, k * P:(k + 1) * P], per["ident"][:, :])
                mm.then_inc(s["p_turned"], 1)

            def product(i, acc, lhs, rhs, b, w_first):
                if i >= 4:
                    pe.wait_ge(s["p_ev"], i - 3)
                last = i == last_use[b]
                for k in range(KD):
                    n = b * KD + k
                    slot = n % RING
                    if i == first_use[b]:
                        pe.wait_ge(s["p_wlo"], n + 1)
                    parts = ((h_hi, w_hi), (h_hi, w_lo), (h_lo, w_hi))
                    for q, (hh, ww) in enumerate(parts):
                        w_ap, h_ap = ww[:, slot, rhs if not w_first else lhs], hh[:, k, lhs if not w_first else rhs]
                        mm = pe.matmul(acc, w_ap if w_first else h_ap, h_ap if w_first else w_ap,
                                       start=(k == 0 and q == 0), stop=(k == KD - 1 and q == 2))
                        if last and q == 2 and k < KD - 1:
                            mm.then_inc(s["p_wfree"], 1)
                if last:
                    mm.then_inc(s["p_acc"], 1)
                else:
                    mm.then_inc(s["p_acc"], 1)

            turn(0)
            turn(1)
            for i, (b, what, j) in enumerate(uses):
                acc = zp[i % 4]
                if b == 0:
                    pe.wait_ge(s["p_h"], j + 1)
                if what in ("z", "u"):
                    product(i, acc[:, :], tile_rows(j), slice(0, NB), b, False)
                elif what == "cv":
                    product(i, acc[:, 0:2 * P], tile_rows(j), slice(2 * P, 4 * P), b, False)
                else:
                    m = 0 if what == "lr" else int(what[2])
                    tb = tok_block(j)
                    product(i, acc[:, 0:tb.stop - tb.start], slice(m * P, (m + 1) * P), tb, b, True)
                if b == 0 and j + 2 < T:
                    turn(j + 2)

        @block.scalar
        def _(act):
            def square(t):
                act.wait_ge(s[f"p_x{t % 2}"], 16 * (t // 2 + 1))
                if t:
                    act.wait_ge(s["p_turned"], t)
                act.activation(xn[:, :], xs[:, t % 2, :], ACT.Square, accum_out=ss[:, 0, t:t + 1]).then_inc(s["p_sq"], 1)
                act.wait_ge(s["p_sq"], t + 1)
                act.activation(ss[:, 1, t:t + 1], ss[:, 0, t:t + 1], ACT.Sqrt, bias=per["eps"][:, :],
                               scale=1.0 / D_MODEL).then_inc(s["p_std"], 1)

            def hi_h(t):
                act.wait_ge(s["p_h32"], t + 1)
                act.copy(h_hi[:, :, tile_rows(t)], h32[:, :, :]).then_inc(s["p_hhi"], 1)

            def hi_w(n):
                cols = BLOCKS[n // KD][2]
                act.wait_ge(s[f"p_w{n % STAGES}"], 16 * (n // STAGES + 1))
                if n >= RING:
                    free_ring(act, n)
                act.copy(w_hi[:, n % RING, 0:cols], stage[:, n % STAGES, 0:cols]).then_inc(s["p_whi"], 1)

            def evacuate(i):
                b, what, j = uses[i]
                act.wait_ge(s["p_acc"], i + 1)
                acc = zp[i % 4]
                if what == "z":
                    if i >= 3:
                        act.wait_ge(s["p_zo"], i - 2)
                    act.copy(zt[:, i % 3, :], acc[:, :]).then_inc(s["p_ev"], 1)
                elif what == "u":
                    q = Z_BLOCKS * T + i - U_USE0
                    act.wait_ge(s[f"p_out{q % 3}"], 16 * len(range(q % 3, q, 3)))
                    act.activation(zo[:, q % 3, :], acc[:, :], ACT.Silu).then_inc(s["p_ev"], 1)
                elif what == "cv":
                    act.copy(per["cv"][:, j, :], acc[:, 0:2 * P]).then_inc(s["p_ev"], 1)
                else:
                    tb = tok_block(j)
                    rows = 2 * RANK if what == "lr" else P
                    dst = per["lrT"] if what == "lr" else per["cqT"] if what == "cT0" else per["ckT"]
                    act.copy(dst[0:rows, tb], acc[0:rows, 0:tb.stop - tb.start]).then_inc(s["p_ev"], 1)

            def head_std(i):
                if BLOCKS[i // T][1] > NB:
                    return
                heads = A_HEADS if BLOCKS[i // T][1] == 0 else A_KV
                n = i - T + 1
                act.wait_ge(s["p_hss"], n)
                act.activation(hst[:, i % 2, 1, 0:heads], hst[:, i % 2, 0, 0:heads], ACT.Sqrt, bias=per["eps"][:, :],
                               scale=1.0 / HEAD_DIM).then_inc(s["p_hstd"], 1)

            square(0)
            for n in range(4):
                hi_w(n)
            hi_h(0)
            square(1)
            for n in range(4, 8):
                hi_w(n)
            hi_h(1)
            square(2)
            for i, (b, what, j) in enumerate(uses):
                if i == last_use[b] and b + 1 < len(BLOCKS):
                    for k in range(4, KD):
                        hi_w((b + 1) * KD + k)
                evacuate(i)
                if 0 < i <= Z_BLOCKS * T:
                    head_std(i - 1)
                if b == 0 and j + 2 < T:
                    hi_h(j + 2)
                    if j + 3 < T:
                        square(j + 3)
                if i == first_use[b] and b + 1 < len(BLOCKS):
                    for k in range(4):
                        hi_w((b + 1) * KD + k)

        @block.vector
        def _(dve):
            do = Chain(dve, s["p_dve"])

            def norm_x(t):
                dve.wait_ge(s["p_std"], t + 1)
                do(dve.reciprocal(ss[:, 2, t:t + 1], ss[:, 1, t:t + 1]))
                dve.tensor_scalar(xn[:, :], xs[:, t % 2, :], ss[:, 2, t:t + 1], None, ALU.mult).then_inc(s["p_xn"], 1)

            def affine(t):
                g = group(t)
                dve.wait_ge(s["p_turned"], t + 1)
                if t:
                    dve.wait_ge(s["p_h"], t)
                for k in range(KD):
                    ins = dve.tensor_scalar(h32[:, k, :], tp[t % 2][:, k, :], per["h_scale"][:, g, k:k + 1],
                                            per["h_shift"][:, g, k:k + 1], ALU.mult, ALU.add)
                ins.then_inc(s["p_h32"], 1)

            def lo_h(t):
                dve.wait_ge(s["p_hhi"], t + 1)
                dve.tensor_tensor(h_lo[:, :, tile_rows(t)], h32[:, :, :], h_hi[:, :, tile_rows(t)].bitcast(F32),
                                  ALU.subtract).then_inc(s["p_h"], 1)

            def lo_w(n):
                cols = BLOCKS[n // KD][2]
                dve.wait_ge(s["p_whi"], n + 1)
                dve.tensor_tensor(w_lo[:, n % RING, 0:cols], stage[:, n % STAGES, 0:cols],
                                  w_hi[:, n % RING, 0:cols].bitcast(F32), ALU.subtract).then_inc(s["p_wlo"], 1)

            def heads_view(ap, heads):
                return ap.rearrange("p (h d) -> p h d", h=heads)

            def rope(dst, src, t, heads, half, cos, sin, tmp):
                d = heads_view(dst, heads)
                x = heads_view(src, heads)
                w = dst.shape[1] // heads
                c = cos[:, t, :].unsqueeze(1).broadcast_to([P, heads, w])
                do(dve.tensor_tensor(d, x, c, ALU.mult))
                x4 = src.rearrange("p (h g e f) -> p h g e f", h=heads, e=2, f=half)
                t4 = tmp.rearrange("p (h g e f) -> p h g e f", h=heads, e=2, f=half)
                s3 = sin[:, t, :].rearrange("p (g e f) -> p g e f", e=2, f=half)
                g = w // (2 * half)
                for e in range(2):
                    sn = s3[:, :, e, :].unsqueeze(1).broadcast_to([P, heads, g, half])
                    do(dve.tensor_tensor(t4[:, :, :, e, :], x4[:, :, :, 1 - e, :], sn, ALU.mult))
                return dve.tensor_tensor(dst, dst, tmp, ALU.add)

            def head_sums(i):
                c0 = BLOCKS[i // T][1]
                if c0 > NB:
                    return
                heads = A_HEADS if c0 == 0 else A_KV
                dve.wait_ge(s["p_ev"], i + 1)
                w = heads * HEAD_DIM
                do(dve.tensor_tensor(tm[:, 0, 0:w], zt[:, i % 3, 0:w], zt[:, i % 3, 0:w], ALU.mult))
                dve.tensor_reduce(hst[:, i % 2, 0, 0:heads], heads_view(tm[:, 0, 0:w], heads), AX_X,
                                  ALU.add).then_inc(s["p_hss"], 1)

            def finish_tile(i):
                b, t = divmod(i, T)
                c0 = BLOCKS[b][1]
                z, o = zt[:, i % 3, :], zo[:, i % 3, :]
                dve.wait_ge(s["p_ev"], i + 1)
                if i >= 3:
                    dve.wait_ge(s[f"p_out{i % 3}"], 16 * (i // 3))
                    if new_stores(i % 3, i):
                        dve.wait_ge(s[f"p_new{i % 3}"], 16 * new_stores(i % 3, i))
                if c0 <= NB:
                    heads = A_HEADS if c0 == 0 else A_KV
                    w = heads * HEAD_DIM
                    dve.wait_ge(s["p_hstd"], i - T + 1)
                    do(dve.reciprocal(hst[:, i % 2, 2, 0:heads], hst[:, i % 2, 1, 0:heads]))
                    zv = heads_view(z[:, 0:w], heads)
                    do(dve.tensor_tensor(heads_view(tm[:, 1, 0:w], heads), zv,
                                         hst[:, i % 2, 2, 0:heads].unsqueeze(2).broadcast_to([P, heads, HEAD_DIM]), ALU.mult))
                    gain = per["gains"][:, 0 if c0 == 0 else 1, :].unsqueeze(1).broadcast_to([P, heads, HEAD_DIM])
                    if t < TS:
                        do(dve.tensor_tensor(heads_view(tm[:, 2, 0:w], heads), heads_view(tm[:, 1, 0:w], heads), gain, ALU.mult))
                        last = rope(o[:, 0:w], tm[:, 2, 0:w], t, heads, 16, per["cosA"], per["sinA"], tm[:, 1, 0:w])
                    else:
                        last = dve.tensor_tensor(heads_view(o[:, 0:w], heads), heads_view(tm[:, 1, 0:w], heads), gain, ALU.mult)
                    if c0 == NB:
                        do(last)
                        do(dve.tensor_copy(o[:, P:2 * P], z[:, P:2 * P]))
                        if t < TS:
                            last = rope(o[:, 2 * P:NB], z[:, 2 * P:NB], t, 2 * B_HEADS, 8, per["cosB"], per["sinB"], tm[:, 1, 0:2 * P])
                        else:
                            last = dve.tensor_copy(o[:, 2 * P:NB], z[:, 2 * P:NB])
                else:
                    do(dve.tensor_copy(o[:, 2 * P:NB], z[:, 2 * P:NB]))
                    if t < TS:
                        last = rope(o[:, 0:2 * P], z[:, 0:2 * P], t, 2 * B_HEADS, 8, per["cosB"], per["sinB"], tm[:, 1, 0:2 * P])
                    else:
                        last = dve.tensor_copy(o[:, 0:2 * P], z[:, 0:2 * P])
                last.then_inc(s["p_zo"], 1)

            norm_x(0)
            for n in range(4):
                lo_w(n)
            affine(0)
            lo_h(0)
            norm_x(1)
            for n in range(4, 8):
                lo_w(n)
            affine(1)
            lo_h(1)
            norm_x(2)
            for i, (b, what, j) in enumerate(uses):
                if i == last_use[b] and b + 1 < len(BLOCKS):
                    for k in range(4, KD):
                        lo_w((b + 1) * KD + k)
                if b == 0 and j + 2 < T:
                    affine(j + 2)
                    lo_h(j + 2)
                    if j + 3 < T:
                        norm_x(j + 3)
                if i < Z_BLOCKS * T:
                    head_sums(i)
                if 0 < i <= Z_BLOCKS * T:
                    finish_tile(i - 1)
                if i == first_use[b] and b + 1 < len(BLOCKS):
                    for k in range(4):
                        lo_w((b + 1) * KD + k)


CHUNK = 64
NC_S, NC_P = DEC_SEQ // CHUNK, SEQ // CHUNK
S_SLOTS = NC_S + 1 + NC_P + 1


def gla_block(nc, l, io, per, mid, s):
    CD, CV = C_HEADS * C_DK, C_HEADS * C_DV
    with ExitStack() as ctx:
        def sb(name, shape, dt=F32):
            return ctx.enter_context(nc.sbuf_tensor(name, shape, dt))

        def ps(name):
            return ctx.enter_context(nc.psum_tensor(name, [P, NB], F32))

        gate = sb("gate", [P, T, 2 * CD])
        soft = sb("gate_soft", [P, T, 2 * CD])
        qt = sb("q_decayed", [P, T, 2, P])
        oi = sb("o_intra", [P, T, CV])
        st = sb("states", [P, 2, S_SLOTS, CV])
        el = sb("exp_last", [P, T, 2, 2])
        lc = sb("last_cum", [P, 2, 2, 2])
        ex = sb("exps", [P, 2, 3, 2, P])
        kt = sb("k_scaled", [P, 2, 2, 2, P])
        qbd = sb("q_blockdiag", [P, 2, 2, C_HEADS, P])
        am = sb("a_masked", [P, 2, 2, C_HEADS, P])
        k2t = sb("k_by_token", [P, 2, 2, P])
        stats = sb("c_stats", [P, 3, T, C_HEADS])
        cum_ps = [ps("cum0"), ps("cum1")]
        at_ps = [ps("at0"), ps("at1")]
        tr_ps, o_ps = ps("gla_tr"), ps("gla_o")
        ds_ps = [ps("ds0"), ps("ds1")]
        block = ctx.enter_context(nc.Block())
        oc = mid["oc"]

        def slot0(t):
            return 0 if t < TS else NC_S + 1

        def step_of(d, t, c):
            n = 2 * (t if t < TS else t - TS) + c
            chunks = NC_S if t < TS else NC_P
            return n if d == 0 else chunks - 1 - n

        @block.sync
        def _(sp):
            sp.wait_ge(s["g_zero"], 2)
            for d, name in enumerate(("state_c_fwd", "state_c_bwd")):
                for h in range(C_HEADS):
                    sp.dma_start(st[h * C_DK:(h + 1) * C_DK, d, 0, h * C_DV:(h + 1) * C_DV],
                                 io[name][bass.ds(l, 1), h, :, :].rearrange("a x y -> (a x) y")).then_inc(s["g_st0"], 16)
            sp.wait_ge(s["g_chain"], 1)
            for d, name in enumerate(("new_state_c_fwd", "new_state_c_bwd")):
                for h in range(C_HEADS):
                    sp.dma_start(io[name][bass.ds(l, 1), h, :, :].rearrange("a x y -> (a x) y"),
                                 st[h * C_DK:(h + 1) * C_DK, d, S_SLOTS - 1, h * C_DV:(h + 1) * C_DV]).then_inc(s["g_new"], 16)
            sp.wait_ge(s["g_new"], 16 * 2 * C_HEADS)

        @block.tensor
        def _(pe):
            for i in range(T // 2):
                if i >= 2:
                    pe.wait_ge(s["g_min"], i - 1)
                for t in (2 * i, 2 * i + 1):
                    mm = pe.matmul(cum_ps[i % 2][:, (t % 2) * 2 * CD:(t % 2 + 1) * 2 * CD], per["lrT"][:, tile_rows(t)],
                                   per["gate_w"][:, :], start=True, stop=True)
                mm.then_inc(s["g_pre"], 1)
            pe.wait_ge(s["g_gate"], 1)

            def running_sums(t):
                if t >= 2:
                    pe.wait_ge(s["g_exp"], t - 1)
                for d in range(2):
                    mm = pe.matmul(cum_ps[t % 2][:, d * P:(d + 1) * P], gate[:, t, d * CD:(d + 1) * CD], per["tri"][:, d, :],
                                   start=True, stop=True)
                mm.then_inc(s["g_cum"], 1)

            running_sums(0)
            running_sums(1)
            for t in range(T):
                b = t % 2
                pe.wait_ge(s["g_mul"], t + 1)
                if t:
                    pe.wait_ge(s["g_k2t"], t)
                for d in range(2):
                    mm = pe.transpose(tr_ps[:, d * P:(d + 1) * P], kt[:, b, 1, d, :], per["ident"][:, :])
                mm.then_inc(s["g_tr"], 1)
                for d in range(2):
                    if t:
                        pe.wait_ge(s["g_am"], 2 * t + d - 1)
                    pe.matmul(at_ps[d][:, :], kt[:, b, 0, d, :], qbd[:, b, d, :, :].rearrange("p h i -> p (h i)"),
                              start=True, stop=True).then_inc(s["g_at"], 1)
                if t + 2 < T:
                    running_sums(t + 2)
                pe.wait_ge(s["g_k2t"], t + 1)
                if t:
                    pe.wait_ge(s["g_dsm"], t)
                for c in range(2):
                    rows = slice(c * CHUNK, (c + 1) * CHUNK)
                    for d in range(2):
                        mm = pe.matmul(ds_ps[c][:, d * CV:(d + 1) * CV], k2t[rows, b, d, :], per["cv"][rows, t, :],
                                       start=True, stop=True)
                mm.then_inc(s["g_ds"], 1)
                pe.wait_ge(s["g_am"], 2 * t + 2)
                if t:
                    pe.wait_ge(s["g_oi"], t)
                for h in range(C_HEADS):
                    cols = slice(h * C_DV, (h + 1) * C_DV)
                    for d in range(2):
                        mm = pe.matmul(o_ps[:, cols], am[:, b, d, h, :], per["cv"][:, t, cols], start=(d == 0), stop=(d == 1))
                mm.then_inc(s["g_o"], 1)
            pe.wait_ge(s["g_chain"], 1)
            for t in range(T):
                if t >= 2:
                    pe.wait_ge(s["g_oc"], t - 1)
                for c in range(2):
                    for d in range(2):
                        mm = pe.matmul(cum_ps[t % 2][c * CHUNK:(c + 1) * CHUNK, 0:CV], qt[:, t, d, c * CHUNK:(c + 1) * CHUNK],
                                       st[:, d, slot0(t) + step_of(d, t, c), :], start=(d == 0), stop=(d == 1))
                mm.then_inc(s["g_inter"], 1)

        @block.scalar
        def _(act):
            do = Chain(act, s["g_act"])
            for i in range(T // 2):
                act.wait_ge(s["g_pre"], i + 1)
                act.activation(soft[:, 2 * i:2 * i + 2, :], cum_ps[i % 2][:, :].rearrange("p (t c) -> p t c", t=2),
                               ACT.Abs).then_inc(s["g_abs"], 1)
            act.wait_ge(s["g_abs"], T // 2)
            do(act.activation(soft[:, :, :], soft[:, :, :], ACT.Exp, scale=-1.0))
            act.activation(soft[:, :, :], soft[:, :, :], ACT.Ln, bias=per["one"][:, :]).then_inc(s["g_ln"], 1)

            def exps(t):
                b = t % 2
                act.wait_ge(s["g_cum"], t + 1)
                if t >= 2:
                    act.wait_ge(s["g_mul"], t - 1)
                cum = cum_ps[b][:, 0:2 * P].rearrange("p (d i) -> p d i", d=2)
                act.activation(ex[:, b, 0, :, :], cum, ACT.Exp, scale=1.0 / TAU)
                act.activation(ex[:, b, 1, :, :], cum, ACT.Exp, scale=-1.0 / TAU)
                do(act.mul(lc[:, b, 0, :], cum[:, 0, CHUNK - 1::CHUNK], 1.0 / TAU))
                do(act.mul(lc[:, b, 1, :], cum[:, 1, 0::CHUNK], 1.0 / TAU))
                act.activation(el[:, t, :, :], lc[:, b, :, :], ACT.Exp)
                for d in range(2):
                    for c in range(2):
                        cols = slice(c * CHUNK, (c + 1) * CHUNK)
                        ins = act.activation(ex[:, b, 2, d, cols], cum[:, d, cols], ACT.Exp, scale=-1.0 / TAU,
                                             bias=lc[:, b, d, c:c + 1])
                ins.then_inc(s["g_exp"], 1)

            exps(0)
            for t in range(T):
                b = t % 2
                if t + 1 < T:
                    exps(t + 1)
                act.wait_ge(s["g_tr"], t + 1)
                if t >= 2:
                    act.wait_ge(s["g_ds"], t - 1)
                act.copy(k2t[:, b, :, :], tr_ps[:, 0:2 * P].rearrange("p (d f) -> p d f", d=2)).then_inc(s["g_k2t"], 1)
                act.wait_ge(s["g_o"], t + 1)
                act.copy(oi[:, t, :], o_ps[:, 0:CV]).then_inc(s["g_oi"], 1)
            act.wait_ge(s["g_css"], 1)
            act.activation(stats[:, 1, :, :], stats[:, 0, :, :], ACT.Sqrt, bias=per["eps"][:, :],
                           scale=1.0 / C_DV).then_inc(s["g_cstd"], 1)

        @block.vector
        def _(dve):
            do = Chain(dve, s["g_dve"])
            dve.memset(st[:, :, 0, :], 0.0).then_inc(s["g_zero"], 1)
            dve.memset(st[:, :, NC_S + 1, :], 0.0).then_inc(s["g_zero"], 1)
            for i in range(T // 2):
                dve.wait_ge(s["g_abs"], i + 1)
                dve.tensor_scalar(gate[:, 2 * i:2 * i + 2, :], cum_ps[i % 2][:, :].rearrange("p (t c) -> p t c", t=2),
                                  0.0, None, ALU.min).then_inc(s["g_min"], 1)
            dve.wait_ge(s["g_min"], T // 2)
            dve.wait_ge(s["g_ln"], 1)
            dve.tensor_tensor(gate[:, :, :], gate[:, :, :], soft[:, :, :], ALU.subtract).then_inc(s["g_gate"], 1)

            def both(ap):
                return ap.unsqueeze(1).broadcast_to([P, 2, P])

            def scale_qk(t):
                b = t % 2
                dve.wait_ge(s["g_exp"], t + 1)
                if t >= 2:
                    dve.wait_ge(s["g_at"], 2 * t - 2)
                q, k = both(per["cqT"][:, tile_rows(t)]), both(per["ckT"][:, tile_rows(t)])
                do(dve.scalar_tensor_tensor(out=qt[:, t, :, :], in0=q, scalar=float(C_DK) ** -0.5, in1=ex[:, b, 0, :, :],
                                            op0=ALU.mult, op1=ALU.mult))
                dve.tensor_tensor(kt[:, b, 0, :, :], k, ex[:, b, 1, :, :], ALU.mult)
                dve.tensor_tensor(kt[:, b, 1, :, :], k, ex[:, b, 2, :, :], ALU.mult)
                for d in range(2):
                    ins = dve.tensor_tensor(qbd[:, b, d, :, :], qt[:, t, d, :].unsqueeze(1).broadcast_to([P, C_HEADS, P]),
                                            per["bdmask"][:, :].unsqueeze(2).broadcast_to([P, C_HEADS, P]), ALU.mult)
                ins.then_inc(s["g_mul"], 1)

            scale_qk(0)
            for t in range(T):
                b = t % 2
                if t + 1 < T:
                    scale_qk(t + 1)
                for d in range(2):
                    dve.wait_ge(s["g_at"], 2 * t + d + 1)
                    if t >= 2:
                        dve.wait_ge(s["g_o"], t - 1)
                    dve.tensor_tensor(am[:, b, d, :, :], at_ps[d][:, :].rearrange("p (h i) -> p h i", h=C_HEADS),
                                      per["tri"][:, d, :].unsqueeze(1).broadcast_to([P, C_HEADS, P]),
                                      ALU.mult).then_inc(s["g_am"], 1)
                dve.wait_ge(s["g_ds"], t + 1)
                for c in range(2):
                    for d in range(2):
                        dst = st[:, d, slot0(t) + step_of(d, t, c) + 1, :].rearrange("p (h e) -> p h e", h=C_HEADS)
                        ins = dve.tensor_tensor(dst, ds_ps[c][:, d * CV:(d + 1) * CV].rearrange("p (h e) -> p h e", h=C_HEADS),
                                                per["bdmask"][:, :].unsqueeze(2).broadcast_to([P, C_HEADS, C_DV]), ALU.mult)
                ins.then_inc(s["g_dsm"], 1)
            dve.wait_ge(s["g_dsm"], T)
            dve.wait_ge(s["g_st0"], 16 * 2 * C_HEADS)
            for base, chunks, tile0 in ((0, NC_S, 0), (NC_S + 1, NC_P, TS)):
                for n in range(chunks):
                    for d in range(2):
                        ch = n if d == 0 else chunks - 1 - n
                        ins = dve.scalar_tensor_tensor(out=st[:, d, base + n + 1, :], in0=st[:, d, base + n, :],
                                                       scalar=el[:, tile0 + ch // 2, d, ch % 2:ch % 2 + 1],
                                                       in1=st[:, d, base + n + 1, :], op0=ALU.mult, op1=ALU.add)
                        do(ins)
            dve.sem_inc(s["g_chain"], 1)
            for t in range(T):
                dve.wait_ge(s["g_inter"], t + 1)
                dve.wait_ge(s["g_oi"], T)
                dve.tensor_tensor(oc[:, t, :], cum_ps[t % 2][:, 0:CV], oi[:, t, :], ALU.add).then_inc(s["g_oc"], 1)
            dve.wait_ge(s["g_oc"], T)
            do(dve.tensor_tensor(oi[:, :, :], oc[:, :, :], oc[:, :, :], ALU.mult))
            dve.tensor_reduce(stats[:, 0, :, :], oi[:, :, :].rearrange("p t (h e) -> p t h e", h=C_HEADS), AX_X,
                              ALU.add).then_inc(s["g_css"], 1)
            dve.wait_ge(s["g_cstd"], 1)
            do(dve.reciprocal(stats[:, 2, :, :], stats[:, 1, :, :]))
            o4 = oc[:, :, :].rearrange("p t (h e) -> p (t h) e", h=C_HEADS)
            r3 = stats[:, 2, :, :].rearrange("p t h -> p (t h)").unsqueeze(2).broadcast_to([P, T * C_HEADS, C_DV])
            do(dve.tensor_tensor(o4, o4, r3, ALU.mult))
            do(dve.tensor_tensor(o4, o4, per["gains"][:, 3, :].unsqueeze(1).broadcast_to([P, T * C_HEADS, C_DV]), ALU.mult))


KT = (PAST + DEC_SEQ + SEQ) // P
KT_S = (PAST + DEC_SEQ) // P
KEYS = KT * P
ATT_STEPS = KT_S + 1
PREP = 30
PREP_Q, PREP_MAX, PREP_LAST = 3, 6, 27
HALF = 5


def attention_block(nc, l, io, per, mid, s):
    A, B = "A", "B"
    W = {A: HEAD_DIM, B: B_QK}
    KR = {A: P, B: 3 * B_QK + 2}
    SCALE = {A: float(HEAD_DIM) ** -0.5, B: float(B_QK) ** -0.5}
    with ExitStack() as ctx:
        def sb(name, shape, dt=F32):
            return ctx.enter_context(nc.sbuf_tensor(name, shape, dt))

        kraw = {u: sb(f"k_raw{u}", [P, KT, W[u]]) for u in (A, B)}
        qraw = {u: sb(f"q_raw{u}", [P, T, W[u]]) for u in (A, B)}
        v = {u: sb(f"v{u}", [P, KT, HEAD_DIM + 1]) for u in (A, B)}
        kst = {u: sb(f"k_stack{u}", [P, KT, KR[u]]) for u in (A, B)}
        qst = {A: sb("q_stackA", [P, T, P]), B: sb("q_stackB", [P, T, KR[B]])}
        qst2 = sb("q_stackA2", [P, T, HEAD_DIM + 2])
        kT = {u: sb(f"kT{u}", [KR[u], KEYS], F32R) for u in (A, B)}
        kT2 = sb("kTA2", [HEAD_DIM + 2, KEYS], F32R)
        qT = {A: sb("qTA", [P, TOK], F32R), B: sb("qTB", [B_QK, TOK], F32R)}
        qT2 = {A: sb("qTA2", [HEAD_DIM + 2, TOK], F32R), B: sb("qTB2", [KR[B], TOK], F32R)}
        pr = sb("probs", [P, 2, DEC_SEQ])
        nmx = sb("neg_max_parts", [P, T, 3])
        nm = sb("neg_max", [P, T])
        rs = sb("recip_sums", [P, 2, HALF])
        sc = [ctx.enter_context(nc.psum_tensor(f"scores{i}", [P, 2, NB], F32)) for i in range(2)]
        ob = ctx.enter_context(nc.psum_tensor("att_out", [P, 2, NB], F32))
        wk = [ctx.enter_context(nc.psum_tensor(f"work{i}", [P, NB], F32)) for i in range(2)]
        block = ctx.enter_context(nc.Block())
        Zs = io["Zs"]
        m_cols = {A: qst2[:, :, HEAD_DIM:], B: qst[B][:, :, 3 * B_QK:]}
        TURNS = A_HEADS

        def step0(u, h):
            return h * 2 * ATT_STEPS + (0 if u == A else ATT_STEPS)

        def unit(u, h):
            return 2 * h + (0 if u == A else 1)

        def col(u, h, what):
            if u == A:
                kv = h // (A_HEADS // A_KV)
                return {"q": h * HEAD_DIM, "k": A_HEADS * HEAD_DIM + kv * HEAD_DIM,
                        "v": (A_HEADS + A_KV) * HEAD_DIM + kv * HEAD_DIM}[what]
            base = (A_HEADS + 2 * A_KV) * HEAD_DIM
            nb = B_HEADS * 2 * B_QK
            return {"q": base + h * B_QK, "k": base + nb + h * B_QK, "v": base + 2 * nb + (h // 2) * B_V}[what]

        @block.sync
        def _(sp):
            def load(u, dst, h, what, sem, w):
                c = col(u, h, what)
                src = Zs[:, bass.ds(c, w)].rearrange("(t p) d -> p t d", p=P)
                first = 0 if what == "q" else PAST // P
                sp.dma_start(dst[:, first:, 0:w], src).then_inc(s[sem], 16)
                if what != "q":
                    cache = io[f"cache_{u.lower()}_{what}"]
                    head = h // (A_HEADS // A_KV) if u == A else h // 2
                    c0 = (h % 2) * B_QK if (u == B and what == "k") else 0
                    src = cache[bass.ds(l, 1), bass.ds(head, 1), :, bass.ds(c0, w)].rearrange("a b (t p) d -> p (a b t) d", p=P)
                    sp.dma_start(dst[:, 0:first, 0:w], src).then_inc(s[sem], 16)

            def load_qk(u, h):
                load(u, kraw[u], h, "k", f"a_raw{u}", W[u])
                load(u, qraw[u], h, "q", f"a_raw{u}", W[u])

            def load_v(u, h):
                load(u, v[u], h, "v", f"a_v{u}", HEAD_DIM)

            for u in (A, B):
                load_qk(u, 0)
            sp.wait_ge(s["a_ones"], 1)
            for u in (A, B):
                load_v(u, 0)
            with sp.Fori(0, TURNS - 1) as h:
                for u in (A, B):
                    sp.wait_ge(s[f"a_split{u}"], h + 1)
                    load_qk(u, h + 1)
                    sp.wait_ge(s["a_pv"], step0(u, h) + ATT_STEPS)
                    load_v(u, h + 1)

        @block.gpsimd
        def _(pool):
            def split(u, h, chain0):
                n = [0]

                def do(ins):
                    n[0] += 1
                    ins.then_inc(s["a_pool"], 1)
                    pool.wait_ge(s["a_pool"], chain0 + n[0])

                def copy(dst, src):
                    one = per["one"][:, :].unsqueeze(2).broadcast_to(list(src.shape))
                    return pool.tensor_tensor(dst, src, one, ALU.mult)

                w = W[u]
                k, q, ks, qs = kraw[u][:, :, :], qraw[u][:, :, :], kst[u], qst[u]
                pool.wait_ge(s[f"a_raw{u}"], 48 * (h + 1))
                do(copy(ks[:, :, 0:w].bitcast(F32R), k))
                do(copy(qs[:, :, 0:w].bitcast(F32R), q))
                if u == A:
                    do(pool.tensor_tensor(ks[:, :, w:2 * w].bitcast(F32R), k, ks[:, :, 0:w], ALU.subtract))
                    do(copy(qs[:, :, w:2 * w], qs[:, :, 0:w]))
                    ins = pool.tensor_tensor(qst2[:, :, 0:w].bitcast(F32R), q, qs[:, :, 0:w], ALU.subtract)
                else:
                    do(pool.tensor_tensor(ks[:, :, 2 * w:3 * w].bitcast(F32R), k, ks[:, :, 0:w], ALU.subtract))
                    do(copy(ks[:, :, w:2 * w], ks[:, :, 0:w]))
                    do(copy(qs[:, :, 2 * w:3 * w], qs[:, :, 0:w]))
                    ins = pool.tensor_tensor(qs[:, :, w:2 * w].bitcast(F32R), q, qs[:, :, 0:w], ALU.subtract)
                ins.then_inc(s[f"a_split{u}"], 1)

            pool.wait_ge(s["a_ones"], 1)
            nA, nB = 4, 5
            split(A, 0, 0)
            split(B, 0, nA)
            with pool.Fori(0, TURNS - 1) as h:
                pool.wait_ge(s["a_work"], PREP * (unit(A, h) + 1))
                split(A, h + 1, (h + 1) * (nA + nB))
                pool.wait_ge(s["a_work"], PREP * (unit(B, h) + 1))
                split(B, h + 1, (h + 1) * (nA + nB) + nA)

        @block.tensor
        def _(pe):
            def prep(u, h, i):
                p = unit(u, h)
                bank = wk[i % 2]
                first_unit = isinstance(h, int) and h == 0 and u == A
                if i < 2:
                    if not first_unit:
                        pe.wait_ge(s["a_wkdve"], (PREP - PREP_MAX) * p - 1 + i)
                elif i < PREP_MAX:
                    pe.wait_ge(s["a_wkact"], PREP_MAX * p + i - 1)
                elif i < PREP_MAX + 2:
                    pe.wait_ge(s["a_wkact"], PREP_MAX * p + PREP_MAX)
                else:
                    pe.wait_ge(s["a_wkdve"], (PREP - PREP_MAX) * p + i - 1 - PREP_MAX)
                if i == 0:
                    pe.wait_ge(s[f"a_split{u}"], h + 1)
                if i == PREP_LAST:
                    pe.wait_ge(s["a_nm"], p + 1)
                w = W[u]
                if i < PREP_Q:
                    for j in range(4):
                        mm = pe.transpose(bank[0:KR[u], j * P:(j + 1) * P], kst[u][:, 4 * i + j, :], per["ident"][:, :])
                elif i < PREP_MAX or i >= PREP_LAST:
                    g = i - (PREP_Q if i < PREP_MAX else PREP_LAST)
                    src = (qst2 if u == A else qst[u]) if i >= PREP_LAST else qst[u]
                    rows = (w + 2 if u == A else KR[u]) if i >= PREP_LAST else (P if u == A else w)
                    for t in range(4 * g, min(4 * g + 4, T)):
                        mm = pe.transpose(bank[0:rows, (t - 4 * g) * P:(t - 4 * g + 1) * P], src[:, t, 0:rows], per["ident"][:, :])
                else:
                    m = i - PREP_MAX
                    if m < 2 * TS:
                        parts = [(m // 2, (m % 2) * NB, NB)]
                    else:
                        q0 = 2 * (m - 2 * TS)
                        keys0 = 2 * NB if q0 < TS else KT_S * P
                        parts = [(q0, keys0, SEQ), (q0 + 1, keys0, SEQ)]
                    for x, (t, k0, n) in enumerate(parts):
                        mm = pe.matmul(bank[:, x * SEQ:x * SEQ + n], qT[u][0:w, tile_rows(t)], kT[u][0:w, k0:k0 + n],
                                       start=True, stop=True)
                mm.then_inc(s["a_work"], 1)

            def scores(u, h, j):
                n = step0(u, h) + j
                if not (isinstance(h, int) and h == 0 and u == A and j < 2):
                    pe.wait_ge(s["a_exp"], n - 1)
                if j == 0:
                    pe.wait_ge(s["a_wkdve"], (PREP - PREP_MAX) * (unit(u, h) + 1))
                slot = sc[(j + (0 if u == A else ATT_STEPS)) % 2]
                for c in range(2):
                    if j < KT_S:
                        keys, q, out = tile_rows(j), slice(c * NB, (c + 1) * NB), slot[:, c, :]
                    else:
                        keys, q, out = tile_rows(KT_S + c), slice(DEC_SEQ, TOK), slot[:, c, 0:SEQ]
                    if u == A:
                        pe.matmul(out, kT[u][:, keys], qT[u][:, q], start=True, stop=False)
                        mm = pe.matmul(out, kT2[:, keys], qT2[u][:, q], start=False, stop=True)
                    else:
                        mm = pe.matmul(out, kT[u][:, keys], qT2[u][:, q], start=True, stop=True)
                mm.then_inc(s["a_scores"], 1)

            def weigh(u, h, j, part):
                n = step0(u, h) + j
                pb = pr[:, (j + (0 if u == A else ATT_STEPS)) % 2, :]
                if part == 0:
                    pe.wait_ge(s["a_exp"], n + 1)
                    if j == 0:
                        pe.wait_ge(s[f"a_v{u}"], 32 * (h + 1))
                        pe.wait_ge(s["a_out"], unit(u, h) + 1)
                if j < KT_S:
                    work = [(t, pb[:, tile_rows(t)], j) for t in range(part * 4, part * 4 + 4)]
                else:
                    t = TS + part
                    work = [(t, pb[:, c * NB + part * P:c * NB + (part + 1) * P], KT_S + c) for c in range(2)]
                for t, probs, key in work:
                    o = ob[:, t // HALF, (t % HALF) * (HEAD_DIM + 1):(t % HALF + 1) * (HEAD_DIM + 1)]
                    mm = pe.matmul(o, probs, v[u][:, key, :], start=(j == 0 and t % HALF == 0),
                                   stop=(j == KT_S - 1 or (j == KT_S and key == KT - 1)), skip_group_check=True)
                if part == 1:
                    mm.then_inc(s["a_pv"], 1)

            def run_unit(u, h, nxt):
                for j in range(ATT_STEPS - 2):
                    uses = list(range(3 * j, 3 * j + 3)) if nxt else []
                    for part in range(2):
                        if nxt:
                            prep(*nxt, uses[part])
                        weigh(u, h, j, part)
                    if nxt:
                        prep(*nxt, uses[2])
                    scores(u, h, j + 2)
                j = ATT_STEPS - 2
                weigh(u, h, j, 0)
                weigh(u, h, j, 1)
                if nxt:
                    for i in range(PREP_LAST, PREP):
                        prep(*nxt, i)
                weigh(u, h, j + 1, 0)
                weigh(u, h, j + 1, 1)
                if nxt:
                    scores(*nxt, 0)
                    scores(*nxt, 1)

            for i in range(PREP):
                prep(A, 0, i)
            scores(A, 0, 0)
            scores(A, 0, 1)
            with pe.Fori(0, TURNS - 1) as h:
                run_unit(A, h, (B, h))
                run_unit(B, h, (A, h + 1))
            run_unit(A, TURNS - 1, (B, TURNS - 1))
            run_unit(B, TURNS - 1, None)

        @block.scalar
        def _(act):
            def stand(u, h, i):
                p = unit(u, h)
                act.wait_ge(s["a_work"], PREP * p + i + 1)
                bank = wk[i % 2]
                if i < PREP_Q:
                    cols = slice(i * NB, (i + 1) * NB)
                    ins = act.copy(kT[u][:, cols], bank[0:KR[u], :])
                    if u == A:
                        ins = act.copy(kT2[0:HEAD_DIM, cols], bank[0:HEAD_DIM, :])
                else:
                    cols = slice((i - PREP_Q) * NB, min((i - PREP_Q + 1) * NB, TOK))
                    ins = act.copy(qT[u][:, cols], bank[0:(P if u == A else B_QK), 0:cols.stop - cols.start])
                ins.then_inc(s["a_wkact"], 1)

            def exps(u, h, j):
                n = step0(u, h) + j
                b = (j + (0 if u == A else ATT_STEPS)) % 2
                act.wait_ge(s["a_scores"], n + 1)
                if j < KT_S:
                    act.activation(pr[:, b, :], sc[b][:, :, :].rearrange("p c n -> p (c n)"), ACT.Exp,
                                   scale=SCALE[u]).then_inc(s["a_exp"], 1)
                else:
                    act.activation(pr[:, b, :].rearrange("p (c n) -> p c n", c=2)[:, :, 0:SEQ], sc[b][:, :, 0:SEQ], ACT.Exp,
                                   scale=SCALE[u]).then_inc(s["a_exp"], 1)

            def run_unit(u, h, nxt):
                for j in range(ATT_STEPS):
                    exps(u, h, j)
                    if nxt and j < 2:
                        for i in range(3 * j, 3 * j + 3):
                            stand(*nxt, i)

            for i in range(PREP_MAX):
                stand(A, 0, i)
            with act.Fori(0, TURNS - 1) as h:
                run_unit(A, h, (B, h))
                run_unit(B, h, (A, h + 1))
            run_unit(A, TURNS - 1, (B, TURNS - 1))
            run_unit(B, TURNS - 1, None)

        @block.vector
        def _(dve):
            def own(u, h, n):
                return 2 * unit(u, h) + n

            def maxima(u, h):
                p = unit(u, h)
                for i in range(PREP_MAX, PREP_LAST):
                    m = i - PREP_MAX
                    dve.wait_ge(s["a_work"], PREP * p + i + 1)
                    if m < 2 * TS:
                        dst, src = nmx[:, m // 2, m % 2:m % 2 + 1], wk[i % 2][:, :]
                    else:
                        q0 = 2 * (m - 2 * TS)
                        dst = nmx[:, q0:q0 + 2, 2] if q0 < TS else nm[:, TS:T]
                        src = wk[i % 2][:, :].rearrange("p (t n) -> p t n", t=2)
                    dve.tensor_reduce(dst, src, AX_X, ALU.max, negate=True).then_inc(s["a_wkdve"], 1)
                dve.wait_ge(s["a_wkdve"], (PREP - PREP_MAX) * p + PREP_LAST - PREP_MAX)
                dve.tensor_reduce(nm[:, 0:TS], nmx[:, 0:TS, :], AX_X, ALU.min).then_inc(s["a_own"], 1)
                dve.wait_ge(s["a_own"], own(u, h, 1))
                mc = m_cols[u]
                dve.tensor_copy(mc[:, :, 0].bitcast(F32R), nm[:, :]).then_inc(s["a_own"], 1)
                dve.wait_ge(s["a_own"], own(u, h, 2))
                dve.tensor_tensor(mc[:, :, 1].bitcast(F32R), nm[:, :], mc[:, :, 0], ALU.subtract).then_inc(s["a_nm"], 1)
                rows = HEAD_DIM + 2 if u == A else KR[u]
                for i in range(PREP_LAST, PREP):
                    cols = slice((i - PREP_LAST) * NB, min((i - PREP_LAST + 1) * NB, TOK))
                    dve.wait_ge(s["a_work"], PREP * p + i + 1)
                    dve.tensor_copy(qT2[u][:, cols], wk[i % 2][0:rows, 0:cols.stop - cols.start]).then_inc(s["a_wkdve"], 1)

            def output(u, h):
                p = unit(u, h)
                o = ob[:, :, 0:HALF * (HEAD_DIM + 1)].rearrange("p b (t e) -> p b t e", e=HEAD_DIM + 1)
                dve.wait_ge(s["a_pv"], step0(u, h) + ATT_STEPS)
                dve.reciprocal(rs[:, :, :], o[:, :, :, HEAD_DIM]).then_inc(s["a_rs"], 1)
                dve.wait_ge(s["a_rs"], p + 1)
                if u == A:
                    dst = mid["oa"][:, :, bass.ds(h * HEAD_DIM, HEAD_DIM)].rearrange("p (b t) e -> p b t e", b=2)
                else:
                    dst = mid["ob"][:, bass.ds(h, 1), :, :].rearrange("p a (b t) e -> p (a b) t e", b=2)
                r = rs[:, :, :].unsqueeze(3).broadcast_to([P, 2, HALF, HEAD_DIM])
                dve.tensor_tensor(dst, o[:, :, :, 0:HEAD_DIM], r, ALU.mult).then_inc(s["a_out"], 1)

            dve.memset(v[A][:, :, HEAD_DIM:], 1.0).then_inc(s["a_out"], 1)
            dve.memset(v[B][:, :, HEAD_DIM:], 1.0)
            dve.memset(kT2[HEAD_DIM:, :].bitcast(F32), 1.0)
            dve.memset(kst[B][:, :, 3 * B_QK:], 1.0).then_inc(s["a_ones"], 1)
            maxima(A, 0)
            with dve.Fori(0, TURNS - 1) as h:
                maxima(B, h)
                output(A, h)
                maxima(A, h + 1)
                output(B, h)
            maxima(B, TURNS - 1)
            output(A, TURNS - 1)
            output(B, TURNS - 1)


def output_block(nc, l, io, per, mid, s):
    BV = B_HEADS * B_V
    AW = A_HEADS * HEAD_DIM
    with ExitStack() as ctx:
        def sb(name, shape, dt=F32):
            return ctx.enter_context(nc.sbuf_tensor(name, shape, dt))

        wst = sb("wo_stage", [P, 2, D_MODEL])
        w_hi = sb("wo_hi", [P, KD, D_MODEL], F32R)
        w_lo = sb("wo_lo", [P, KD, D_MODEL], F32R)
        ones = sb("ones", [P, P])
        gp = sb("post_rows", [P, 2, D_MODEL])
        su = per["cv"][:, :, :].rearrange("p t c -> p (t c)")[:, 0:2 * D_MODEL].rearrange("p (b c) -> p b c", b=2)
        xt = sb("xo_tiles", [P, 2, D_MODEL])
        yt = sb("y_tiles", [P, 2, D_MODEL])
        diag = yt[:, :, :].rearrange("p g (k n) -> p g k n", n=P)
        mx = sb("mixed", [P, D_MODEL])
        bo = sb("b_out", [P, 2, B_HEADS, B_V])
        bsq = sb("b_sq", [P, B_HEADS, B_V])
        bst = sb("b_stats", [P, 2, 3, B_HEADS])
        yst = sb("y_stats", [P, 3, T])
        m_hi = sb("mT_hi", [P, 2, KD, P], F32R)
        m_lo = sb("mT_lo", [P, 2, KD, P], F32R)
        tp = [ctx.enter_context(nc.psum_tensor(f"m_tr{i}", [P, KD, P], F32)) for i in range(2)]
        yp = [ctx.enter_context(nc.psum_tensor(f"y_acc{i}", [P, D_MODEL], F32)) for i in range(2)]
        block = ctx.enter_context(nc.Block())

        def group(t):
            return 0 if t < TS else 1

        @block.sync
        def _(sp):
            def load_tile(t):
                if t >= 2:
                    sp.wait_ge(s["o_mix"], t - 1)
                sp.dma_start(su[:, t % 2, :], io["Us"][tile_rows(t), :]).then_inc(s[f"o_su{t % 2}"], 16)
                if t >= 2:
                    sp.wait_ge(s["o_y"], t - 1)
                new, old, r = ((io["y_sample"], io["x_sample"], t * P) if t < TS
                               else (io["y_prompt"], io["x_prompt"], (t - TS) * P))
                with sp.If(l < 1):
                    sp.dma_start(xt[:, t % 2, :], old[r:r + P, :]).then_inc(s[f"o_x{t % 2}"], 16)
                with sp.Else():
                    sp.dma_start(xt[:, t % 2, :], new[r:r + P, :]).then_inc(s[f"o_x{t % 2}"], 16)

            def store(t):
                dst, r = (io["y_sample"], t * P) if t < TS else (io["y_prompt"], (t - TS) * P)
                sp.wait_ge(s["o_y"], t + 1)
                sp.dma_start(dst[r:r + P, :], yt[:, t % 2, :]).then_inc(s[f"o_st{t % 2}"], 16)

            load_tile(0)
            load_tile(1)
            for k in range(KD):
                if k >= 2:
                    sp.wait_ge(s["o_wlo"], k - 1)
                sp.dma_start(wst[:, k % 2, :], io["w_out"][bass.ds(l, 1), k * P:(k + 1) * P, :].rearrange("a p n -> (a p) n")
                             ).then_inc(s[f"o_w{k % 2}"], 16)
            for t in range(T):
                if t + 2 < T:
                    load_tile(t + 2)
                store(t)
            for i in range(2):
                sp.wait_ge(s[f"o_st{i}"], 16 * T // 2)

        @block.tensor
        def _(pe):
            pe.wait_ge(s["o_diag"], 1)
            for g in range(2):
                for k in range(KD):
                    mm = pe.matmul(yp[g][:, k * P:(k + 1) * P], ones[:, :], diag[:, g, k, :], start=True, stop=True)
                mm.then_inc(s["o_gp"], 1)

            def turn(t):
                pe.wait_ge(s["o_mix"], t + 1)
                if t >= 2:
                    pe.wait_ge(s["o_mlo"], t - 1)
                for k in range(KD):
                    mm = pe.transpose(tp[t % 2][:, k, :], mx[:, k * P:(k + 1) * P], per["ident"][:, :])
                mm.then_inc(s["o_turned"], 1)

            turn(0)
            turn(1)
            for t in range(T):
                pe.wait_ge(s["o_mlo"], t + 1)
                if t < 2:
                    pe.wait_ge(s["o_gpcopy"], t + 1)
                else:
                    pe.wait_ge(s["o_y1"], t - 1)
                for c in range(2):
                    cols = slice(c * NB, (c + 1) * NB)
                    for k in range(KD):
                        if t == 0:
                            pe.wait_ge(s["o_wlo"], k + 1)
                        for q, (mm_, ww) in enumerate(((m_hi, w_hi), (m_hi, w_lo), (m_lo, w_hi))):
                            mm = pe.matmul(yp[t % 2][:, cols], mm_[:, t % 2, k, :], ww[:, k, cols],
                                           start=(k == 0 and q == 0), stop=(k == KD - 1 and q == 2))
                mm.then_inc(s["o_acc"], 1)
                if t + 2 < T:
                    turn(t + 2)

        @block.scalar
        def _(act):
            def b_std(t):
                act.wait_ge(s["o_bss"], t + 1)
                act.activation(bst[:, t % 2, 1, :], bst[:, t % 2, 0, :], ACT.Sqrt, bias=per["eps"][:, :],
                               scale=1.0 / B_V).then_inc(s["o_bstd"], 1)

            def hi(t):
                act.wait_ge(s["o_turned"], t + 1)
                if t >= 2:
                    act.wait_ge(s["o_acc"], t - 1)
                act.copy(m_hi[:, t % 2, :, :], tp[t % 2][:, :, :]).then_inc(s["o_mhi"], 1)

            def w_split(k):
                act.wait_ge(s[f"o_w{k % 2}"], 16 * (k // 2 + 1))
                act.copy(w_hi[:, k, :], wst[:, k % 2, :]).then_inc(s["o_whi"], 1)

            for g in range(2):
                act.wait_ge(s["o_gp"], g + 1)
                act.copy(gp[:, g, :], yp[g][:, :]).then_inc(s["o_gpcopy"], 1)
            b_std(0)
            w_split(0)
            w_split(1)
            b_std(1)
            hi(0)
            w_split(2)
            w_split(3)
            b_std(2)
            hi(1)
            for k in range(4, KD):
                w_split(k)
            for t in range(T):
                if t + 3 < T:
                    b_std(t + 3)
                act.wait_ge(s["o_acc"], t + 1)
                if t >= 2:
                    act.wait_ge(s[f"o_st{t % 2}"], 16 * (t // 2))
                act.activation(yt[:, t % 2, :], yp[t % 2][:, :], ACT.Square, accum_out=yst[:, 0, t:t + 1]).then_inc(s["o_sq"], 1)
                act.wait_ge(s["o_sq"], t + 1)
                act.activation(yst[:, 1, t:t + 1], yst[:, 0, t:t + 1], ACT.Sqrt, bias=per["eps"][:, :],
                               scale=1.0 / D_MODEL).then_inc(s["o_std"], 1)
                if t + 2 < T:
                    hi(t + 2)

        @block.vector
        def _(dve):
            do = Chain(dve, s["o_dve"])
            dve.memset(ones[:, :], 1.0)
            for g in range(2):
                for k in range(KD):
                    ins = dve.tensor_scalar(diag[:, g, k, :], per["ident"][:, :], per["post"][:, g, k:k + 1], None, ALU.mult)
            ins.then_inc(s["o_diag"], 1)

            def b_diff(t):
                o = mid["ob"]
                if t >= 2:
                    dve.wait_ge(s["o_mix"], t - 1)
                do(dve.scalar_tensor_tensor(out=bo[:, t % 2, :, :], in0=o[:, 1::2, t, :], scalar=per["neg_lam"][:, 0:1],
                                            in1=o[:, 0::2, t, :], op0=ALU.mult, op1=ALU.add))
                do(dve.tensor_tensor(bsq[:, :, :], bo[:, t % 2, :, :], bo[:, t % 2, :, :], ALU.mult))
                dve.tensor_reduce(bst[:, t % 2, 0, :], bsq[:, :, :], AX_X, ALU.add).then_inc(s["o_bss"], 1)

            def mix(t):
                b = t % 2
                dve.wait_ge(s["o_bstd"], t + 1)
                do(dve.reciprocal(bst[:, b, 2, :], bst[:, b, 1, :]))
                do(dve.tensor_tensor(bo[:, b, :, :], bo[:, b, :, :], bst[:, b, 2, :].unsqueeze(2).broadcast_to([P, B_HEADS, B_V]), ALU.mult))
                do(dve.tensor_tensor(bo[:, b, :, :], bo[:, b, :, :],
                                     per["gains"][:, 2, :].unsqueeze(1).broadcast_to([P, B_HEADS, B_V]), ALU.mult))
                dve.wait_ge(s[f"o_su{b}"], 16 * (t // 2 + 1))
                if t:
                    dve.wait_ge(s["o_turned"], t)
                dve.tensor_tensor(mx[:, 0:AW], mid["oa"][:, t, :], su[:, b, 0:AW], ALU.mult)
                dve.tensor_tensor(mx[:, AW:AW + BV], bo[:, b, :, :].rearrange("p h e -> p (h e)"), su[:, b, AW:AW + BV], ALU.mult)
                dve.tensor_tensor(mx[:, AW + BV:], mid["oc"][:, t, :], su[:, b, AW + BV:], ALU.mult).then_inc(s["o_mix"], 1)

            def lo(t):
                dve.wait_ge(s["o_mhi"], t + 1)
                dve.tensor_tensor(m_lo[:, t % 2, :, :], tp[t % 2][:, :, :], m_hi[:, t % 2, :, :].bitcast(F32),
                                  ALU.subtract).then_inc(s["o_mlo"], 1)

            def w_lo_part(k):
                dve.wait_ge(s["o_whi"], k + 1)
                dve.tensor_tensor(w_lo[:, k, :], wst[:, k % 2, :], w_hi[:, k, :].bitcast(F32), ALU.subtract).then_inc(s["o_wlo"], 1)

            def finish(t):
                b, g = t % 2, group(t)
                dve.wait_ge(s["o_std"], t + 1)
                do(dve.reciprocal(yst[:, 2, t:t + 1], yst[:, 1, t:t + 1]))
                dve.wait_ge(s["o_gpcopy"], 2)
                dve.scalar_tensor_tensor(out=yt[:, b, :], in0=yp[b][:, :], scalar=yst[:, 2, t:t + 1], in1=gp[:, g, :],
                                         op0=ALU.mult, op1=ALU.mult).then_inc(s["o_y1"], 1)
                dve.wait_ge(s["o_y1"], t + 1)
                dve.wait_ge(s[f"o_x{b}"], 16 * (t // 2 + 1))
                dve.tensor_tensor(yt[:, b, :], yt[:, b, :], xt[:, b, :], ALU.add).then_inc(s["o_y"], 1)

            b_diff(0)
            b_diff(1)
            w_lo_part(0)
            w_lo_part(1)
            mix(0)
            lo(0)
            w_lo_part(2)
            w_lo_part(3)
            b_diff(2)
            mix(1)
            lo(1)
            for k in range(4, KD):
                w_lo_part(k)
            for t in range(T):
                if t + 3 < T:
                    b_diff(t + 3)
                if t + 2 < T:
                    mix(t + 2)
                finish(t)
                if t + 2 < T:
                    lo(t + 2)


def prologue_block(nc, io, per, s):
    with ExitStack() as ctx:
        crow = ctx.enter_context(nc.sbuf_tensor("cond_rows", [2 * KD, P], F32))
        tr = ctx.enter_context(nc.psum_tensor("cond_tr", [P, NB], F32))
        block = ctx.enter_context(nc.Block())
        loads = [(per["ident"][:, :], io["ident"]), (crow[0:KD, :], io["c"].rearrange("b (k p) -> (b k) p", p=P)),
                 (crow[KD:, :], io["c_ctx"].rearrange("(k p) -> k p", p=P)),
                 (per["tri"][:, :, :], io["tri"]), (per["bdmask"][:, :], io["bdmask"]),
                 (per["cosA"][:, :, :], io["ropeA"][0].rearrange("(t p) d -> p t d", p=P)),
                 (per["sinA"][:, :, :], io["ropeA"][1].rearrange("(t p) d -> p t d", p=P)),
                 (per["cosB"][:, :, :], io["ropeB"][0].rearrange("(t p) d -> p t d", p=P)),
                 (per["sinB"][:, :, :], io["ropeB"][1].rearrange("(t p) d -> p t d", p=P))]

        @block.sync
        def _(sp):
            for dst, src in loads:
                sp.dma_start(dst, src).then_inc(s["c_load"], 16)

        @block.vector
        def _(dve):
            dve.memset(per["eps"][:, :], EPS).then_inc(s["c_set"], 1)
            dve.memset(per["gate_w"][:, :], 0.0).then_inc(s["c_set"], 1)
            dve.memset(per["lrT"][2 * RANK:2 * RANK + 1, :], 1.0).then_inc(s["c_set"], 1)
            dve.memset(per["one"][:, :], 1.0).then_inc(s["c_set"], 1)
            dve.wait_ge(s["c_set"], 4)

        @block.tensor
        def _(pe):
            pe.wait_ge(s["c_load"], 16 * len(loads))
            pe.transpose(tr[:, 0:2 * KD], crow[:, :], per["ident"][0:2 * KD, 0:2 * KD]).then_inc(s["c_tr"], 1)

        @block.scalar
        def _(act):
            act.wait_ge(s["c_tr"], 1)
            act.activation(per["cond"][:, :, :].rearrange("p k g -> p g k"), tr[:, 0:2 * KD].rearrange("p (g k) -> p g k", g=2),
                           ACT.Silu).then_inc(s["c_silu"], 1)
            act.wait_ge(s["c_silu"], 1)


SEMS = (["c_load", "c_set", "c_tr", "c_silu"]
        + ["m_small", "m_used", "m_tr", "m_dot", "m_exp", "m_dve"] + [f"m_w{i}" for i in range(3)]
        + ["p_x0", "p_x1", "p_xn", "p_wlo", "p_whi", "p_zo", "p_ev", "p_turned", "p_h32", "p_hhi", "p_h", "p_acc", "p_wfree",
           "p_sq", "p_std", "p_hss", "p_hstd", "p_dve"]
        + ["g_zero", "g_st0", "g_chain", "g_new", "g_min", "g_pre", "g_gate", "g_exp", "g_cum", "g_mul", "g_k2t", "g_tr", "g_am",
           "g_at", "g_dsm", "g_ds", "g_oi", "g_o", "g_oc", "g_inter", "g_act", "g_abs", "g_ln", "g_css", "g_cstd", "g_dve"]
        + ["a_ones", "a_rawA", "a_rawB", "a_vA", "a_vB", "a_splitA", "a_splitB", "a_pv", "a_pool", "a_work", "a_wkdve", "a_wkact",
           "a_nm", "a_exp", "a_scores", "a_out", "a_own", "a_rs"]
        + ["o_mix", "o_su0", "o_su1", "o_y", "o_x0", "o_x1", "o_st0", "o_st1", "o_wlo", "o_w0", "o_w1", "o_diag", "o_gp", "o_mlo",
           "o_turned", "o_gpcopy", "o_y1", "o_acc", "o_bss", "o_bstd", "o_mhi", "o_whi", "o_sq", "o_std", "o_dve"]
        + [f"p_w{i}" for i in range(STAGES)] + [f"p_out{i}" for i in range(3)] + [f"p_new{i}" for i in range(3)])


def program(nc, io):
    with ExitStack() as ctx:
        def sb(name, shape, dt=F32):
            return ctx.enter_context(nc.sbuf_tensor(name, shape, dt))

        s = {n: ctx.enter_context(nc.semaphore(n)) for n in SEMS}
        per = {
            "ident": sb("ident", [P, P]), "tri": sb("tri", [P, 2, P]), "bdmask": sb("bdmask", [P, C_HEADS]),
            "cosA": sb("cosA", [P, TS, HEAD_DIM]), "sinA": sb("sinA", [P, TS, HEAD_DIM]),
            "cosB": sb("cosB", [P, TS, B_QK]), "sinB": sb("sinB", [P, TS, B_QK]),
            "cond": sb("cond", [P, KD, 2]), "eps": sb("eps", [P, 1]), "one": sb("one", [P, 1]),
            "gains": sb("gains", [P, 4, HEAD_DIM]), "neg_lam": sb("neg_lam", [P, 1]),
            "h_scale": sb("h_scale", [P, 2, KD]), "h_shift": sb("h_shift", [P, 2, KD]), "post": sb("post", [P, 2, KD]),
            "gate_w": sb("gate_w", [2 * RANK + 1, 2 * C_HEADS * C_DK]), "lrT": sb("lrT", [2 * RANK + 1, TOK]),
            "cqT": sb("cqT", [P, TOK]), "ckT": sb("ckT", [P, TOK]), "cv": sb("cv", [P, T, C_HEADS * C_DV]),
        }
        io["Zs"] = nc.dram_tensor("z_scratch", [TOK, Z_COLS], F32).ap()
        io["Us"] = nc.dram_tensor("u_scratch", [TOK, D_MODEL], F32).ap()
        prologue_block(nc, io, per, s)
        with nc.Fori(0, DEPTH) as l:
            modulation_block(nc, l, io, per, s)
            projection_block(nc, l, io, per, s)
            with ExitStack() as branch:
                mid = {n: branch.enter_context(nc.sbuf_tensor(n, shape, F32)) for n, shape in (
                    ("oa", [P, T, A_HEADS * HEAD_DIM]), ("ob", [P, 2 * B_HEADS, T, B_V]), ("oc", [P, T, C_HEADS * C_DV]))}
                gla_block(nc, l, io, per, mid, s)
                attention_block(nc, l, io, per, mid, s)
                output_block(nc, l, io, per, mid, s)
            nc.all_engine_barrier(sems_to_clear=range(s[SEMS[4]].num, s[SEMS[-1]].num + 1))


_OUTS = {"y_prompt": (1, SEQ, D_MODEL), "y_sample": (1, DEC_SEQ, D_MODEL),
         "new_a_k": (1, DEPTH, A_KV, SEQ, HEAD_DIM), "new_a_v": (1, DEPTH, A_KV, SEQ, HEAD_DIM),
         "new_b_k": (1, DEPTH, B_HEADS, SEQ, 2 * B_QK), "new_b_v": (1, DEPTH, B_HEADS, SEQ, B_V),
         "new_state_c_fwd": (1, DEPTH, C_HEADS, C_DK, C_DV), "new_state_c_bwd": (1, DEPTH, C_HEADS, C_DK, C_DV)}


def shape_constants():
    import numpy as np

    f = np.float32
    j, i = np.arange(P)[:, None], np.arange(P)[None, :]
    same = j // 64 == i // 64
    tri = np.stack([same & (j <= i), same & (j >= i)], 1).astype(f)
    bd = (np.arange(P)[:, None] // C_DK == np.arange(C_HEADS)[None, :]).astype(f)
    t = np.arange(DEC_SEQ)

    def rope(d):
        half = d // 4
        freq = (f(ROPE_THETA) ** (-np.arange(half, dtype=f) / f(half))).astype(f)
        cos, sin = [], []
        for pos in (t // GRID_W, t % GRID_W):
            ang = pos.astype(f)[:, None] * freq[None, :]
            cos += [np.cos(ang), np.cos(ang)]
            sin += [-np.sin(ang), np.sin(ang)]
        return np.stack([np.concatenate(cos, 1), np.concatenate(sin, 1)]).astype(f)

    lam = np.array([[0.8 - 0.6 * np.exp(-0.3 * l), 0.2 + 0.6 * np.exp(-0.3 * l)] for l in range(DEPTH)], f)
    return {"ident": np.eye(P, dtype=f), "tri": tri, "bdmask": bd, "ropeA": rope(HEAD_DIM), "ropeB": rope(B_QK),
            "lam_consts": lam}


def kernel(**inputs):
    import numpy as np
    import concourse.bacc as bacc
    from concourse.bass_utils import run_bass_kernel_spmd

    nc = bacc.Bacc("TRN2", target_bir_lowering=False, num_devices=1)
    arrays, io = {}, {}
    for name, a in {**inputs, **shape_constants()}.items():
        a = np.ascontiguousarray(a)
        arrays[f"in_{name}"] = a
        io[name] = nc.dram_tensor(f"in_{name}", a.shape, mybir.dt.from_np(a.dtype), kind="ExternalInput").ap()
    for name, shape in _OUTS.items():
        io[name] = nc.dram_tensor(f"out_{name}", shape, F32, kind="ExternalOutput").ap()
    for name in ("x_prompt", "x_sample", "y_prompt", "y_sample"):
        io[name] = io[name].rearrange("b t d -> (b t) d")
    for name in ("new_a_k", "new_a_v", "new_b_k", "new_b_v", "new_state_c_fwd", "new_state_c_bwd",
                 "cache_a_k", "cache_a_v", "cache_b_k", "cache_b_v", "state_c_fwd", "state_c_bwd"):
        io[name] = io[name].rearrange("b l h x y -> (b l) h x y")
    program(nc, io)
    r = run_bass_kernel_spmd(nc, [arrays], core_ids=[0])
    return tuple(r.results[0][f"out_{name}"] for name in _OUTS)
```

```python
from contextlib import ExitStack

import concourse.bass as bass
from concourse import mybir

F32 = mybir.dt.float32
F32R = mybir.dt.float32r
ACT = mybir.ActivationFunctionType
ALU = mybir.AluOpType
AX_X = mybir.AxisListType.X

P = 128
D_MODEL = 1024
DEPTH = 2
SEQ, DEC_SEQ, PAST = 256, 1024, 256
GRID_W = 64
HEAD_DIM = 64
A_HEADS, A_KV = 8, 2
B_HEADS, B_QK, B_V = 4, 32, 64
C_HEADS, C_DK, C_DV = 4, 32, 64
RANK, TAU = 16, 16.0
EPS = 1e-6
ROPE_THETA = 10000.0

KD = D_MODEL // P
TS = DEC_SEQ // P
TP = SEQ // P
T = TS + TP
TOK = T * P
NB = 512
Z_COLS = 3 * NB
C_COL0 = Z_COLS
LR_COL0 = C_COL0 + NB
U_COL0 = LR_COL0 + 2 * RANK
IN_WIDTH = U_COL0 + D_MODEL

BLOCKS = [("z", 2 * NB, NB), ("z", 0, NB), ("z", NB, NB), ("c", C_COL0, NB), ("lr", LR_COL0, P),
          ("u", U_COL0, NB), ("u", U_COL0 + NB, NB)]
Z_BLOCKS = 3
RING = 12
STAGES = 3


def tile_rows(t):
    return slice(t * P, (t + 1) * P)


class Chain:

    def __init__(self, eng, sem):
        self.eng, self.sem, self.n = eng, sem, 0

    def __call__(self, ins):
        self.n += 1
        ins.then_inc(self.sem, 1)
        self.eng.wait_ge(self.sem, self.n)


def modulation_block(nc, l, io, per, s):
    NT = 3 * KD
    WST, KH = 4, KD // 2
    CH = 3 * D_MODEL // NB
    MB = NB // P
    with ExitStack() as ctx:
        def sb(name, shape, dt=F32):
            return ctx.enter_context(nc.sbuf_tensor(name, shape, dt))

        wst = sb("mod_w", [P, WST, KH, NB])
        w_hi = sb("mod_w_hi", [P, 2, KH, NB], F32R)
        w_lo = sb("mod_w_lo", [P, 2, KH, NB], F32R)
        cond = sb("mod_cond", [P, KD, P], F32R)
        parts = sb("mod_parts", [2 * 2, CH, NB])
        rows = sb("mod_rows", [NT + 2 * KD, P])
        lams = sb("mod_lams", [P, 4, B_QK])
        prod = sb("mod_prod", [P, 2, B_QK])
        dots = sb("mod_dots", [P, 2])
        lam_c = sb("mod_lam_c", [P, 2])
        mod = sb("mod_cols", [P, 2, NT])
        one_scale = sb("mod_one_scale", [P, 2, KD])
        bcols = sb("mod_bcols", [P, NT + 2 * KD])
        acc = [ctx.enter_context(nc.psum_tensor(f"mod_acc{i}", [P, NB], F32)) for i in range(2)]
        tr = ctx.enter_context(nc.psum_tensor("mod_tr", [P, NB], F32))
        col = ctx.enter_context(nc.psum_tensor("mod_col", [P, NT, 4], F32))
        block = ctx.enter_context(nc.Block())

        def layer(ap):
            return ap[bass.ds(l, 1)]

        @block.sync
        def _(sp):
            def load_w(i):
                c, k0 = i // 2, (i % 2) * KH
                if i >= WST:
                    sp.wait_ge(s["m_lo"], i - WST + 1)
                src = io["w_mod"][bass.ds(l, 1), k0 * P:(k0 + KH) * P, c * NB:(c + 1) * NB]
                sp.dma_start(wst[:, i % WST, :, :], src.rearrange("a (k p) n -> p (a k) n", p=P)).then_inc(s[f"m_w{i % WST}"], 16)

            for i in range(WST):
                load_w(i)
            sp.dma_start(rows[0:NT, :], layer(io["b_mod"]).rearrange("a (m p) -> (a m) p", p=P)).then_inc(s["m_small"], 16)
            sp.dma_start(rows[NT:NT + KD, :], layer(io["g_pre"]).rearrange("a (m p) -> (a m) p", p=P)).then_inc(s["m_small"], 16)
            sp.dma_start(rows[NT + KD:, :], layer(io["g_post"]).rearrange("a (m p) -> (a m) p", p=P)).then_inc(s["m_small"], 16)
            for i, name in enumerate(("b_lambda_q1", "b_lambda_k1", "b_lambda_q2", "b_lambda_k2")):
                sp.dma_start(lams[:, i, :], layer(io[name]).broadcast_to([P, B_QK])).then_inc(s["m_small"], 16)
            for i, name in enumerate(("a_q_gain", "a_k_gain", "b_out_gain", "c_out_gain")):
                sp.dma_start(per["gains"][:, i, :], layer(io[name]).broadcast_to([P, HEAD_DIM])).then_inc(s["m_small"], 16)
            sp.dma_start(lam_c[:, :], layer(io["lam_consts"]).broadcast_to([P, 2])).then_inc(s["m_small"], 16)
            C = C_HEADS * C_DK
            gw = per["gate_w"]
            sp.dma_start(gw[0:RANK, 0:C], layer(io["c_gate_w_fwd"]).rearrange("a r c -> (a r) c")).then_inc(s["m_small"], 16)
            sp.dma_start(gw[RANK:2 * RANK, C:2 * C], layer(io["c_gate_w_bwd"]).rearrange("a r c -> (a r) c")).then_inc(s["m_small"], 16)
            sp.dma_start(gw[2 * RANK:2 * RANK + 1, 0:C], layer(io["c_gate_b_fwd"])).then_inc(s["m_small"], 16)
            sp.dma_start(gw[2 * RANK:2 * RANK + 1, C:2 * C], layer(io["c_gate_b_bwd"])).then_inc(s["m_small"], 16)
            for i in range(WST, 2 * CH):
                load_w(i)

        @block.tensor
        def _(pe):
            def turn(c):
                pe.wait_ge(s["m_evac"], c + 1)
                for m in range(MB):
                    mm = pe.transpose(col[:, c * MB + m, :], parts[:, c, m * P:(m + 1) * P], per["ident"][0:4, 0:4])
                mm.then_inc(s["m_turned"], 1)

            pe.wait_ge(s["m_cond"], 2)
            for i in range(2 * CH):
                c = i // 2
                pe.wait_ge(s["m_lo"], i + 1)
                if i % 2 == 0 and c >= 2:
                    pe.wait_ge(s["m_evac"], c - 1)
                for kk in range(KH):
                    for q, w in enumerate((w_hi, w_lo)):
                        mm = pe.matmul(acc[c % 2][:, :], cond[:, (i % 2) * KH + kk, :], w[:, i % 2, kk, :],
                                       start=(i % 2 == 0 and kk == 0 and q == 0), stop=(i % 2 == 1 and kk == KH - 1 and q == 1))
                mm.then_inc(s["m_used"], 1)
                if i % 2 and c:
                    turn(c - 1)
            pe.wait_ge(s["m_small"], 16 * 16)
            pe.transpose(tr[:, 0:NT + 2 * KD], rows[:, :], per["ident"][0:NT + 2 * KD, 0:NT + 2 * KD]).then_inc(s["m_tr"], 1)
            turn(CH - 1)

        @block.scalar
        def _(act):
            def hi(i):
                act.wait_ge(s[f"m_w{i % WST}"], 16 * (i // WST + 1))
                if i >= 2:
                    act.wait_ge(s["m_used"], i - 1)
                act.copy(w_hi[:, i % 2, :, :], wst[:, i % WST, :, :]).then_inc(s["m_hi"], 1)

            hi(0)
            hi(1)
            for c in range(CH):
                if c + 1 < CH:
                    hi(2 * c + 2)
                act.wait_ge(s["m_used"], 2 * c + 2)
                act.copy(parts[:, c, :], acc[c % 2][0:4, :]).then_inc(s["m_evac"], 1)
                if c + 1 < CH:
                    hi(2 * c + 3)
            act.wait_ge(s["m_dot"], 2)
            act.activation(dots[:, :], dots[:, :], ACT.Exp).then_inc(s["m_exp"], 1)

        @block.vector
        def _(dve):
            do = Chain(dve, s["m_dve"])
            do(dve.memset(cond[:, :, :].bitcast(F32), 0.0))
            do(dve.tensor_copy(cond[:, :, 0:2], per["cond"][:, :, :]))
            dve.tensor_tensor(cond[:, :, 2:4], per["cond"][:, :, :], cond[:, :, 0:2].bitcast(F32), ALU.subtract).then_inc(s["m_cond"], 2)
            for i in range(2 * CH):
                dve.wait_ge(s["m_hi"], i + 1)
                dve.tensor_tensor(w_lo[:, i % 2, :, :], wst[:, i % WST, :, :], w_hi[:, i % 2, :, :].bitcast(F32),
                                  ALU.subtract).then_inc(s["m_lo"], 1)
            dve.wait_ge(s["m_small"], 16 * 16)
            do(dve.tensor_tensor(prod[:, :, :], lams[:, 0:4:2, :], lams[:, 1:4:2, :], ALU.mult))
            dve.tensor_reduce(dots[:, :], prod[:, :, :], AX_X, ALU.add).then_inc(s["m_dot"], 2)
            dve.wait_ge(s["m_exp"], 1)
            do(dve.tensor_tensor(per["neg_lam"][:, :], dots[:, 1:2], dots[:, 0:1], ALU.subtract))
            do(dve.tensor_tensor(per["neg_lam"][:, :], per["neg_lam"][:, :], lam_c[:, 0:1], ALU.subtract))
            do(dve.tensor_scalar(per["gains"][:, 2, :], per["gains"][:, 2, :], lam_c[:, 1:2], None, ALU.mult))
            dve.wait_ge(s["m_tr"], 1)
            do(dve.tensor_copy(bcols[:, :], tr[:, 0:NT + 2 * KD]))
            dve.wait_ge(s["m_turned"], CH)
            for g in range(2):
                do(dve.tensor_tensor(mod[:, g, :], col[:, :, g], bcols[:, 0:NT], ALU.add))
                do(dve.tensor_tensor(mod[:, g, :], mod[:, g, :], col[:, :, 2 + g], ALU.add))
                do(dve.tensor_copy(per["h_shift"][:, g, :], mod[:, g, 0:KD]))
                do(dve.tensor_scalar(one_scale[:, g, :], mod[:, g, KD:2 * KD], 1.0, None, ALU.add))
                do(dve.tensor_tensor(per["h_scale"][:, g, :], one_scale[:, g, :], bcols[:, NT:NT + KD], ALU.mult))
                do(dve.tensor_tensor(per["post"][:, g, :], mod[:, g, 2 * KD:], bcols[:, NT + KD:], ALU.mult))


def projection_block(nc, l, io, per, s):
    with ExitStack() as ctx:
        def sb(name, shape, dt=F32):
            return ctx.enter_context(nc.sbuf_tensor(name, shape, dt))

        h_hi = sb("h_hi", [P, KD, TOK], F32R)
        h_lo = sb("h_lo", [P, KD, TOK], F32R)
        w_hi = sb("w_hi", [P, RING, NB], F32R)
        w_lo = sb("w_lo", [P, RING, NB], F32R)
        stage = sb("w_stage", [P, STAGES, NB])
        xs = sb("x_tiles", [P, 2, D_MODEL])
        xn = sb("x_normed", [P, D_MODEL])
        h32 = sb("h32", [P, KD, P])
        ss = sb("x_stats", [P, 3, T])
        zt = sb("z_raw", [P, 3, NB])
        zo = sb("z_out", [P, 3, NB])
        tm = sb("z_tmp", [P, 3, NB])
        hst = sb("head_stats", [P, 2, 3, A_HEADS])
        tp = [ctx.enter_context(nc.psum_tensor(f"h_tr{i}", [P, KD, P], F32)) for i in range(2)]
        zp = [ctx.enter_context(nc.psum_tensor(f"z_acc{i}", [P, NB], F32)) for i in range(4)]
        block = ctx.enter_context(nc.Block())
        w_in, Zs, Us = io["w_in"], io["Zs"], io["Us"]
        NW = KD * len(BLOCKS)

        def group(t):
            return 0 if t < TS else 1

        uses = []
        for b, (kind, _, _) in enumerate(BLOCKS):
            if kind in ("z", "u"):
                uses += [(b, kind, t) for t in range(T)]
            elif kind == "c":
                uses += [(b, f"cT{m}", tb) for m in range(2) for tb in range(3)] + [(b, "cv", t) for t in range(T)]
            else:
                uses += [(b, "lr", tb) for tb in range(3)]
        first_use = {b: min(i for i, u in enumerate(uses) if u[0] == b) for b in range(len(BLOCKS))}
        last_use = {b: max(i for i, u in enumerate(uses) if u[0] == b) for b in range(len(BLOCKS))}
        U_USE0 = first_use[len(BLOCKS) - 2]

        def new_stores(slot, i):
            return sum(2 for j in range(slot, i, 3) if j % T >= TS and BLOCKS[j // T][1] > 0)

        def tok_block(tb):
            return slice(tb * NB, min((tb + 1) * NB, TOK))

        def free_ring(eng, n):
            b, k = divmod(n - RING, KD)
            if k < KD - 1:
                eng.wait_ge(s["p_wfree"], b * (KD - 1) + k + 1)
            else:
                eng.wait_ge(s["p_acc"], last_use[b] + 1)

        @block.sync
        def _(sp):
            def load_x(t):
                if t >= 2:
                    sp.wait_ge(s["p_xn"], t - 1)
                src_new = (io["y_sample"], t * P) if t < TS else (io["y_prompt"], (t - TS) * P)
                src_in = (io["x_sample"], t * P) if t < TS else (io["x_prompt"], (t - TS) * P)
                with sp.If(l < 1):
                    sp.dma_start(xs[:, t % 2, :], src_in[0][src_in[1]:src_in[1] + P, :]).then_inc(s[f"p_x{t % 2}"], 16)
                with sp.Else():
                    sp.dma_start(xs[:, t % 2, :], src_new[0][src_new[1]:src_new[1] + P, :]).then_inc(s[f"p_x{t % 2}"], 16)

            def load_w(first, end):
                for n in range(first, min(end, NW)):
                    (_, c0, cols), k = BLOCKS[n // KD], n % KD
                    if n >= STAGES:
                        sp.wait_ge(s["p_wlo"], n - STAGES + 1)
                    sp.dma_start(stage[:, n % STAGES, 0:cols],
                                 w_in[bass.ds(l, 1), k * P:(k + 1) * P, c0:c0 + cols].rearrange("a p n -> (a p) n")
                                 ).then_inc(s[f"p_w{n % STAGES}"], 16)

            def store_z(b, t):
                i = b * T + t
                sp.wait_ge(s["p_zo"], i + 1)
                c0 = BLOCKS[b][1]
                sp.dma_start(Zs[tile_rows(t), c0:c0 + NB], zo[:, i % 3, :]).then_inc(s[f"p_out{i % 3}"], 16)
                if t >= TS:
                    rows = slice((t - TS) * P, (t - TS + 1) * P)
                    outs = {0: (), NB: (("new_a_k", 0, A_KV), ("new_a_v", A_KV * HEAD_DIM, A_KV)),
                            2 * NB: (("new_b_k", 0, B_HEADS), ("new_b_v", B_HEADS * B_V, B_HEADS))}[c0]
                    for name, c, heads in outs:
                        dst = io[name][bass.ds(l, 1), :, rows, :].rearrange("a h t d -> t (a h) d")
                        sp.dma_start(dst, zo[:, i % 3, c:c + heads * HEAD_DIM].rearrange("t (h d) -> t h d", h=heads)
                                     ).then_inc(s[f"p_new{i % 3}"], 16)

            def store_u(b, t):
                j = (b - len(BLOCKS) + 2) * T + t
                i = Z_BLOCKS * T + j
                sp.wait_ge(s["p_ev"], U_USE0 + j + 1)
                c0 = BLOCKS[b][1] - U_COL0
                sp.dma_start(Us[tile_rows(t), c0:c0 + NB], zo[:, i % 3, :]).then_inc(s[f"p_out{i % 3}"], 16)

            ahead = 4 + STAGES
            load_x(0)
            load_x(1)
            load_w(0, KD)
            load_x(2)
            load_x(3)
            for b, (kind, _, _) in enumerate(BLOCKS):
                load_w((b + 1) * KD, (b + 1) * KD + ahead)
                for t in range(T):
                    if b == 0 and t + 4 < T:
                        load_x(t + 4)
                    if t == T - 2:
                        load_w((b + 1) * KD + ahead, (b + 2) * KD)
                    if kind == "z":
                        store_z(b, t)
                    elif kind == "u":
                        store_u(b, t)
            n = Z_BLOCKS * T + 2 * T
            for i in range(3):
                sp.wait_ge(s[f"p_out{i}"], 16 * len(range(i, n, 3)))
                sp.wait_ge(s[f"p_new{i}"], 16 * new_stores(i, Z_BLOCKS * T))

        @block.tensor
        def _(pe):
            def turn(t):
                pe.wait_ge(s["p_xn"], t + 1)
                if t >= 2:
                    pe.wait_ge(s["p_h32"], t - 1)
                for k in range(KD):
                    mm = pe.transpose(tp[t % 2][:, k, :], xn[:, k * P:(k + 1) * P], per["ident"][:, :])
                mm.then_inc(s["p_turned"], 1)

            def product(i, acc, lhs, rhs, b, w_first):
                if i >= 4:
                    pe.wait_ge(s["p_ev"], i - 3)
                last = i == last_use[b]
                for k in range(KD):
                    n = b * KD + k
                    slot = n % RING
                    if i == first_use[b]:
                        pe.wait_ge(s["p_wlo"], n + 1)
                    parts = ((h_hi, w_hi), (h_hi, w_lo), (h_lo, w_hi))
                    for q, (hh, ww) in enumerate(parts):
                        w_ap, h_ap = ww[:, slot, rhs if not w_first else lhs], hh[:, k, lhs if not w_first else rhs]
                        mm = pe.matmul(acc, w_ap if w_first else h_ap, h_ap if w_first else w_ap,
                                       start=(k == 0 and q == 0), stop=(k == KD - 1 and q == 2))
                        if last and q == 2 and k < KD - 1:
                            mm.then_inc(s["p_wfree"], 1)
                if last:
                    mm.then_inc(s["p_acc"], 1)
                else:
                    mm.then_inc(s["p_acc"], 1)

            turn(0)
            turn(1)
            for i, (b, what, j) in enumerate(uses):
                acc = zp[i % 4]
                if b == 0:
                    pe.wait_ge(s["p_h"], j + 1)
                if what in ("z", "u"):
                    product(i, acc[:, :], tile_rows(j), slice(0, NB), b, False)
                elif what == "cv":
                    product(i, acc[:, 0:2 * P], tile_rows(j), slice(2 * P, 4 * P), b, False)
                else:
                    m = 0 if what == "lr" else int(what[2])
                    tb = tok_block(j)
                    product(i, acc[:, 0:tb.stop - tb.start], slice(m * P, (m + 1) * P), tb, b, True)
                if b == 0 and j + 2 < T:
                    turn(j + 2)

        @block.scalar
        def _(act):
            def square(t):
                act.wait_ge(s[f"p_x{t % 2}"], 16 * (t // 2 + 1))
                if t:
                    act.wait_ge(s["p_turned"], t)
                act.activation(xn[:, :], xs[:, t % 2, :], ACT.Square, accum_out=ss[:, 0, t:t + 1]).then_inc(s["p_sq"], 1)
                act.wait_ge(s["p_sq"], t + 1)
                act.activation(ss[:, 1, t:t + 1], ss[:, 0, t:t + 1], ACT.Sqrt, bias=per["eps"][:, :],
                               scale=1.0 / D_MODEL).then_inc(s["p_std"], 1)

            def hi_h(t):
                act.wait_ge(s["p_h32"], t + 1)
                act.copy(h_hi[:, :, tile_rows(t)], h32[:, :, :]).then_inc(s["p_hhi"], 1)

            def hi_w(n):
                cols = BLOCKS[n // KD][2]
                act.wait_ge(s[f"p_w{n % STAGES}"], 16 * (n // STAGES + 1))
                if n >= RING:
                    free_ring(act, n)
                act.copy(w_hi[:, n % RING, 0:cols], stage[:, n % STAGES, 0:cols]).then_inc(s["p_whi"], 1)

            def evacuate(i):
                b, what, j = uses[i]
                act.wait_ge(s["p_acc"], i + 1)
                acc = zp[i % 4]
                if what == "z":
                    if i >= 3:
                        act.wait_ge(s["p_zo"], i - 2)
                    act.copy(zt[:, i % 3, :], acc[:, :]).then_inc(s["p_ev"], 1)
                elif what == "u":
                    q = Z_BLOCKS * T + i - U_USE0
                    act.wait_ge(s[f"p_out{q % 3}"], 16 * len(range(q % 3, q, 3)))
                    act.activation(zo[:, q % 3, :], acc[:, :], ACT.Silu).then_inc(s["p_ev"], 1)
                elif what == "cv":
                    act.copy(per["cv"][:, j, :], acc[:, 0:2 * P]).then_inc(s["p_ev"], 1)
                else:
                    tb = tok_block(j)
                    rows = 2 * RANK if what == "lr" else P
                    dst = per["lrT"] if what == "lr" else per["cqT"] if what == "cT0" else per["ckT"]
                    act.copy(dst[0:rows, tb], acc[0:rows, 0:tb.stop - tb.start]).then_inc(s["p_ev"], 1)

            def head_std(i):
                if BLOCKS[i // T][1] > NB:
                    return
                heads = A_HEADS if BLOCKS[i // T][1] == 0 else A_KV
                n = i - T + 1
                act.wait_ge(s["p_hss"], n)
                act.activation(hst[:, i % 2, 1, 0:heads], hst[:, i % 2, 0, 0:heads], ACT.Sqrt, bias=per["eps"][:, :],
                               scale=1.0 / HEAD_DIM).then_inc(s["p_hstd"], 1)

            square(0)
            for n in range(4):
                hi_w(n)
            hi_h(0)
            square(1)
            for n in range(4, 8):
                hi_w(n)
            hi_h(1)
            square(2)
            for i, (b, what, j) in enumerate(uses):
                if i == last_use[b] and b + 1 < len(BLOCKS):
                    for k in range(4, KD):
                        hi_w((b + 1) * KD + k)
                evacuate(i)
                if 0 < i <= Z_BLOCKS * T:
                    head_std(i - 1)
                if b == 0 and j + 2 < T:
                    hi_h(j + 2)
                    if j + 3 < T:
                        square(j + 3)
                if i == first_use[b] and b + 1 < len(BLOCKS):
                    for k in range(4):
                        hi_w((b + 1) * KD + k)

        @block.vector
        def _(dve):
            do = Chain(dve, s["p_dve"])

            def norm_x(t):
                dve.wait_ge(s["p_std"], t + 1)
                do(dve.reciprocal(ss[:, 2, t:t + 1], ss[:, 1, t:t + 1]))
                dve.tensor_scalar(xn[:, :], xs[:, t % 2, :], ss[:, 2, t:t + 1], None, ALU.mult).then_inc(s["p_xn"], 1)

            def affine(t):
                g = group(t)
                dve.wait_ge(s["p_turned"], t + 1)
                if t:
                    dve.wait_ge(s["p_h"], t)
                for k in range(KD):
                    ins = dve.tensor_scalar(h32[:, k, :], tp[t % 2][:, k, :], per["h_scale"][:, g, k:k + 1],
                                            per["h_shift"][:, g, k:k + 1], ALU.mult, ALU.add)
                ins.then_inc(s["p_h32"], 1)

            def lo_h(t):
                dve.wait_ge(s["p_hhi"], t + 1)
                dve.tensor_tensor(h_lo[:, :, tile_rows(t)], h32[:, :, :], h_hi[:, :, tile_rows(t)].bitcast(F32),
                                  ALU.subtract).then_inc(s["p_h"], 1)

            def lo_w(n):
                cols = BLOCKS[n // KD][2]
                dve.wait_ge(s["p_whi"], n + 1)
                dve.tensor_tensor(w_lo[:, n % RING, 0:cols], stage[:, n % STAGES, 0:cols],
                                  w_hi[:, n % RING, 0:cols].bitcast(F32), ALU.subtract).then_inc(s["p_wlo"], 1)

            def heads_view(ap, heads):
                return ap.rearrange("p (h d) -> p h d", h=heads)

            def rope(dst, src, t, heads, half, cos, sin, tmp):
                d = heads_view(dst, heads)
                x = heads_view(src, heads)
                w = dst.shape[1] // heads
                c = cos[:, t, :].unsqueeze(1).broadcast_to([P, heads, w])
                do(dve.tensor_tensor(d, x, c, ALU.mult))
                x4 = src.rearrange("p (h g e f) -> p h g e f", h=heads, e=2, f=half)
                t4 = tmp.rearrange("p (h g e f) -> p h g e f", h=heads, e=2, f=half)
                s3 = sin[:, t, :].rearrange("p (g e f) -> p g e f", e=2, f=half)
                g = w // (2 * half)
                for e in range(2):
                    sn = s3[:, :, e, :].unsqueeze(1).broadcast_to([P, heads, g, half])
                    do(dve.tensor_tensor(t4[:, :, :, e, :], x4[:, :, :, 1 - e, :], sn, ALU.mult))
                return dve.tensor_tensor(dst, dst, tmp, ALU.add)

            def head_sums(i):
                c0 = BLOCKS[i // T][1]
                if c0 > NB:
                    return
                heads = A_HEADS if c0 == 0 else A_KV
                dve.wait_ge(s["p_ev"], i + 1)
                w = heads * HEAD_DIM
                do(dve.tensor_tensor(tm[:, 0, 0:w], zt[:, i % 3, 0:w], zt[:, i % 3, 0:w], ALU.mult))
                dve.tensor_reduce(hst[:, i % 2, 0, 0:heads], heads_view(tm[:, 0, 0:w], heads), AX_X,
                                  ALU.add).then_inc(s["p_hss"], 1)

            def finish_tile(i):
                b, t = divmod(i, T)
                c0 = BLOCKS[b][1]
                z, o = zt[:, i % 3, :], zo[:, i % 3, :]
                dve.wait_ge(s["p_ev"], i + 1)
                if i >= 3:
                    dve.wait_ge(s[f"p_out{i % 3}"], 16 * (i // 3))
                    if new_stores(i % 3, i):
                        dve.wait_ge(s[f"p_new{i % 3}"], 16 * new_stores(i % 3, i))
                if c0 <= NB:
                    heads = A_HEADS if c0 == 0 else A_KV
                    w = heads * HEAD_DIM
                    dve.wait_ge(s["p_hstd"], i - T + 1)
                    do(dve.reciprocal(hst[:, i % 2, 2, 0:heads], hst[:, i % 2, 1, 0:heads]))
                    zv = heads_view(z[:, 0:w], heads)
                    do(dve.tensor_tensor(heads_view(tm[:, 1, 0:w], heads), zv,
                                         hst[:, i % 2, 2, 0:heads].unsqueeze(2).broadcast_to([P, heads, HEAD_DIM]), ALU.mult))
                    gain = per["gains"][:, 0 if c0 == 0 else 1, :].unsqueeze(1).broadcast_to([P, heads, HEAD_DIM])
                    if t < TS:
                        do(dve.tensor_tensor(heads_view(tm[:, 2, 0:w], heads), heads_view(tm[:, 1, 0:w], heads), gain, ALU.mult))
                        last = rope(o[:, 0:w], tm[:, 2, 0:w], t, heads, 16, per["cosA"], per["sinA"], tm[:, 1, 0:w])
                    else:
                        last = dve.tensor_tensor(heads_view(o[:, 0:w], heads), heads_view(tm[:, 1, 0:w], heads), gain, ALU.mult)
                    if c0 == NB:
                        do(last)
                        do(dve.tensor_copy(o[:, P:2 * P], z[:, P:2 * P]))
                        if t < TS:
                            last = rope(o[:, 2 * P:NB], z[:, 2 * P:NB], t, 2 * B_HEADS, 8, per["cosB"], per["sinB"], tm[:, 1, 0:2 * P])
                        else:
                            last = dve.tensor_copy(o[:, 2 * P:NB], z[:, 2 * P:NB])
                else:
                    do(dve.tensor_copy(o[:, 2 * P:NB], z[:, 2 * P:NB]))
                    if t < TS:
                        last = rope(o[:, 0:2 * P], z[:, 0:2 * P], t, 2 * B_HEADS, 8, per["cosB"], per["sinB"], tm[:, 1, 0:2 * P])
                    else:
                        last = dve.tensor_copy(o[:, 0:2 * P], z[:, 0:2 * P])
                last.then_inc(s["p_zo"], 1)

            norm_x(0)
            for n in range(4):
                lo_w(n)
            affine(0)
            lo_h(0)
            norm_x(1)
            for n in range(4, 8):
                lo_w(n)
            affine(1)
            lo_h(1)
            norm_x(2)
            for i, (b, what, j) in enumerate(uses):
                if i == last_use[b] and b + 1 < len(BLOCKS):
                    for k in range(4, KD):
                        lo_w((b + 1) * KD + k)
                if b == 0 and j + 2 < T:
                    affine(j + 2)
                    lo_h(j + 2)
                    if j + 3 < T:
                        norm_x(j + 3)
                if i < Z_BLOCKS * T:
                    head_sums(i)
                if 0 < i <= Z_BLOCKS * T:
                    finish_tile(i - 1)
                if i == first_use[b] and b + 1 < len(BLOCKS):
                    for k in range(4):
                        lo_w((b + 1) * KD + k)


CHUNK = 64
NC_S, NC_P = DEC_SEQ // CHUNK, SEQ // CHUNK
S_SLOTS = NC_S + 1 + NC_P + 1


def gla_block(nc, l, io, per, mid, att, s):
    CD, CV = C_HEADS * C_DK, C_HEADS * C_DV
    with ExitStack() as ctx:
        def sb(name, shape, dt=F32):
            return ctx.enter_context(nc.sbuf_tensor(name, shape, dt))

        def ps(name):
            return ctx.enter_context(nc.psum_tensor(name, [P, NB], F32))

        oa2 = mid["oa"][:, :, :].rearrange("p t c -> p (t c)").rearrange("p (x t c) -> p x t c", x=2, t=T)
        ob2 = mid["ob"][:, :, :, :].rearrange("p a t c -> p (a t c)").rearrange("p (x t c) -> p x t c", x=2, t=T)
        gate, soft = oa2[:, 0, :, :], oa2[:, 1, :, :]
        qt, oi = ob2[:, 0, :, :].rearrange("p t (d i) -> p t d i", d=2), ob2[:, 1, :, :]
        st = sb("states", [P, 2, S_SLOTS, CV])
        el = sb("exp_last", [P, T, 2, 2])
        lc = sb("last_cum", [P, 2, 2, 2])
        ex = sb("exps", [P, 2, 3, 2, P])
        kt = sb("k_scaled", [P, 2, 2, 2, P])
        qbd = sb("q_blockdiag", [P, 2, 2, C_HEADS, P])
        am = sb("a_masked", [P, 2, 2, C_HEADS, P])
        k2t = sb("k_by_token", [P, 2, 2, P])
        cum_ps = [ps("cum0"), ps("cum1")]
        at_ps = [ps("at0"), ps("at1")]
        tr_ps, o_ps = ps("gla_tr"), ps("gla_o")
        ds_ps = [ps("ds0"), ps("ds1")]
        block = ctx.enter_context(nc.Block())
        oc = mid["oc"]

        def slot0(t):
            return 0 if t < TS else NC_S + 1

        def step_of(d, t, c):
            n = 2 * (t if t < TS else t - TS) + c
            chunks = NC_S if t < TS else NC_P
            return n if d == 0 else chunks - 1 - n

        backward = list(range(TS - 1, -1, -1)) + list(range(T - 1, TS - 1, -1))

        @block.sync
        def _(sp):
            for u in ("A", "B"):
                load_qk(sp, s, l, io, att, u, 0)
            sp.wait_ge(s["g_zero"], 2)
            for d, name in enumerate(("state_c_fwd", "state_c_bwd")):
                for h in range(C_HEADS):
                    sp.dma_start(st[h * C_DK:(h + 1) * C_DK, d, 0, h * C_DV:(h + 1) * C_DV],
                                 io[name][bass.ds(l, 1), h, :, :].rearrange("a x y -> (a x) y")).then_inc(s["g_st0"], 16)
            sp.wait_ge(s["a_ones"], 6)
            for u in ("A", "B"):
                load_v(sp, s, l, io, att, u, 0)
            sp.wait_ge(s["g_chain"], 1)
            for d, name in enumerate(("new_state_c_fwd", "new_state_c_bwd")):
                for h in range(C_HEADS):
                    sp.dma_start(io[name][bass.ds(l, 1), h, :, :].rearrange("a x y -> (a x) y"),
                                 st[h * C_DK:(h + 1) * C_DK, d, S_SLOTS - 1, h * C_DV:(h + 1) * C_DV]).then_inc(s["g_new"], 16)
            sp.wait_ge(s["g_new"], 16 * 2 * C_HEADS)

        @block.tensor
        def _(pe):
            for i in range(T // 2):
                if i >= 2:
                    pe.wait_ge(s["g_min"], i - 1)
                for t in (2 * i, 2 * i + 1):
                    mm = pe.matmul(cum_ps[i % 2][:, (t % 2) * 2 * CD:(t % 2 + 1) * 2 * CD], per["lrT"][:, tile_rows(t)],
                                   per["gate_w"][:, :], start=True, stop=True)
                mm.then_inc(s["g_pre"], 1)
            pe.wait_ge(s["g_gate"], 1)

            def running_sums(t):
                if t >= 2:
                    pe.wait_ge(s["g_exp"], t - 1)
                for d in range(2):
                    mm = pe.matmul(cum_ps[t % 2][:, d * P:(d + 1) * P], gate[:, t, d * CD:(d + 1) * CD], per["tri"][:, d, :],
                                   start=True, stop=True)
                mm.then_inc(s["g_cum"], 1)

            running_sums(0)
            running_sums(1)
            for t in range(T):
                b = t % 2
                pe.wait_ge(s["g_mul"], t + 1)
                if t:
                    pe.wait_ge(s["g_k2t"], t)
                for d in range(2):
                    mm = pe.transpose(tr_ps[:, d * P:(d + 1) * P], kt[:, b, 1, d, :], per["ident"][:, :])
                mm.then_inc(s["g_tr"], 1)
                for d in range(2):
                    if t:
                        pe.wait_ge(s["g_am"], 2 * t + d - 1)
                    if d == 0:
                        pe.wait_ge(s["g_qbd"], t + 1)
                    pe.matmul(at_ps[d][:, :], kt[:, b, 0, d, :], qbd[:, b, d, :, :].rearrange("p h i -> p (h i)"),
                              start=True, stop=True).then_inc(s["g_at"], 1)
                if t + 2 < T:
                    running_sums(t + 2)
                pe.wait_ge(s["g_k2t"], t + 1)
                if t:
                    pe.wait_ge(s["g_dsm"], t)
                for c in range(2):
                    rows = slice(c * CHUNK, (c + 1) * CHUNK)
                    for d in range(2):
                        mm = pe.matmul(ds_ps[c][:, d * CV:(d + 1) * CV], k2t[rows, b, d, :], per["cv"][rows, t, :],
                                       start=True, stop=True)
                mm.then_inc(s["g_ds"], 1)
                pe.wait_ge(s["g_am"], 2 * t + 2)
                if t:
                    pe.wait_ge(s["g_oi"], t)
                for h in range(C_HEADS):
                    cols = slice(h * C_DV, (h + 1) * C_DV)
                    for d in range(2):
                        mm = pe.matmul(o_ps[:, cols], am[:, b, d, h, :], per["cv"][:, t, cols], start=(d == 0), stop=(d == 1))
                mm.then_inc(s["g_o"], 1)
            for n, t in enumerate(backward):
                if n == 0:
                    pe.wait_ge(s["g_oi"], T)
                pe.wait_ge(s["g_bwd"], n + 1)
                if n >= 2:
                    pe.wait_ge(s["g_oc"], n - 1)
                for c in range(2):
                    for d in range(2):
                        mm = pe.matmul(cum_ps[n % 2][c * CHUNK:(c + 1) * CHUNK, 0:CV], qt[:, t, d, c * CHUNK:(c + 1) * CHUNK],
                                       st[:, d, slot0(t) + step_of(d, t, c), :], start=(d == 0), stop=(d == 1))
                mm.then_inc(s["g_inter"], 1)

        @block.gpsimd
        def _(pool):
            def blockdiag(t):
                b = t % 2
                pool.wait_ge(s["g_qt"], t + 1)
                if t >= 2:
                    pool.wait_ge(s["g_at"], 2 * t - 2)
                for d in range(2):
                    ins = pool.tensor_tensor(qbd[:, b, d, :, :], qt[:, t, d, :].unsqueeze(1).broadcast_to([P, C_HEADS, P]),
                                             per["bdmask"][:, :].unsqueeze(2).broadcast_to([P, C_HEADS, P]), ALU.mult)
                ins.then_inc(s["g_qbd"], 1)

            pool.wait_ge(s["a_ones"], 6)
            split(pool, s, per, att, "A", 0, 0)
            for t in range(T):
                blockdiag(t)
            split(pool, s, per, att, "B", 0, SPLIT_CHAIN["A"])

        @block.scalar
        def _(act):
            do = Chain(act, s["g_act"])
            for i in range(T // 2):
                act.wait_ge(s["g_pre"], i + 1)
                act.activation(soft[:, 2 * i:2 * i + 2, :], cum_ps[i % 2][:, :].rearrange("p (t c) -> p t c", t=2),
                               ACT.Abs).then_inc(s["g_abs"], 1)
            act.wait_ge(s["g_abs"], T // 2)
            do(act.activation(soft[:, :, :], soft[:, :, :], ACT.Exp, scale=-1.0))
            act.activation(soft[:, :, :], soft[:, :, :], ACT.Ln, bias=per["one"][:, :]).then_inc(s["g_ln"], 1)

            def exps(t):
                b = t % 2
                act.wait_ge(s["g_cum"], t + 1)
                if t >= 2:
                    act.wait_ge(s["g_mul"], t - 1)
                cum = cum_ps[b][:, 0:2 * P].rearrange("p (d i) -> p d i", d=2)
                act.activation(ex[:, b, 0, :, :], cum, ACT.Exp, scale=1.0 / TAU)
                act.activation(ex[:, b, 1, :, :], cum, ACT.Exp, scale=-1.0 / TAU)
                do(act.mul(lc[:, b, 0, :], cum[:, 0, CHUNK - 1::CHUNK], 1.0 / TAU))
                do(act.mul(lc[:, b, 1, :], cum[:, 1, 0::CHUNK], 1.0 / TAU))
                act.activation(el[:, t, :, :], lc[:, b, :, :], ACT.Exp)
                for d in range(2):
                    for c in range(2):
                        cols = slice(c * CHUNK, (c + 1) * CHUNK)
                        ins = act.activation(ex[:, b, 2, d, cols], cum[:, d, cols], ACT.Exp, scale=-1.0 / TAU,
                                             bias=lc[:, b, d, c:c + 1])
                ins.then_inc(s["g_exp"], 1)

            exps(0)
            for t in range(T):
                b = t % 2
                if t + 1 < T:
                    exps(t + 1)
                act.wait_ge(s["g_tr"], t + 1)
                if t >= 2:
                    act.wait_ge(s["g_ds"], t - 1)
                act.copy(k2t[:, b, :, :], tr_ps[:, 0:2 * P].rearrange("p (d f) -> p d f", d=2)).then_inc(s["g_k2t"], 1)
                act.wait_ge(s["g_o"], t + 1)
                act.copy(oi[:, t, :], o_ps[:, 0:CV]).then_inc(s["g_oi"], 1)

        @block.vector
        def _(dve):
            do = Chain(dve, s["g_dve"])
            kst, qst, qst2, v = att["kst"], att["qst"], att["qst2"], att["v"]
            ones0, ones1 = 3 * B_QK, 3 * B_QK + 2
            for ap, value in ((kst["B"][:, :, ones0:ones1].bitcast(F32), 1.0), (kst["B"][:, :, ones1:].bitcast(F32), 0.0),
                              (qst["B"][:, :, ones0:].bitcast(F32), 0.0), (qst2[:, :, HEAD_DIM:].bitcast(F32), 0.0),
                              (v["A"][:, :, HEAD_DIM:], 1.0), (v["B"][:, :, HEAD_DIM:], 1.0)):
                dve.memset(ap, value).then_inc(s["a_ones"], 1)
            dve.memset(st[:, :, 0, :], 0.0).then_inc(s["g_zero"], 1)
            dve.memset(st[:, :, NC_S + 1, :], 0.0).then_inc(s["g_zero"], 1)
            for i in range(T // 2):
                dve.wait_ge(s["g_abs"], i + 1)
                dve.tensor_scalar(gate[:, 2 * i:2 * i + 2, :], cum_ps[i % 2][:, :].rearrange("p (t c) -> p t c", t=2),
                                  0.0, None, ALU.min).then_inc(s["g_min"], 1)
            dve.wait_ge(s["g_min"], T // 2)
            dve.wait_ge(s["g_ln"], 1)
            dve.tensor_tensor(gate[:, :, :], gate[:, :, :], soft[:, :, :], ALU.subtract).then_inc(s["g_gate"], 1)

            def both(ap):
                return ap.unsqueeze(1).broadcast_to([P, 2, P])

            def scale_qk(t):
                b = t % 2
                dve.wait_ge(s["g_exp"], t + 1)
                if t >= 2:
                    dve.wait_ge(s["g_at"], 2 * t - 2)
                q, k = both(per["cqT"][:, tile_rows(t)]), both(per["ckT"][:, tile_rows(t)])
                dve.scalar_tensor_tensor(out=qt[:, t, :, :], in0=q, scalar=float(C_DK) ** -0.5, in1=ex[:, b, 0, :, :],
                                         op0=ALU.mult, op1=ALU.mult).then_inc(s["g_qt"], 1)
                dve.tensor_tensor(kt[:, b, 0, :, :], k, ex[:, b, 1, :, :], ALU.mult)
                dve.tensor_tensor(kt[:, b, 1, :, :], k, ex[:, b, 2, :, :], ALU.mult).then_inc(s["g_mul"], 1)

            def advance(d, t, c):
                n = slot0(t) + step_of(d, t, c)
                do(dve.scalar_tensor_tensor(out=st[:, d, n + 1, :], in0=st[:, d, n, :], scalar=el[:, t, d, c:c + 1],
                                            in1=st[:, d, n + 1, :], op0=ALU.mult, op1=ALU.add))

            scale_qk(0)
            for t in range(T):
                b = t % 2
                if t + 1 < T:
                    scale_qk(t + 1)
                for d in range(2):
                    dve.wait_ge(s["g_at"], 2 * t + d + 1)
                    if t >= 2:
                        dve.wait_ge(s["g_o"], t - 1)
                    dve.tensor_tensor(am[:, b, d, :, :], at_ps[d][:, :].rearrange("p (h i) -> p h i", h=C_HEADS),
                                      per["tri"][:, d, :].unsqueeze(1).broadcast_to([P, C_HEADS, P]),
                                      ALU.mult).then_inc(s["g_am"], 1)
                dve.wait_ge(s["g_ds"], t + 1)
                for c in range(2):
                    for d in range(2):
                        dst = st[:, d, slot0(t) + step_of(d, t, c) + 1, :].rearrange("p (h e) -> p h e", h=C_HEADS)
                        ins = dve.tensor_tensor(dst, ds_ps[c][:, d * CV:(d + 1) * CV].rearrange("p (h e) -> p h e", h=C_HEADS),
                                                per["bdmask"][:, :].unsqueeze(2).broadcast_to([P, C_HEADS, C_DV]), ALU.mult)
                ins.then_inc(s["g_dsm"], 1)
                dve.wait_ge(s["g_dsm"], t + 1)
                if t == 0:
                    dve.wait_ge(s["g_st0"], 16 * 2 * C_HEADS)
                for c in range(2):
                    advance(0, t, c)

            def join(n):
                t = backward[n]
                dve.wait_ge(s["g_inter"], n + 1)
                dve.tensor_tensor(oc[:, t, :], cum_ps[n % 2][:, 0:CV], oi[:, t, :], ALU.add).then_inc(s["g_oc"], 1)

            dve.wait_ge(s["g_oi"], T)
            for n, t in enumerate(backward):
                advance(1, t, 1)
                advance(1, t, 0)
                dve.sem_inc(s["g_bwd"], 1)
                if n >= 2:
                    join(n - 2)
            dve.sem_inc(s["g_chain"], 1)
            join(T - 2)
            join(T - 1)


KT = (PAST + DEC_SEQ + SEQ) // P
KT_S = (PAST + DEC_SEQ) // P
KEYS = KT * P
ATT_STEPS = KT_S + 1
PREP = 30
PREP_AT = (3, 3, 4, 4, 4, 3, 3, 3, 3, 0, 0)
PREP_Q, PREP_MAX, PREP_LAST = 3, 6, 27
HALF = 5


QK_W = {"A": HEAD_DIM, "B": B_QK}
SPLIT_CHAIN = {"A": 4, "B": 5}


def attention_front(nc, ctx):
    def sb(name, shape, dt=F32):
        return ctx.enter_context(nc.sbuf_tensor(name, shape, dt))

    return {
        "kraw": {u: sb(f"k_raw{u}", [P, KT, QK_W[u]]) for u in "AB"},
        "qraw": {u: sb(f"q_raw{u}", [P, T, QK_W[u]]) for u in "AB"},
        "v": {u: sb(f"v{u}", [P, KT, HEAD_DIM + 1]) for u in "AB"},
        "kst": {u: sb(f"k_stack{u}", [P, KT, P], F32R) for u in "AB"},
        "qst": {u: sb(f"q_stack{u}", [P, T, P], F32R) for u in "AB"},
        "qst2": sb("q_stackA2", [P, T, P], F32R)}


def load_part(sp, s, l, io, u, dst, h, what, sem):
    w = HEAD_DIM if what == "v" else QK_W[u]
    if u == "A":
        kv = h // (A_HEADS // A_KV)
        c = {"q": h * HEAD_DIM, "k": A_HEADS * HEAD_DIM + kv * HEAD_DIM,
             "v": (A_HEADS + A_KV) * HEAD_DIM + kv * HEAD_DIM}[what]
    else:
        base, nb = (A_HEADS + 2 * A_KV) * HEAD_DIM, B_HEADS * 2 * B_QK
        c = {"q": base + h * B_QK, "k": base + nb + h * B_QK, "v": base + 2 * nb + (h // 2) * B_V}[what]
    src = io["Zs"][:, bass.ds(c, w)].rearrange("(t p) d -> p t d", p=P)
    first = 0 if what == "q" else PAST // P
    sp.dma_start(dst[:, first:, 0:w], src).then_inc(s[sem], 16)
    if what != "q":
        cache = io[f"cache_{u.lower()}_{what}"]
        head = h // (A_HEADS // A_KV) if u == "A" else h // 2
        c0 = (h % 2) * B_QK if (u == "B" and what == "k") else 0
        src = cache[bass.ds(l, 1), bass.ds(head, 1), :, bass.ds(c0, w)].rearrange("a b (t p) d -> p (a b t) d", p=P)
        sp.dma_start(dst[:, 0:first, 0:w], src).then_inc(s[sem], 16)


def load_qk(sp, s, l, io, att, u, h):
    load_part(sp, s, l, io, u, att["kraw"][u], h, "k", f"a_raw{u}")
    load_part(sp, s, l, io, u, att["qraw"][u], h, "q", f"a_raw{u}")


def load_v(sp, s, l, io, att, u, h):
    load_part(sp, s, l, io, u, att["v"][u], h, "v", f"a_v{u}")


def split(pool, s, per, att, u, h, chain0):
    n = [0]

    def do(ins):
        n[0] += 1
        ins.then_inc(s["a_pool"], 1)
        pool.wait_ge(s["a_pool"], chain0 + n[0])

    def copy(dst, src):
        one = per["one"][:, :].unsqueeze(2).broadcast_to(list(src.shape))
        return pool.tensor_tensor(dst, src, one, ALU.mult)

    w = QK_W[u]
    k, q, ks, qs = att["kraw"][u][:, :, :], att["qraw"][u][:, :, :], att["kst"][u], att["qst"][u]
    pool.wait_ge(s[f"a_raw{u}"], 48 * (h + 1))
    do(copy(ks[:, :, 0:w], k))
    do(copy(qs[:, :, 0:w], q))
    if u == "A":
        do(pool.tensor_tensor(ks[:, :, w:2 * w], k, ks[:, :, 0:w].bitcast(F32), ALU.subtract))
        do(copy(qs[:, :, w:2 * w], qs[:, :, 0:w].bitcast(F32)))
        ins = pool.tensor_tensor(att["qst2"][:, :, 0:w], q, qs[:, :, 0:w].bitcast(F32), ALU.subtract)
    else:
        do(pool.tensor_tensor(ks[:, :, 2 * w:3 * w], k, ks[:, :, 0:w].bitcast(F32), ALU.subtract))
        do(copy(ks[:, :, w:2 * w], ks[:, :, 0:w].bitcast(F32)))
        do(copy(qs[:, :, 2 * w:3 * w], qs[:, :, 0:w].bitcast(F32)))
        ins = pool.tensor_tensor(qs[:, :, w:2 * w], q, qs[:, :, 0:w].bitcast(F32), ALU.subtract)
    ins.then_inc(s[f"a_split{u}"], 1)


def attention_block(nc, l, io, per, mid, att, s):
    A, B = "A", "B"
    W = {A: HEAD_DIM, B: B_QK}
    KR = {A: P, B: 3 * B_QK + 2}
    SCALE = {A: float(HEAD_DIM) ** -0.5, B: float(B_QK) ** -0.5}
    with ExitStack() as ctx:
        def sb(name, shape, dt=F32):
            return ctx.enter_context(nc.sbuf_tensor(name, shape, dt))

        v, kst, qst, qst2 = att["v"], att["kst"], att["qst"], att["qst2"]
        kT = {u: sb(f"kT{u}", [P, KEYS], F32R) for u in (A, B)}
        kT2 = sb("kTA2", [P, KEYS], F32R)
        qT = {u: sb(f"qT{u}", [P, TOK], F32R) for u in (A, B)}
        qT2 = {u: sb(f"qT2{u}", [P, TOK], F32R) for u in (A, B)}
        pr = sb("probs", [P, 2, DEC_SEQ])
        nmx = sb("neg_max_parts", [P, T, 3])
        nm = sb("neg_max", [P, T])
        rs = sb("recip_sums", [P, 2, HALF])
        csq = sb("c_squares", [P, T, C_HEADS * C_DV])
        stats = sb("c_stats", [P, 3, T, C_HEADS])
        sc = [ctx.enter_context(nc.psum_tensor(f"scores{i}", [P, 2, NB], F32)) for i in range(2)]
        ob = ctx.enter_context(nc.psum_tensor("att_out", [P, 2, NB], F32))
        wk = [ctx.enter_context(nc.psum_tensor(f"work{i}", [P, NB], F32)) for i in range(2)]
        block = ctx.enter_context(nc.Block())
        m_cols = {A: qst2[:, :, HEAD_DIM:HEAD_DIM + 2], B: qst[B][:, :, 3 * B_QK:KR[B]]}
        TURNS = A_HEADS

        def step0(u, h):
            return h * 2 * ATT_STEPS + (0 if u == A else ATT_STEPS)

        def unit(u, h):
            return 2 * h + (0 if u == A else 1)

        @block.sync
        def _(sp):
            with sp.Fori(0, TURNS - 1) as h:
                for u in (A, B):
                    sp.wait_ge(s[f"a_split{u}"], h + 1)
                    load_qk(sp, s, l, io, att, u, h + 1)
                    sp.wait_ge(s["a_pv"], step0(u, h) + ATT_STEPS)
                    load_v(sp, s, l, io, att, u, h + 1)

        @block.gpsimd
        def _(pool):
            nA, nB = SPLIT_CHAIN[A], SPLIT_CHAIN[B]
            with pool.Fori(0, TURNS - 1) as h:
                pool.wait_ge(s["a_work"], PREP * (unit(A, h) + 1))
                split(pool, s, per, att, A, h + 1, (h + 1) * (nA + nB))
                pool.wait_ge(s["a_work"], PREP * (unit(B, h) + 1))
                split(pool, s, per, att, B, h + 1, (h + 1) * (nA + nB) + nA)

        @block.tensor
        def _(pe):
            def prep(u, h, i):
                p = unit(u, h)
                bank = wk[i % 2]
                first_unit = isinstance(h, int) and h == 0 and u == A
                if i < 2:
                    if not first_unit:
                        pe.wait_ge(s["a_wkdve"], (PREP - PREP_MAX) * p - 1 + i)
                elif i < PREP_MAX:
                    pe.wait_ge(s["a_wkact"], PREP_MAX * p + i - 1)
                elif i < PREP_MAX + 2:
                    pe.wait_ge(s["a_wkact"], PREP_MAX * p + PREP_MAX)
                else:
                    pe.wait_ge(s["a_wkdve"], (PREP - PREP_MAX) * p + i - 1 - PREP_MAX)
                if i == 0:
                    pe.wait_ge(s[f"a_split{u}"], h + 1)
                if i == PREP_LAST:
                    pe.wait_ge(s["a_nm"], p + 1)
                if i < PREP_Q:
                    for j in range(4):
                        mm = pe.matmul(bank[:, j * P:(j + 1) * P], kst[u][:, 4 * i + j, :], per["ident_r"][:, :],
                                       start=True, stop=True)
                elif i < PREP_MAX or i >= PREP_LAST:
                    g = i - (PREP_Q if i < PREP_MAX else PREP_LAST)
                    src = qst2 if u == A and i >= PREP_LAST else qst[u]
                    for t in range(4 * g, min(4 * g + 4, T)):
                        mm = pe.matmul(bank[:, (t - 4 * g) * P:(t - 4 * g + 1) * P], src[:, t, :], per["ident_r"][:, :],
                                       start=True, stop=True)
                else:
                    m, rows = i - PREP_MAX, P if u == A else 3 * B_QK
                    if m < 2 * TS:
                        parts = [(m // 2, (m % 2) * NB, NB)]
                    else:
                        q0 = 2 * (m - 2 * TS)
                        keys0 = 2 * NB if q0 < TS else KT_S * P
                        parts = [(q0, keys0, SEQ), (q0 + 1, keys0, SEQ)]
                    for x, (t, k0, n) in enumerate(parts):
                        mm = pe.matmul(bank[:, x * SEQ:x * SEQ + n], qT[u][0:rows, tile_rows(t)], kT[u][0:rows, k0:k0 + n],
                                       start=True, stop=True)
                mm.then_inc(s["a_work"], 1)

            def scores(u, h, j):
                n = step0(u, h) + j
                if not (isinstance(h, int) and h == 0 and u == A and j < 2):
                    pe.wait_ge(s["a_exp"], n - 1)
                if j == 0:
                    pe.wait_ge(s["a_wkdve"], (PREP - PREP_MAX) * (unit(u, h) + 1))
                slot = sc[(j + (0 if u == A else ATT_STEPS)) % 2]
                for c in range(2):
                    if j < KT_S:
                        keys, q, out = tile_rows(j), slice(c * NB, (c + 1) * NB), slot[:, c, :]
                    else:
                        keys, q, out = tile_rows(KT_S + c), slice(DEC_SEQ, TOK), slot[:, c, 0:SEQ]
                    if u == A:
                        pe.matmul(out, kT[u][:, keys], qT[u][:, q], start=True, stop=False)
                        mm = pe.matmul(out, kT2[:, keys], qT2[u][:, q], start=False, stop=True)
                    else:
                        mm = pe.matmul(out, kT[u][:, keys], qT2[u][:, q], start=True, stop=True)
                mm.then_inc(s["a_scores"], 1)

            def weigh(u, h, j, part):
                n = step0(u, h) + j
                pb = pr[:, (j + (0 if u == A else ATT_STEPS)) % 2, :]
                if part == 0:
                    pe.wait_ge(s["a_exp"], n + 1)
                    if j == 0:
                        pe.wait_ge(s[f"a_v{u}"], 32 * (h + 1))
                        pe.wait_ge(s["a_out"], unit(u, h) + 1)
                if j < KT_S:
                    work = [(t, pb[:, tile_rows(t)], j) for t in range(part * 4, part * 4 + 4)]
                else:
                    t = TS + part
                    work = [(t, pb[:, c * NB + part * P:c * NB + (part + 1) * P], KT_S + c) for c in range(2)]
                for t, probs, key in work:
                    o = ob[:, t // HALF, (t % HALF) * (HEAD_DIM + 1):(t % HALF + 1) * (HEAD_DIM + 1)]
                    mm = pe.matmul(o, probs, v[u][:, key, :], start=(j == 0 and t % HALF == 0),
                                   stop=(j == KT_S - 1 or (j == KT_S and key == KT - 1)), skip_group_check=True)
                if part == 1:
                    mm.then_inc(s["a_pv"], 1)

            def run_unit(u, h, nxt):
                def prep_uses(first, n):
                    for i in range(first, first + n):
                        prep(*nxt, i)

                def scores_ahead(j):
                    if j + 2 < ATT_STEPS:
                        scores(u, h, j + 2)
                    elif nxt:
                        scores(*nxt, j + 2 - ATT_STEPS)

                done = 0
                for j in range(ATT_STEPS):
                    n = PREP_AT[j] if nxt else 0
                    if j == 0:
                        prep_uses(done, min(n, 2))
                        scores_ahead(j)
                        weigh(u, h, j, 0)
                        prep_uses(done + 2, n - 2)
                        weigh(u, h, j, 1)
                    elif done < PREP_LAST:
                        prep_uses(done, (n + 1) // 2)
                        weigh(u, h, j, 0)
                        prep_uses(done + (n + 1) // 2, n // 2)
                        weigh(u, h, j, 1)
                        scores_ahead(j)
                    else:
                        weigh(u, h, j, 0)
                        prep_uses(done, (n + 1) // 2)
                        weigh(u, h, j, 1)
                        prep_uses(done + (n + 1) // 2, n // 2)
                        scores_ahead(j)
                    done += n

            for i in range(PREP):
                prep(A, 0, i)
            scores(A, 0, 0)
            scores(A, 0, 1)
            with pe.Fori(0, TURNS - 1) as h:
                run_unit(A, h, (B, h))
                run_unit(B, h, (A, h + 1))
            run_unit(A, TURNS - 1, (B, TURNS - 1))
            run_unit(B, TURNS - 1, None)

        @block.scalar
        def _(act):
            def stand(u, h, i):
                p = unit(u, h)
                act.wait_ge(s["a_work"], PREP * p + i + 1)
                bank = wk[i % 2]
                if i < PREP_Q:
                    cols = slice(i * NB, (i + 1) * NB)
                    ins = act.copy(kT[u][:, cols], bank[:, :])
                    if u == A:
                        ins = act.copy(kT2[0:HEAD_DIM, cols], bank[0:HEAD_DIM, :])
                else:
                    cols = slice((i - PREP_Q) * NB, min((i - PREP_Q + 1) * NB, TOK))
                    ins = act.copy(qT[u][:, cols], bank[:, 0:cols.stop - cols.start])
                ins.then_inc(s["a_wkact"], 1)

            def exps(u, h, j):
                n = step0(u, h) + j
                b = (j + (0 if u == A else ATT_STEPS)) % 2
                act.wait_ge(s["a_scores"], n + 1)
                if j == 2:
                    act.wait_ge(s["a_pv"], n - 1)
                if j < KT_S:
                    act.activation(pr[:, b, :], sc[b][:, :, :].rearrange("p c n -> p (c n)"), ACT.Exp,
                                   scale=SCALE[u]).then_inc(s["a_exp"], 1)
                else:
                    act.activation(pr[:, b, :].rearrange("p (c n) -> p c n", c=2)[:, :, 0:SEQ], sc[b][:, :, 0:SEQ], ACT.Exp,
                                   scale=SCALE[u]).then_inc(s["a_exp"], 1)

            def run_unit(u, h, nxt):
                for j in range(ATT_STEPS):
                    exps(u, h, j)
                    if nxt and j < 2:
                        for i in range(3 * j, 3 * j + 3):
                            stand(*nxt, i)
                    if not nxt and j == ATT_STEPS // 2:
                        act.wait_ge(s["g_css"], 1)
                        act.activation(stats[:, 1, :, :], stats[:, 0, :, :], ACT.Sqrt, bias=per["eps"][:, :],
                                       scale=1.0 / C_DV).then_inc(s["g_cstd"], 1)

            for i in range(PREP_MAX):
                stand(A, 0, i)
            with act.Fori(0, TURNS - 1) as h:
                run_unit(A, h, (B, h))
                run_unit(B, h, (A, h + 1))
            run_unit(A, TURNS - 1, (B, TURNS - 1))
            run_unit(B, TURNS - 1, None)

        @block.vector
        def _(dve):
            def own(u, h, n):
                return 2 * unit(u, h) + n

            def maxima(u, h):
                p = unit(u, h)
                for i in range(PREP_MAX, PREP_LAST):
                    m = i - PREP_MAX
                    dve.wait_ge(s["a_work"], PREP * p + i + 1)
                    if m < 2 * TS:
                        dst, src = nmx[:, m // 2, m % 2:m % 2 + 1], wk[i % 2][:, :]
                    else:
                        q0 = 2 * (m - 2 * TS)
                        dst = nmx[:, q0:q0 + 2, 2] if q0 < TS else nm[:, TS:T]
                        src = wk[i % 2][:, :].rearrange("p (t n) -> p t n", t=2)
                    dve.tensor_reduce(dst, src, AX_X, ALU.max, negate=True).then_inc(s["a_wkdve"], 1)
                dve.wait_ge(s["a_wkdve"], (PREP - PREP_MAX) * p + PREP_LAST - PREP_MAX)
                dve.tensor_reduce(nm[:, 0:TS], nmx[:, 0:TS, :], AX_X, ALU.min).then_inc(s["a_own"], 1)
                dve.wait_ge(s["a_own"], own(u, h, 1))
                mc = m_cols[u]
                dve.tensor_copy(mc[:, :, 0], nm[:, :]).then_inc(s["a_own"], 1)
                dve.wait_ge(s["a_own"], own(u, h, 2))
                dve.tensor_tensor(mc[:, :, 1], nm[:, :], mc[:, :, 0].bitcast(F32), ALU.subtract).then_inc(s["a_nm"], 1)
                for i in range(PREP_LAST, PREP):
                    cols = slice((i - PREP_LAST) * NB, min((i - PREP_LAST + 1) * NB, TOK))
                    dve.wait_ge(s["a_work"], PREP * p + i + 1)
                    dve.tensor_copy(qT2[u][:, cols], wk[i % 2][:, 0:cols.stop - cols.start]).then_inc(s["a_wkdve"], 1)

            def output(u, h):
                p = unit(u, h)
                o = ob[:, :, 0:HALF * (HEAD_DIM + 1)].rearrange("p b (t e) -> p b t e", e=HEAD_DIM + 1)
                dve.wait_ge(s["a_pv"], step0(u, h) + ATT_STEPS)
                dve.reciprocal(rs[:, :, :], o[:, :, :, HEAD_DIM]).then_inc(s["a_rs"], 1)
                dve.wait_ge(s["a_rs"], p + 1)
                if u == A:
                    dst = mid["oa"][:, :, bass.ds(h * HEAD_DIM, HEAD_DIM)].rearrange("p (b t) e -> p b t e", b=2)
                else:
                    dst = mid["ob"][:, bass.ds(h, 1), :, :].rearrange("p a (b t) e -> p (a b) t e", b=2)
                r = rs[:, :, :].unsqueeze(3).broadcast_to([P, 2, HALF, HEAD_DIM])
                dve.tensor_tensor(dst, o[:, :, :, 0:HEAD_DIM], r, ALU.mult).then_inc(s["a_out"], 1)

            def gla_norm():
                do = Chain(dve, s["g_norm"])
                oc = mid["oc"]
                do(dve.tensor_tensor(csq[:, :, :], oc[:, :, :], oc[:, :, :], ALU.mult))
                dve.tensor_reduce(stats[:, 0, :, :], csq[:, :, :].rearrange("p t (h e) -> p t h e", h=C_HEADS), AX_X,
                                  ALU.add).then_inc(s["g_css"], 1)
                dve.wait_ge(s["g_cstd"], 1)
                do(dve.reciprocal(stats[:, 2, :, :], stats[:, 1, :, :]))
                o4 = oc[:, :, :].rearrange("p t (h e) -> p (t h) e", h=C_HEADS)
                r3 = stats[:, 2, :, :].rearrange("p t h -> p (t h)").unsqueeze(2).broadcast_to([P, T * C_HEADS, C_DV])
                do(dve.tensor_tensor(o4, o4, r3, ALU.mult))
                do(dve.tensor_tensor(o4, o4, per["gains"][:, 3, :].unsqueeze(1).broadcast_to([P, T * C_HEADS, C_DV]), ALU.mult))

            dve.memset(kT2[HEAD_DIM:, :].bitcast(F32), 0.0).then_inc(s["a_out"], 1)
            dve.wait_ge(s["a_out"], 1)
            dve.memset(kT2[HEAD_DIM:HEAD_DIM + 2, :].bitcast(F32), 1.0)
            maxima(A, 0)
            with dve.Fori(0, TURNS - 1) as h:
                maxima(B, h)
                output(A, h)
                maxima(A, h + 1)
                output(B, h)
            maxima(B, TURNS - 1)
            output(A, TURNS - 1)
            gla_norm()
            output(B, TURNS - 1)


def output_block(nc, l, io, per, mid, s):
    BV = B_HEADS * B_V
    AW = A_HEADS * HEAD_DIM
    with ExitStack() as ctx:
        def sb(name, shape, dt=F32):
            return ctx.enter_context(nc.sbuf_tensor(name, shape, dt))

        wst = sb("wo_stage", [P, 2, D_MODEL])
        w_hi = sb("wo_hi", [P, KD, D_MODEL], F32R)
        w_lo = sb("wo_lo", [P, KD, D_MODEL], F32R)
        ones = sb("ones", [P, P])
        gp = sb("post_rows", [P, 2, D_MODEL])
        su = per["cv"][:, :, :].rearrange("p t c -> p (t c)")[:, 0:2 * D_MODEL].rearrange("p (b c) -> p b c", b=2)
        xt = sb("xo_tiles", [P, 2, D_MODEL])
        yt = sb("y_tiles", [P, 2, D_MODEL])
        diag = yt[:, :, :].rearrange("p g (k n) -> p g k n", n=P)
        mx = sb("mixed", [P, D_MODEL])
        bo = sb("b_out", [P, 2, B_HEADS, B_V])
        bsq = sb("b_sq", [P, B_HEADS, B_V])
        bst = sb("b_stats", [P, 2, 3, B_HEADS])
        yst = sb("y_stats", [P, 3, T])
        m_hi = sb("mT_hi", [P, 2, KD, P], F32R)
        m_lo = sb("mT_lo", [P, 2, KD, P], F32R)
        tp = [ctx.enter_context(nc.psum_tensor(f"m_tr{i}", [P, KD, P], F32)) for i in range(2)]
        yp = [ctx.enter_context(nc.psum_tensor(f"y_acc{i}", [P, D_MODEL], F32)) for i in range(2)]
        block = ctx.enter_context(nc.Block())

        def group(t):
            return 0 if t < TS else 1

        @block.sync
        def _(sp):
            def load_tile(t):
                if t >= 2:
                    sp.wait_ge(s["o_mix"], t - 1)
                sp.dma_start(su[:, t % 2, :], io["Us"][tile_rows(t), :]).then_inc(s[f"o_su{t % 2}"], 16)
                if t >= 2:
                    sp.wait_ge(s["o_y"], t - 1)
                new, old, r = ((io["y_sample"], io["x_sample"], t * P) if t < TS
                               else (io["y_prompt"], io["x_prompt"], (t - TS) * P))
                with sp.If(l < 1):
                    sp.dma_start(xt[:, t % 2, :], old[r:r + P, :]).then_inc(s[f"o_x{t % 2}"], 16)
                with sp.Else():
                    sp.dma_start(xt[:, t % 2, :], new[r:r + P, :]).then_inc(s[f"o_x{t % 2}"], 16)

            def store(t):
                dst, r = (io["y_sample"], t * P) if t < TS else (io["y_prompt"], (t - TS) * P)
                sp.wait_ge(s["o_y"], t + 1)
                sp.dma_start(dst[r:r + P, :], yt[:, t % 2, :]).then_inc(s[f"o_st{t % 2}"], 16)

            load_tile(0)
            load_tile(1)
            for k in range(KD):
                if k >= 2:
                    sp.wait_ge(s["o_wlo"], k - 1)
                sp.dma_start(wst[:, k % 2, :], io["w_out"][bass.ds(l, 1), k * P:(k + 1) * P, :].rearrange("a p n -> (a p) n")
                             ).then_inc(s[f"o_w{k % 2}"], 16)
            for t in range(T):
                if t + 2 < T:
                    load_tile(t + 2)
                store(t)
            for i in range(2):
                sp.wait_ge(s[f"o_st{i}"], 16 * T // 2)

        @block.tensor
        def _(pe):
            pe.wait_ge(s["o_diag"], 1)
            for g in range(2):
                for k in range(KD):
                    mm = pe.matmul(yp[g][:, k * P:(k + 1) * P], ones[:, :], diag[:, g, k, :], start=True, stop=True)
                mm.then_inc(s["o_gp"], 1)

            def turn(t):
                pe.wait_ge(s["o_mix"], t + 1)
                if t >= 2:
                    pe.wait_ge(s["o_mlo"], t - 1)
                for k in range(KD):
                    mm = pe.transpose(tp[t % 2][:, k, :], mx[:, k * P:(k + 1) * P], per["ident"][:, :])
                mm.then_inc(s["o_turned"], 1)

            turn(0)
            turn(1)
            for t in range(T):
                pe.wait_ge(s["o_mlo"], t + 1)
                if t < 2:
                    pe.wait_ge(s["o_gpcopy"], t + 1)
                else:
                    pe.wait_ge(s["o_y1"], t - 1)
                for c in range(2):
                    cols = slice(c * NB, (c + 1) * NB)
                    for k in range(KD):
                        if t == 0:
                            pe.wait_ge(s["o_wlo"], k + 1)
                        for q, (mm_, ww) in enumerate(((m_hi, w_hi), (m_hi, w_lo), (m_lo, w_hi))):
                            mm = pe.matmul(yp[t % 2][:, cols], mm_[:, t % 2, k, :], ww[:, k, cols],
                                           start=(k == 0 and q == 0), stop=(k == KD - 1 and q == 2))
                mm.then_inc(s["o_acc"], 1)
                if t + 2 < T:
                    turn(t + 2)

        @block.scalar
        def _(act):
            def b_std(t):
                act.wait_ge(s["o_bss"], t + 1)
                act.activation(bst[:, t % 2, 1, :], bst[:, t % 2, 0, :], ACT.Sqrt, bias=per["eps"][:, :],
                               scale=1.0 / B_V).then_inc(s["o_bstd"], 1)

            def hi(t):
                act.wait_ge(s["o_turned"], t + 1)
                if t >= 2:
                    act.wait_ge(s["o_acc"], t - 1)
                act.copy(m_hi[:, t % 2, :, :], tp[t % 2][:, :, :]).then_inc(s["o_mhi"], 1)

            def w_split(k):
                act.wait_ge(s[f"o_w{k % 2}"], 16 * (k // 2 + 1))
                act.copy(w_hi[:, k, :], wst[:, k % 2, :]).then_inc(s["o_whi"], 1)

            for g in range(2):
                act.wait_ge(s["o_gp"], g + 1)
                act.copy(gp[:, g, :], yp[g][:, :]).then_inc(s["o_gpcopy"], 1)
            b_std(0)
            w_split(0)
            w_split(1)
            b_std(1)
            hi(0)
            w_split(2)
            w_split(3)
            b_std(2)
            hi(1)
            for k in range(4, KD):
                w_split(k)
            for t in range(T):
                if t + 3 < T:
                    b_std(t + 3)
                act.wait_ge(s["o_acc"], t + 1)
                if t >= 2:
                    act.wait_ge(s[f"o_st{t % 2}"], 16 * (t // 2))
                act.activation(yt[:, t % 2, :], yp[t % 2][:, :], ACT.Square, accum_out=yst[:, 0, t:t + 1]).then_inc(s["o_sq"], 1)
                act.wait_ge(s["o_sq"], t + 1)
                act.activation(yst[:, 1, t:t + 1], yst[:, 0, t:t + 1], ACT.Sqrt, bias=per["eps"][:, :],
                               scale=1.0 / D_MODEL).then_inc(s["o_std"], 1)
                if t + 2 < T:
                    hi(t + 2)

        @block.vector
        def _(dve):
            do = Chain(dve, s["o_dve"])
            dve.memset(ones[:, :], 1.0)
            for g in range(2):
                for k in range(KD):
                    ins = dve.tensor_scalar(diag[:, g, k, :], per["ident"][:, :], per["post"][:, g, k:k + 1], None, ALU.mult)
            ins.then_inc(s["o_diag"], 1)

            def b_diff(t):
                o = mid["ob"]
                if t >= 2:
                    dve.wait_ge(s["o_mix"], t - 1)
                do(dve.scalar_tensor_tensor(out=bo[:, t % 2, :, :], in0=o[:, 1::2, t, :], scalar=per["neg_lam"][:, 0:1],
                                            in1=o[:, 0::2, t, :], op0=ALU.mult, op1=ALU.add))
                do(dve.tensor_tensor(bsq[:, :, :], bo[:, t % 2, :, :], bo[:, t % 2, :, :], ALU.mult))
                dve.tensor_reduce(bst[:, t % 2, 0, :], bsq[:, :, :], AX_X, ALU.add).then_inc(s["o_bss"], 1)

            def mix(t):
                b = t % 2
                dve.wait_ge(s["o_bstd"], t + 1)
                do(dve.reciprocal(bst[:, b, 2, :], bst[:, b, 1, :]))
                do(dve.tensor_tensor(bo[:, b, :, :], bo[:, b, :, :], bst[:, b, 2, :].unsqueeze(2).broadcast_to([P, B_HEADS, B_V]), ALU.mult))
                do(dve.tensor_tensor(bo[:, b, :, :], bo[:, b, :, :],
                                     per["gains"][:, 2, :].unsqueeze(1).broadcast_to([P, B_HEADS, B_V]), ALU.mult))
                dve.wait_ge(s[f"o_su{b}"], 16 * (t // 2 + 1))
                if t:
                    dve.wait_ge(s["o_turned"], t)
                dve.tensor_tensor(mx[:, 0:AW], mid["oa"][:, t, :], su[:, b, 0:AW], ALU.mult)
                dve.tensor_tensor(mx[:, AW:AW + BV], bo[:, b, :, :].rearrange("p h e -> p (h e)"), su[:, b, AW:AW + BV], ALU.mult)
                dve.tensor_tensor(mx[:, AW + BV:], mid["oc"][:, t, :], su[:, b, AW + BV:], ALU.mult).then_inc(s["o_mix"], 1)

            def lo(t):
                dve.wait_ge(s["o_mhi"], t + 1)
                dve.tensor_tensor(m_lo[:, t % 2, :, :], tp[t % 2][:, :, :], m_hi[:, t % 2, :, :].bitcast(F32),
                                  ALU.subtract).then_inc(s["o_mlo"], 1)

            def w_lo_part(k):
                dve.wait_ge(s["o_whi"], k + 1)
                dve.tensor_tensor(w_lo[:, k, :], wst[:, k % 2, :], w_hi[:, k, :].bitcast(F32), ALU.subtract).then_inc(s["o_wlo"], 1)

            def finish(t):
                b, g = t % 2, group(t)
                dve.wait_ge(s["o_std"], t + 1)
                do(dve.reciprocal(yst[:, 2, t:t + 1], yst[:, 1, t:t + 1]))
                dve.wait_ge(s["o_gpcopy"], 2)
                dve.scalar_tensor_tensor(out=yt[:, b, :], in0=yp[b][:, :], scalar=yst[:, 2, t:t + 1], in1=gp[:, g, :],
                                         op0=ALU.mult, op1=ALU.mult).then_inc(s["o_y1"], 1)
                dve.wait_ge(s["o_y1"], t + 1)
                dve.wait_ge(s[f"o_x{b}"], 16 * (t // 2 + 1))
                dve.tensor_tensor(yt[:, b, :], yt[:, b, :], xt[:, b, :], ALU.add).then_inc(s["o_y"], 1)

            b_diff(0)
            b_diff(1)
            w_lo_part(0)
            w_lo_part(1)
            mix(0)
            lo(0)
            w_lo_part(2)
            w_lo_part(3)
            b_diff(2)
            mix(1)
            lo(1)
            for k in range(4, KD):
                w_lo_part(k)
            for t in range(T):
                if t + 3 < T:
                    b_diff(t + 3)
                if t + 2 < T:
                    mix(t + 2)
                finish(t)
                if t + 2 < T:
                    lo(t + 2)


def prologue_block(nc, io, per, s):
    with ExitStack() as ctx:
        crow = ctx.enter_context(nc.sbuf_tensor("cond_rows", [2 * KD, P], F32))
        tr = ctx.enter_context(nc.psum_tensor("cond_tr", [P, NB], F32))
        block = ctx.enter_context(nc.Block())
        loads = [(per["ident"][:, :], io["ident"]), (crow[0:KD, :], io["c"].rearrange("b (k p) -> (b k) p", p=P)),
                 (crow[KD:, :], io["c_ctx"].rearrange("(k p) -> k p", p=P)),
                 (per["tri"][:, :, :], io["tri"]), (per["bdmask"][:, :], io["bdmask"]),
                 (per["cosA"][:, :, :], io["ropeA"][0].rearrange("(t p) d -> p t d", p=P)),
                 (per["sinA"][:, :, :], io["ropeA"][1].rearrange("(t p) d -> p t d", p=P)),
                 (per["cosB"][:, :, :], io["ropeB"][0].rearrange("(t p) d -> p t d", p=P)),
                 (per["sinB"][:, :, :], io["ropeB"][1].rearrange("(t p) d -> p t d", p=P))]

        @block.sync
        def _(sp):
            for dst, src in loads:
                sp.dma_start(dst, src).then_inc(s["c_load"], 16)

        @block.vector
        def _(dve):
            dve.memset(per["eps"][:, :], EPS).then_inc(s["c_set"], 1)
            dve.memset(per["gate_w"][:, :], 0.0).then_inc(s["c_set"], 1)
            dve.memset(per["lrT"][2 * RANK:2 * RANK + 1, :], 1.0).then_inc(s["c_set"], 1)
            dve.memset(per["one"][:, :], 1.0).then_inc(s["c_set"], 1)
            dve.wait_ge(s["c_load"], 16 * len(loads))
            dve.tensor_copy(per["ident_r"][:, :], per["ident"][:, :]).then_inc(s["c_set"], 1)
            dve.wait_ge(s["c_set"], 5)

        @block.tensor
        def _(pe):
            pe.wait_ge(s["c_load"], 16 * len(loads))
            pe.transpose(tr[:, 0:2 * KD], crow[:, :], per["ident"][0:2 * KD, 0:2 * KD]).then_inc(s["c_tr"], 1)

        @block.scalar
        def _(act):
            act.wait_ge(s["c_tr"], 1)
            act.activation(per["cond"][:, :, :].rearrange("p k g -> p g k"), tr[:, 0:2 * KD].rearrange("p (g k) -> p g k", g=2),
                           ACT.Silu).then_inc(s["c_silu"], 1)
            act.wait_ge(s["c_silu"], 1)


SEMS = (["c_load", "c_set", "c_tr", "c_silu"]
        + ["m_small", "m_used", "m_tr", "m_dot", "m_exp", "m_dve"] + ["m_hi", "m_lo", "m_evac", "m_turned", "m_cond"] + [f"m_w{i}" for i in range(4)]
        + ["p_x0", "p_x1", "p_xn", "p_wlo", "p_whi", "p_zo", "p_ev", "p_turned", "p_h32", "p_hhi", "p_h", "p_acc", "p_wfree",
           "p_sq", "p_std", "p_hss", "p_hstd", "p_dve"]
        + ["g_zero", "g_st0", "g_chain", "g_new", "g_min", "g_pre", "g_gate", "g_exp", "g_cum", "g_mul", "g_k2t", "g_tr", "g_am",
           "g_at", "g_dsm", "g_ds", "g_oi", "g_o", "g_oc", "g_inter", "g_act", "g_abs", "g_ln", "g_css", "g_cstd", "g_dve", "g_norm", "g_qbd", "g_qt", "g_bwd"]
        + ["a_ones", "a_rawA", "a_rawB", "a_vA", "a_vB", "a_splitA", "a_splitB", "a_pv", "a_pool", "a_work", "a_wkdve", "a_wkact",
           "a_nm", "a_exp", "a_scores", "a_out", "a_own", "a_rs"]
        + ["o_mix", "o_su0", "o_su1", "o_y", "o_x0", "o_x1", "o_st0", "o_st1", "o_wlo", "o_w0", "o_w1", "o_diag", "o_gp", "o_mlo",
           "o_turned", "o_gpcopy", "o_y1", "o_acc", "o_bss", "o_bstd", "o_mhi", "o_whi", "o_sq", "o_std", "o_dve"]
        + [f"p_w{i}" for i in range(STAGES)] + [f"p_out{i}" for i in range(3)] + [f"p_new{i}" for i in range(3)])


def program(nc, io):
    with ExitStack() as ctx:
        def sb(name, shape, dt=F32):
            return ctx.enter_context(nc.sbuf_tensor(name, shape, dt))

        s = {n: ctx.enter_context(nc.semaphore(n)) for n in SEMS}
        per = {
            "ident": sb("ident", [P, P]), "ident_r": sb("ident_r", [P, P], F32R), "tri": sb("tri", [P, 2, P]), "bdmask": sb("bdmask", [P, C_HEADS]),
            "cosA": sb("cosA", [P, TS, HEAD_DIM]), "sinA": sb("sinA", [P, TS, HEAD_DIM]),
            "cosB": sb("cosB", [P, TS, B_QK]), "sinB": sb("sinB", [P, TS, B_QK]),
            "cond": sb("cond", [P, KD, 2]), "eps": sb("eps", [P, 1]), "one": sb("one", [P, 1]),
            "gains": sb("gains", [P, 4, HEAD_DIM]), "neg_lam": sb("neg_lam", [P, 1]),
            "h_scale": sb("h_scale", [P, 2, KD]), "h_shift": sb("h_shift", [P, 2, KD]), "post": sb("post", [P, 2, KD]),
            "gate_w": sb("gate_w", [2 * RANK + 1, 2 * C_HEADS * C_DK]), "lrT": sb("lrT", [2 * RANK + 1, TOK]),
            "cqT": sb("cqT", [P, TOK]), "ckT": sb("ckT", [P, TOK]), "cv": sb("cv", [P, T, C_HEADS * C_DV]),
        }
        io["Zs"] = nc.dram_tensor("z_scratch", [TOK, Z_COLS], F32).ap()
        io["Us"] = nc.dram_tensor("u_scratch", [TOK, D_MODEL], F32).ap()
        prologue_block(nc, io, per, s)
        with nc.Fori(0, DEPTH) as l:
            modulation_block(nc, l, io, per, s)
            projection_block(nc, l, io, per, s)
            with ExitStack() as branch:
                mid = {n: branch.enter_context(nc.sbuf_tensor(n, shape, F32)) for n, shape in (
                    ("oa", [P, T, A_HEADS * HEAD_DIM]), ("ob", [P, 2 * B_HEADS, T, B_V]), ("oc", [P, T, C_HEADS * C_DV]))}
                with ExitStack() as front:
                    att = attention_front(nc, front)
                    gla_block(nc, l, io, per, mid, att, s)
                    attention_block(nc, l, io, per, mid, att, s)
                output_block(nc, l, io, per, mid, s)
            nc.all_engine_barrier(sems_to_clear=range(s[SEMS[4]].num, s[SEMS[-1]].num + 1))


_OUTS = {"y_prompt": (1, SEQ, D_MODEL), "y_sample": (1, DEC_SEQ, D_MODEL),
         "new_a_k": (1, DEPTH, A_KV, SEQ, HEAD_DIM), "new_a_v": (1, DEPTH, A_KV, SEQ, HEAD_DIM),
         "new_b_k": (1, DEPTH, B_HEADS, SEQ, 2 * B_QK), "new_b_v": (1, DEPTH, B_HEADS, SEQ, B_V),
         "new_state_c_fwd": (1, DEPTH, C_HEADS, C_DK, C_DV), "new_state_c_bwd": (1, DEPTH, C_HEADS, C_DK, C_DV)}


def shape_constants():
    import numpy as np

    f = np.float32
    j, i = np.arange(P)[:, None], np.arange(P)[None, :]
    same = j // 64 == i // 64
    tri = np.stack([same & (j <= i), same & (j >= i)], 1).astype(f)
    bd = (np.arange(P)[:, None] // C_DK == np.arange(C_HEADS)[None, :]).astype(f)
    t = np.arange(DEC_SEQ)

    def rope(d):
        half = d // 4
        freq = (f(ROPE_THETA) ** (-np.arange(half, dtype=f) / f(half))).astype(f)
        cos, sin = [], []
        for pos in (t // GRID_W, t % GRID_W):
            ang = pos.astype(f)[:, None] * freq[None, :]
            cos += [np.cos(ang), np.cos(ang)]
            sin += [-np.sin(ang), np.sin(ang)]
        return np.stack([np.concatenate(cos, 1), np.concatenate(sin, 1)]).astype(f)

    lam = np.array([[0.8 - 0.6 * np.exp(-0.3 * l), 0.2 + 0.6 * np.exp(-0.3 * l)] for l in range(DEPTH)], f)
    return {"ident": np.eye(P, dtype=f), "tri": tri, "bdmask": bd, "ropeA": rope(HEAD_DIM), "ropeB": rope(B_QK),
            "lam_consts": lam}


def kernel(**inputs):
    import numpy as np
    import concourse.bacc as bacc
    from concourse.bass_utils import run_bass_kernel_spmd

    nc = bacc.Bacc("TRN2", target_bir_lowering=False, num_devices=1)
    arrays, io = {}, {}
    for name, a in {**inputs, **shape_constants()}.items():
        a = np.ascontiguousarray(a)
        arrays[f"in_{name}"] = a
        io[name] = nc.dram_tensor(f"in_{name}", a.shape, mybir.dt.from_np(a.dtype), kind="ExternalInput").ap()
    for name, shape in _OUTS.items():
        io[name] = nc.dram_tensor(f"out_{name}", shape, F32, kind="ExternalOutput").ap()
    for name in ("x_prompt", "x_sample", "y_prompt", "y_sample"):
        io[name] = io[name].rearrange("b t d -> (b t) d")
    for name in ("new_a_k", "new_a_v", "new_b_k", "new_b_v", "new_state_c_fwd", "new_state_c_bwd",
                 "cache_a_k", "cache_a_v", "cache_b_k", "cache_b_v", "state_c_fwd", "state_c_bwd"):
        io[name] = io[name].rearrange("b l h x y -> (b l) h x y")
    program(nc, io)
    r = run_bass_kernel_spmd(nc, [arrays], core_ids=[0])
    return tuple(r.results[0][f"out_{name}"] for name in _OUTS)
```

```python
from contextlib import ExitStack

import concourse.bass as bass
from concourse import mybir

F32 = mybir.dt.float32
F32R = mybir.dt.float32r
ACT = mybir.ActivationFunctionType
ALU = mybir.AluOpType
AX_X = mybir.AxisListType.X

P = 128
D_MODEL = 1024
DEPTH = 2
SEQ, DEC_SEQ, PAST = 256, 1024, 256
GRID_W = 64
HEAD_DIM = 64
A_HEADS, A_KV = 8, 2
B_HEADS, B_QK, B_V = 4, 32, 64
C_HEADS, C_DK, C_DV = 4, 32, 64
RANK, TAU = 16, 16.0
EPS = 1e-6
ROPE_THETA = 10000.0

KD = D_MODEL // P
TS = DEC_SEQ // P
TP = SEQ // P
T = TS + TP
TOK = T * P
NB = 512
Z_COLS = 3 * NB
C_COL0 = Z_COLS
LR_COL0 = C_COL0 + NB
U_COL0 = LR_COL0 + 2 * RANK
IN_WIDTH = U_COL0 + D_MODEL

BLOCKS = [("z", 2 * NB, NB), ("z", 0, NB), ("z", NB, NB), ("c", C_COL0, NB),
          ("u", U_COL0, NB), ("u", U_COL0 + NB, NB), ("lr", LR_COL0, P)]
Z_BLOCKS = 3
RING = 12
STAGES = 4


def tile_rows(t):
    return slice(t * P, (t + 1) * P)


class Chain:

    def __init__(self, eng, sem):
        self.eng, self.sem, self.n = eng, sem, 0

    def __call__(self, ins):
        self.n += 1
        ins.then_inc(self.sem, 1)
        self.eng.wait_ge(self.sem, self.n)


class ProjectionFront:

    def __init__(self, nc, ctx, l, io, per, s):
        self.l, self.io, self.per, self.s = l, io, per, s
        self.stage = ctx.enter_context(nc.sbuf_tensor("w_stage", [P, STAGES, NB], F32))
        self.xs = ctx.enter_context(nc.sbuf_tensor("x_tiles", [P, 2, D_MODEL], F32))
        self.xn = ctx.enter_context(nc.sbuf_tensor("x_normed", [P, D_MODEL], F32))
        self.ss = ctx.enter_context(nc.sbuf_tensor("x_stats", [P, 3, T], F32))
        self.tp = [ctx.enter_context(nc.psum_tensor(f"h_tr{i}", [P, KD, P], F32)) for i in range(2)]

    def load_x(self, sp, t):
        s, io = self.s, self.io
        if t >= 2:
            sp.wait_ge(s["p_xn"], t - 1)
        new, old, r = ((io["y_sample"], io["x_sample"], t * P) if t < TS
                       else (io["y_prompt"], io["x_prompt"], (t - TS) * P))
        with sp.If(self.l < 1):
            sp.dma_start(self.xs[:, t % 2, :], old[r:r + P, :]).then_inc(s[f"p_x{t % 2}"], 16)
        with sp.Else():
            sp.dma_start(self.xs[:, t % 2, :], new[r:r + P, :]).then_inc(s[f"p_x{t % 2}"], 16)

    def load_w(self, sp, first, end):
        s = self.s
        for n in range(first, min(end, KD * len(BLOCKS))):
            (_, c0, cols), k = BLOCKS[n // KD], n % KD
            if n >= STAGES:
                sp.wait_ge(s["p_wlo"], n - STAGES + 1)
            sp.dma_start(self.stage[:, n % STAGES, 0:cols],
                         self.io["w_in"][bass.ds(self.l, 1), k * P:(k + 1) * P, c0:c0 + cols].rearrange("a p n -> (a p) n")
                         ).then_inc(s[f"p_w{n % STAGES}"], 16)

    def square(self, act, t):
        s, ss = self.s, self.ss
        act.wait_ge(s[f"p_x{t % 2}"], 16 * (t // 2 + 1))
        if t:
            act.wait_ge(s["p_turned"], t)
        act.activation(self.xn[:, :], self.xs[:, t % 2, :], ACT.Square, accum_out=ss[:, 0, t:t + 1]).then_inc(s["p_sq"], 1)
        act.wait_ge(s["p_sq"], t + 1)
        act.activation(ss[:, 1, t:t + 1], ss[:, 0, t:t + 1], ACT.Sqrt, bias=self.per["eps"][:, :],
                       scale=1.0 / D_MODEL).then_inc(s["p_std"], 1)

    def norm_x(self, dve, t):
        s, ss = self.s, self.ss
        dve.wait_ge(s["p_std"], t + 1)
        dve.reciprocal(ss[:, 2, t:t + 1], ss[:, 1, t:t + 1]).then_inc(s["p_rstd"], 1)
        dve.wait_ge(s["p_rstd"], t + 1)
        dve.tensor_scalar(self.xn[:, :], self.xs[:, t % 2, :], ss[:, 2, t:t + 1], None, ALU.mult).then_inc(s["p_xn"], 1)

    def turn(self, pe, t):
        s = self.s
        pe.wait_ge(s["p_xn"], t + 1)
        if t >= 2:
            pe.wait_ge(s["p_h32"], t - 1)
        for k in range(KD):
            mm = pe.transpose(self.tp[t % 2][:, k, :], self.xn[:, k * P:(k + 1) * P], self.per["ident"][:, :])
        mm.then_inc(s["p_turned"], 1)


def modulation_block(nc, l, io, per, f, s):
    NT = 3 * KD
    WST, WSP, KH = 4, 3, KD // 2
    CH = 3 * D_MODEL // NB
    MB = NB // P
    with ExitStack() as ctx:
        def sb(name, shape, dt=F32):
            return ctx.enter_context(nc.sbuf_tensor(name, shape, dt))

        wst = sb("mod_w", [P, WST, KH, NB])
        w_hi = sb("mod_w_hi", [P, WSP, KH, NB], F32R)
        w_lo = sb("mod_w_lo", [P, WSP, KH, NB], F32R)
        cond = sb("mod_cond", [P, KD, P], F32R)
        parts = sb("mod_parts", [2 * 2, CH, NB])
        rows = sb("mod_rows", [NT + 2 * KD, P])
        lams = sb("mod_lams", [P, 4, B_QK])
        prod = sb("mod_prod", [P, 2, B_QK])
        dots = sb("mod_dots", [P, 2])
        lam_c = sb("mod_lam_c", [P, 2])
        mod = sb("mod_cols", [P, 2, NT])
        one_scale = sb("mod_one_scale", [P, 2, KD])
        bcols = sb("mod_bcols", [P, NT + 2 * KD])
        acc = [ctx.enter_context(nc.psum_tensor(f"mod_acc{i}", [P, NB], F32)) for i in range(2)]
        tr = ctx.enter_context(nc.psum_tensor("mod_tr", [P, NB], F32))
        col = ctx.enter_context(nc.psum_tensor("mod_col", [P, 2 * KD, 4], F32))
        gate_col = tr[:, 2 * NT:2 * NT + 4 * KD].rearrange("p (m s) -> p m s", s=4)

        def sums(m0, m1):
            return col[:, m0:m1, :] if m1 <= 2 * KD else gate_col[:, m0 - 2 * KD:m1 - 2 * KD, :]

        block = ctx.enter_context(nc.Block())

        def layer(ap):
            return ap[bass.ds(l, 1)]

        @block.sync
        def _(sp):
            def load_w(i):
                c, k0 = i // 2, (i % 2) * KH
                if i >= WST:
                    sp.wait_ge(s["m_lo"], i - WST + 1)
                src = io["w_mod"][bass.ds(l, 1), k0 * P:(k0 + KH) * P, c * NB:(c + 1) * NB]
                sp.dma_start(wst[:, i % WST, :, :], src.rearrange("a (k p) n -> p (a k) n", p=P)).then_inc(s[f"m_w{i % WST}"], 16)

            for i in range(WST):
                load_w(i)
            sp.dma_start(rows[0:NT, :], layer(io["b_mod"]).rearrange("a (m p) -> (a m) p", p=P)).then_inc(s["m_small"], 16)
            sp.dma_start(rows[NT:NT + KD, :], layer(io["g_pre"]).rearrange("a (m p) -> (a m) p", p=P)).then_inc(s["m_small"], 16)
            sp.dma_start(rows[NT + KD:, :], layer(io["g_post"]).rearrange("a (m p) -> (a m) p", p=P)).then_inc(s["m_small"], 16)
            for i, name in enumerate(("b_lambda_q1", "b_lambda_k1", "b_lambda_q2", "b_lambda_k2")):
                sp.dma_start(lams[:, i, :], layer(io[name]).broadcast_to([P, B_QK])).then_inc(s["m_small"], 16)
            for i, name in enumerate(("a_q_gain", "a_k_gain", "b_out_gain", "c_out_gain")):
                sp.dma_start(per["gains"][:, i, :], layer(io[name]).broadcast_to([P, HEAD_DIM])).then_inc(s["m_small"], 16)
            sp.dma_start(lam_c[:, :], layer(io["lam_consts"]).broadcast_to([P, 2])).then_inc(s["m_small"], 16)
            C = C_HEADS * C_DK
            gw = per["gate_w"]
            sp.dma_start(gw[0:RANK, 0:C], layer(io["c_gate_w_fwd"]).rearrange("a r c -> (a r) c")).then_inc(s["m_small"], 16)
            sp.dma_start(gw[RANK:2 * RANK, C:2 * C], layer(io["c_gate_w_bwd"]).rearrange("a r c -> (a r) c")).then_inc(s["m_small"], 16)
            sp.dma_start(gw[2 * RANK:2 * RANK + 1, 0:C], layer(io["c_gate_b_fwd"])).then_inc(s["m_small"], 16)
            sp.dma_start(gw[2 * RANK:2 * RANK + 1, C:2 * C], layer(io["c_gate_b_bwd"])).then_inc(s["m_small"], 16)
            for i in range(WST, 2 * CH):
                load_w(i)
            f.load_x(sp, 0)
            f.load_x(sp, 1)
            f.load_w(sp, 0, STAGES)

        @block.tensor
        def _(pe):
            def turn(c):
                pe.wait_ge(s["m_evac"], c + 1)
                for m in range(MB):
                    mm = pe.transpose(sums(c * MB + m, c * MB + m + 1).rearrange("p m s -> p (m s)"), parts[:, c, m * P:(m + 1) * P], per["ident"][0:4, 0:4])
                mm.then_inc(s["m_turned"], 1)

            pe.wait_ge(s["m_cond"], 2)
            for i in range(2 * CH):
                c = i // 2
                pe.wait_ge(s["m_lo"], i + 1)
                if i % 2 == 0 and c >= 2:
                    pe.wait_ge(s["m_evac"], c - 1)
                for kk in range(KH):
                    for q, w in enumerate((w_hi, w_lo)):
                        mm = pe.matmul(acc[c % 2][:, :], cond[:, (i % 2) * KH + kk, :], w[:, i % WSP, kk, :],
                                       start=(i % 2 == 0 and kk == 0 and q == 0), stop=(i % 2 == 1 and kk == KH - 1 and q == 1))
                mm.then_inc(s["m_used"], 1)
                if i % 2 and c:
                    turn(c - 1)
                if i == WST:
                    pe.wait_ge(s["m_small"], 16 * 16)
                    pe.transpose(tr[:, 0:NT + 2 * KD], rows[:, :], per["ident"][0:NT + 2 * KD, 0:NT + 2 * KD]).then_inc(s["m_tr"], 1)
            f.turn(pe, 0)
            turn(CH - 1)

        @block.scalar
        def _(act):
            def hi(i):
                act.wait_ge(s[f"m_w{i % WST}"], 16 * (i // WST + 1))
                if i >= WSP:
                    act.wait_ge(s["m_used"], i - WSP + 1)
                act.copy(w_hi[:, i % WSP, :, :], wst[:, i % WST, :, :]).then_inc(s["m_hi"], 1)

            for i in range(WSP):
                hi(i)
            for c in range(CH):
                if c + 2 < CH:
                    hi(2 * c + 3)
                    act.wait_ge(s["m_used"], 2 * c + 2)
                    act.copy(parts[:, c, :], acc[c % 2][0:4, :]).then_inc(s["m_evac"], 1)
                    hi(2 * c + 4)
                    if c == 1:
                        act.wait_ge(s["m_dot"], 2)
                        act.activation(dots[:, :], dots[:, :], ACT.Exp).then_inc(s["m_exp"], 1)
                else:
                    if c + 1 < CH:
                        hi(2 * c + 3)
                        f.square(act, 0)
                    act.wait_ge(s["m_used"], 2 * c + 2)
                    act.copy(parts[:, c, :], acc[c % 2][0:4, :]).then_inc(s["m_evac"], 1)
            f.square(act, 1)

        @block.vector
        def _(dve):
            do = Chain(dve, s["m_dve"])
            do(dve.memset(cond[:, :, :].bitcast(F32), 0.0))
            do(dve.tensor_copy(cond[:, :, 0:2], per["cond"][:, :, :]))
            dve.tensor_tensor(cond[:, :, 2:4], per["cond"][:, :, :], cond[:, :, 0:2].bitcast(F32), ALU.subtract).then_inc(s["m_cond"], 2)
            def both(ap, n):
                return ap.unsqueeze(1).broadcast_to([P, 2, n])

            def columns(m0, m1):
                out = mod[:, :, m0:m1]
                for g0 in (0, 2):
                    add = both(bcols[:, m0:m1], m1 - m0) if g0 == 0 else out
                    do(dve.tensor_tensor(out, sums(m0, m1)[:, :, g0:g0 + 2].rearrange("p m g -> p g m"), add, ALU.add))

            for i in range(2 * CH):
                dve.wait_ge(s["m_hi"], i + 1)
                dve.tensor_tensor(w_lo[:, i % WSP, :, :], wst[:, i % WST, :, :], w_hi[:, i % WSP, :, :].bitcast(F32),
                                  ALU.subtract).then_inc(s["m_lo"], 1)
                if i == WST:
                    dve.wait_ge(s["m_small"], 16 * 16)
                    do(dve.tensor_tensor(prod[:, :, :], lams[:, 0:4:2, :], lams[:, 1:4:2, :], ALU.mult))
                    dve.tensor_reduce(dots[:, :], prod[:, :, :], AX_X, ALU.add).then_inc(s["m_dot"], 2)
                if i == 2 * WST:
                    dve.wait_ge(s["m_exp"], 1)
                    do(dve.tensor_tensor(per["neg_lam"][:, :], dots[:, 1:2], dots[:, 0:1], ALU.subtract))
                    do(dve.tensor_tensor(per["neg_lam"][:, :], per["neg_lam"][:, :], lam_c[:, 0:1], ALU.subtract))
                    do(dve.tensor_scalar(per["gains"][:, 2, :], per["gains"][:, 2, :], lam_c[:, 1:2], None, ALU.mult))
                    dve.wait_ge(s["m_tr"], 1)
                    do(dve.tensor_copy(bcols[:, :], tr[:, 0:NT + 2 * KD]))
            f.norm_x(dve, 0)
            dve.wait_ge(s["m_turned"], 2 * KD // MB)
            columns(0, 2 * KD)
            do(dve.tensor_copy(per["h_shift"][:, :, :], mod[:, :, 0:KD]))
            do(dve.tensor_scalar(one_scale[:, :, :], mod[:, :, KD:2 * KD], 1.0, None, ALU.add))
            do(dve.tensor_tensor(per["h_scale"][:, :, :], one_scale[:, :, :], both(bcols[:, NT:NT + KD], KD), ALU.mult))
            f.norm_x(dve, 1)
            dve.wait_ge(s["m_turned"], CH)
            columns(2 * KD, NT)
            do(dve.tensor_tensor(per["post"][:, :, :], mod[:, :, 2 * KD:], both(bcols[:, NT + KD:], KD), ALU.mult))


def projection_block(nc, l, io, per, f, s):
    with ExitStack() as ctx:
        def sb(name, shape, dt=F32):
            return ctx.enter_context(nc.sbuf_tensor(name, shape, dt))

        h_hi = sb("h_hi", [P, KD, TOK], F32R)
        h_lo = sb("h_lo", [P, KD, TOK], F32R)
        w_hi = sb("w_hi", [P, RING, NB], F32R)
        w_lo = sb("w_lo", [P, RING, NB], F32R)
        stage, tp = f.stage, f.tp
        h32 = sb("h32", [P, KD, P])
        zt = sb("z_raw", [P, 3, NB])
        zo = sb("z_out", [P, 3, NB])
        tm = sb("z_tmp", [P, 3, NB])
        hst = sb("head_stats", [P, 2, 3, A_HEADS])
        zp = [ctx.enter_context(nc.psum_tensor(f"z_acc{i}", [P, NB], F32)) for i in range(4)]
        block = ctx.enter_context(nc.Block())
        Zs, Us = io["Zs"], io["Us"]
        NW = KD * len(BLOCKS)

        def group(t):
            return 0 if t < TS else 1

        uses = []
        for b, (kind, _, _) in enumerate(BLOCKS):
            if kind in ("z", "u"):
                uses += [(b, kind, t) for t in range(T)]
            elif kind == "c":
                uses += [(b, f"cT{m}", tb) for m in range(2) for tb in range(3)] + [(b, "cv", t) for t in range(T)]
            else:
                uses += [(b, "lr", tb) for tb in range(3)]
        first_use = {b: min(i for i, u in enumerate(uses) if u[0] == b) for b in range(len(BLOCKS))}
        last_use = {b: max(i for i, u in enumerate(uses) if u[0] == b) for b in range(len(BLOCKS))}
        U_BLOCK = [kind for kind, _, _ in BLOCKS].index("u")
        U_USE0 = first_use[U_BLOCK]

        def new_stores(slot, i):
            return sum(2 for j in range(slot, i, 3) if j % T >= TS and BLOCKS[j // T][1] > 0)

        def tok_block(tb):
            return slice(tb * NB, min((tb + 1) * NB, TOK))

        def free_ring(eng, n):
            b, k = divmod(n - RING, KD)
            if k < KD - 1:
                eng.wait_ge(s["p_wfree"], b * (KD - 1) + k + 1)
            else:
                eng.wait_ge(s["p_acc"], last_use[b] + 1)

        @block.sync
        def _(sp):
            def store_z(b, t):
                i = b * T + t
                sp.wait_ge(s["p_zo"], i + 1)
                c0 = BLOCKS[b][1]
                sp.dma_start(Zs[tile_rows(t), c0:c0 + NB], zo[:, i % 3, :]).then_inc(s[f"p_out{i % 3}"], 16)
                if t >= TS:
                    rows = slice((t - TS) * P, (t - TS + 1) * P)
                    outs = {0: (), NB: (("new_a_k", 0, A_KV), ("new_a_v", A_KV * HEAD_DIM, A_KV)),
                            2 * NB: (("new_b_k", 0, B_HEADS), ("new_b_v", B_HEADS * B_V, B_HEADS))}[c0]
                    for name, c, heads in outs:
                        dst = io[name][bass.ds(l, 1), :, rows, :].rearrange("a h t d -> t (a h) d")
                        sp.dma_start(dst, zo[:, i % 3, c:c + heads * HEAD_DIM].rearrange("t (h d) -> t h d", h=heads)
                                     ).then_inc(s[f"p_new{i % 3}"], 16)

            def store_u(b, t):
                j = (b - U_BLOCK) * T + t
                i = Z_BLOCKS * T + j
                sp.wait_ge(s["p_ev"], U_USE0 + j + 1)
                c0 = BLOCKS[b][1] - U_COL0
                sp.dma_start(Us[tile_rows(t), c0:c0 + NB], zo[:, i % 3, :]).then_inc(s[f"p_out{i % 3}"], 16)

            f.load_x(sp, 2)
            f.load_w(sp, STAGES, KD)
            f.load_x(sp, 3)
            for b, (kind, _, _) in enumerate(BLOCKS):
                for t in range(T):
                    if b == 0 and t + 4 < T:
                        f.load_x(sp, t + 4)
                    if t == 0:
                        f.load_w(sp, (b + 1) * KD, (b + 1) * KD + (KD if b else STAGES))
                    elif b == 0 and t == T - 4:
                        f.load_w(sp, KD + STAGES, 2 * KD)
                    if kind == "z":
                        store_z(b, t)
                    elif kind == "u":
                        store_u(b, t)
            n = Z_BLOCKS * T + 2 * T
            for i in range(3):
                sp.wait_ge(s[f"p_out{i}"], 16 * len(range(i, n, 3)))
                sp.wait_ge(s[f"p_new{i}"], 16 * new_stores(i, Z_BLOCKS * T))

        @block.tensor
        def _(pe):
            def product(i, acc, lhs, rhs, b, w_first):
                if i >= 4:
                    pe.wait_ge(s["p_ev"], i - 3)
                last = i == last_use[b]
                for k in range(KD):
                    n = b * KD + k
                    slot = n % RING
                    if i == first_use[b]:
                        pe.wait_ge(s["p_wlo"], n + 1)
                    parts = ((h_hi, w_hi), (h_hi, w_lo), (h_lo, w_hi))
                    for q, (hh, ww) in enumerate(parts):
                        w_ap, h_ap = ww[:, slot, rhs if not w_first else lhs], hh[:, k, lhs if not w_first else rhs]
                        mm = pe.matmul(acc, w_ap if w_first else h_ap, h_ap if w_first else w_ap,
                                       start=(k == 0 and q == 0), stop=(k == KD - 1 and q == 2))
                        if last and q == 2 and k < KD - 1:
                            mm.then_inc(s["p_wfree"], 1)
                mm.then_inc(s["p_acc"], 1)

            f.turn(pe, 1)
            for i, (b, what, j) in enumerate(uses):
                acc = zp[i % 4]
                if b == 0:
                    pe.wait_ge(s["p_h"], j + 1)
                if what in ("z", "u"):
                    product(i, acc[:, :], tile_rows(j), slice(0, NB), b, False)
                elif what == "cv":
                    product(i, acc[:, 0:2 * P], tile_rows(j), slice(2 * P, 4 * P), b, False)
                else:
                    m = 0 if what == "lr" else int(what[2])
                    tb = tok_block(j)
                    product(i, acc[:, 0:tb.stop - tb.start], slice(m * P, (m + 1) * P), tb, b, True)
                if b == 0 and j + 2 < T:
                    f.turn(pe, j + 2)

        @block.scalar
        def _(act):
            def hi_h(t):
                act.wait_ge(s["p_h32"], t + 1)
                act.copy(h_hi[:, :, tile_rows(t)], h32[:, :, :]).then_inc(s["p_hhi"], 1)

            def hi_w(n):
                cols = BLOCKS[n // KD][2]
                act.wait_ge(s[f"p_w{n % STAGES}"], 16 * (n // STAGES + 1))
                if n >= RING:
                    free_ring(act, n)
                act.copy(w_hi[:, n % RING, 0:cols], stage[:, n % STAGES, 0:cols]).then_inc(s["p_whi"], 1)

            def evacuate(i):
                b, what, j = uses[i]
                act.wait_ge(s["p_acc"], i + 1)
                acc = zp[i % 4]
                if what == "z":
                    if i >= 3:
                        act.wait_ge(s["p_zo"], i - 2)
                    if BLOCKS[b][1] <= NB:
                        w = (A_HEADS if BLOCKS[b][1] == 0 else A_KV) * HEAD_DIM
                        if i > T:
                            act.wait_ge(s["p_hss"], i - T)
                        act.activation(tm[:, 0, 0:w], acc[:, 0:w], ACT.Square)
                    act.copy(zt[:, i % 3, :], acc[:, :]).then_inc(s["p_ev"], 1)
                elif what == "u":
                    q = Z_BLOCKS * T + i - U_USE0
                    act.wait_ge(s[f"p_out{q % 3}"], 16 * len(range(q % 3, q, 3)))
                    act.activation(zo[:, q % 3, :], acc[:, :], ACT.Silu).then_inc(s["p_ev"], 1)
                elif what == "cv":
                    act.copy(per["cv"][:, j, :], acc[:, 0:2 * P]).then_inc(s["p_ev"], 1)
                else:
                    tb = tok_block(j)
                    rows = 2 * RANK if what == "lr" else P
                    dst = per["lrT"] if what == "lr" else per["cqT"] if what == "cT0" else per["ckT"]
                    act.copy(dst[0:rows, tb], acc[0:rows, 0:tb.stop - tb.start]).then_inc(s["p_ev"], 1)

            def head_std(i):
                if BLOCKS[i // T][1] > NB:
                    return
                heads = A_HEADS if BLOCKS[i // T][1] == 0 else A_KV
                n = i - T + 1
                act.wait_ge(s["p_hss"], n)
                act.activation(hst[:, i % 2, 1, 0:heads], hst[:, i % 2, 0, 0:heads], ACT.Sqrt, bias=per["eps"][:, :],
                               scale=1.0 / HEAD_DIM).then_inc(s["p_hstd"], 1)

            for n in range(STAGES):
                hi_w(n)
            hi_h(0)
            hi_w(4)
            hi_h(1)
            f.square(act, 2)
            for n in range(5, KD):
                hi_w(n)
            for i, (b, what, j) in enumerate(uses):
                if i == last_use[b] and b + 1 < len(BLOCKS):
                    for k in range(4, KD):
                        hi_w((b + 1) * KD + k)
                evacuate(i)
                if 0 < i <= Z_BLOCKS * T:
                    head_std(i - 1)
                if b == 0 and j + 2 < T:
                    hi_h(j + 2)
                    if j + 3 < T:
                        f.square(act, j + 3)
                if i == first_use[b] and b + 1 < len(BLOCKS):
                    for k in range(4):
                        hi_w((b + 1) * KD + k)

        @block.gpsimd
        def _(pool):
            for n in range(NW):
                cols = BLOCKS[n // KD][2]
                pool.wait_ge(s["p_whi"], n + 1)
                pool.tensor_tensor(w_lo[:, n % RING, 0:cols], stage[:, n % STAGES, 0:cols],
                                   w_hi[:, n % RING, 0:cols].bitcast(F32), ALU.subtract).then_inc(s["p_wlo"], 1)

        @block.vector
        def _(dve):
            do = Chain(dve, s["p_dve"])

            def affine(t):
                g = group(t)
                dve.wait_ge(s["p_turned"], t + 1)
                if t:
                    dve.wait_ge(s["p_h"], t)
                for k in range(KD):
                    ins = dve.tensor_scalar(h32[:, k, :], tp[t % 2][:, k, :], per["h_scale"][:, g, k:k + 1],
                                            per["h_shift"][:, g, k:k + 1], ALU.mult, ALU.add)
                ins.then_inc(s["p_h32"], 1)

            def lo_h(t):
                dve.wait_ge(s["p_hhi"], t + 1)
                dve.tensor_tensor(h_lo[:, :, tile_rows(t)], h32[:, :, :], h_hi[:, :, tile_rows(t)].bitcast(F32),
                                  ALU.subtract).then_inc(s["p_h"], 1)

            def heads_view(ap, heads):
                return ap.rearrange("p (h d) -> p h d", h=heads)

            def rope(dst, src, t, heads, half, cos, sin, tmp):
                d = heads_view(dst, heads)
                x = heads_view(src, heads)
                w = dst.shape[1] // heads
                c = cos[:, t, :].unsqueeze(1).broadcast_to([P, heads, w])
                do(dve.tensor_tensor(d, x, c, ALU.mult))
                x4 = src.rearrange("p (h g e f) -> p h g e f", h=heads, e=2, f=half)
                t4 = tmp.rearrange("p (h g e f) -> p h g e f", h=heads, e=2, f=half)
                s3 = sin[:, t, :].rearrange("p (g e f) -> p g e f", e=2, f=half)
                g = w // (2 * half)
                for e in range(2):
                    sn = s3[:, :, e, :].unsqueeze(1).broadcast_to([P, heads, g, half])
                    do(dve.tensor_tensor(t4[:, :, :, e, :], x4[:, :, :, 1 - e, :], sn, ALU.mult))
                return dve.tensor_tensor(dst, dst, tmp, ALU.add)

            def head_sums(i):
                c0 = BLOCKS[i // T][1]
                if c0 > NB:
                    return
                heads = A_HEADS if c0 == 0 else A_KV
                dve.wait_ge(s["p_ev"], i + 1)
                w = heads * HEAD_DIM
                dve.tensor_reduce(hst[:, i % 2, 0, 0:heads], heads_view(tm[:, 0, 0:w], heads), AX_X,
                                  ALU.add).then_inc(s["p_hss"], 1)

            def finish_tile(i):
                b, t = divmod(i, T)
                c0 = BLOCKS[b][1]
                z, o = zt[:, i % 3, :], zo[:, i % 3, :]
                dve.wait_ge(s["p_ev"], i + 1)
                if i >= 3:
                    dve.wait_ge(s[f"p_out{i % 3}"], 16 * (i // 3))
                    if new_stores(i % 3, i):
                        dve.wait_ge(s[f"p_new{i % 3}"], 16 * new_stores(i % 3, i))
                if c0 <= NB:
                    heads = A_HEADS if c0 == 0 else A_KV
                    w = heads * HEAD_DIM
                    dve.wait_ge(s["p_hstd"], i - T + 1)
                    do(dve.reciprocal(hst[:, i % 2, 2, 0:heads], hst[:, i % 2, 1, 0:heads]))
                    zv = heads_view(z[:, 0:w], heads)
                    do(dve.tensor_tensor(heads_view(tm[:, 1, 0:w], heads), zv,
                                         hst[:, i % 2, 2, 0:heads].unsqueeze(2).broadcast_to([P, heads, HEAD_DIM]), ALU.mult))
                    gain = per["gains"][:, 0 if c0 == 0 else 1, :].unsqueeze(1).broadcast_to([P, heads, HEAD_DIM])
                    if t < TS:
                        do(dve.tensor_tensor(heads_view(tm[:, 2, 0:w], heads), heads_view(tm[:, 1, 0:w], heads), gain, ALU.mult))
                        last = rope(o[:, 0:w], tm[:, 2, 0:w], t, heads, 16, per["cosA"], per["sinA"], tm[:, 1, 0:w])
                    else:
                        last = dve.tensor_tensor(heads_view(o[:, 0:w], heads), heads_view(tm[:, 1, 0:w], heads), gain, ALU.mult)
                    if c0 == NB:
                        do(last)
                        do(dve.tensor_copy(o[:, P:2 * P], z[:, P:2 * P]))
                        if t < TS:
                            last = rope(o[:, 2 * P:NB], z[:, 2 * P:NB], t, 2 * B_HEADS, 8, per["cosB"], per["sinB"], tm[:, 1, 0:2 * P])
                        else:
                            last = dve.tensor_copy(o[:, 2 * P:NB], z[:, 2 * P:NB])
                else:
                    do(dve.tensor_copy(o[:, 2 * P:NB], z[:, 2 * P:NB]))
                    if t < TS:
                        last = rope(o[:, 0:2 * P], z[:, 0:2 * P], t, 2 * B_HEADS, 8, per["cosB"], per["sinB"], tm[:, 1, 0:2 * P])
                    else:
                        last = dve.tensor_copy(o[:, 0:2 * P], z[:, 0:2 * P])
                last.then_inc(s["p_zo"], 1)

            affine(0)
            lo_h(0)
            affine(1)
            lo_h(1)
            f.norm_x(dve, 2)
            for i, (b, what, j) in enumerate(uses):
                if b == 0 and j + 2 < T:
                    affine(j + 2)
                    lo_h(j + 2)
                    if j + 3 < T:
                        f.norm_x(dve, j + 3)
                if i < Z_BLOCKS * T:
                    head_sums(i)
                if 0 < i <= Z_BLOCKS * T:
                    finish_tile(i - 1)


CHUNK = 64
NC_S, NC_P = DEC_SEQ // CHUNK, SEQ // CHUNK
S_SLOTS = NC_S + 1 + NC_P + 1


def gla_block(nc, l, io, per, mid, att, s):
    CD, CV = C_HEADS * C_DK, C_HEADS * C_DV
    with ExitStack() as ctx:
        def sb(name, shape, dt=F32):
            return ctx.enter_context(nc.sbuf_tensor(name, shape, dt))

        def ps(name):
            return ctx.enter_context(nc.psum_tensor(name, [P, NB], F32))

        oa2 = mid["oa"][:, :, :].rearrange("p t c -> p (t c)").rearrange("p (x t c) -> p x t c", x=2, t=T)
        ob2 = mid["ob"][:, :, :, :].rearrange("p a t c -> p (a t c)").rearrange("p (x t c) -> p x t c", x=2, t=T)
        gate, soft = oa2[:, 0, :, :], oa2[:, 1, :, :]
        qt, oi = ob2[:, 0, :, :].rearrange("p t (d i) -> p t d i", d=2), ob2[:, 1, :, :]
        st = sb("states", [P, 2, S_SLOTS, CV])
        el = sb("exp_last", [P, T, 2, 2])
        lc = sb("last_cum", [P, 2, 2, 2])
        ex = sb("exps", [P, 2, 3, 2, P])
        kt = sb("k_scaled", [P, 2, 2, 2, P])
        qbd = sb("q_blockdiag", [P, 2, 2, C_HEADS, P])
        am = sb("a_masked", [P, 2, 2, C_HEADS, P])
        k2t = sb("k_by_token", [P, 2, 2, P])
        post = sb("post_by_row", [2 * KD, P])
        cum_ps = [ps("cum0"), ps("cum1")]
        at_ps = [ps("at0"), ps("at1")]
        tr_ps, o_ps = ps("gla_tr"), ps("gla_o")
        ds_ps = [ps("ds0"), ps("ds1")]
        block = ctx.enter_context(nc.Block())
        oc = mid["oc"]

        def slot0(t):
            return 0 if t < TS else NC_S + 1

        def step_of(d, t, c):
            n = 2 * (t if t < TS else t - TS) + c
            chunks = NC_S if t < TS else NC_P
            return n if d == 0 else chunks - 1 - n

        backward = list(range(T - 1, TS - 1, -1)) + list(range(TS - 1, -1, -1))

        @block.sync
        def _(sp):
            for u in ("A", "B"):
                load_qk(sp, s, l, io, att, u, 0)
            sp.wait_ge(s["g_zero"], 2)
            for d, name in enumerate(("state_c_fwd", "state_c_bwd")):
                for h in range(C_HEADS):
                    sp.dma_start(st[h * C_DK:(h + 1) * C_DK, d, 0, h * C_DV:(h + 1) * C_DV],
                                 io[name][bass.ds(l, 1), h, :, :].rearrange("a x y -> (a x) y")).then_inc(s["g_st0"], 16)
            sp.wait_ge(s["g_post"], 1)
            sp.dma_start(io["Gs"].rearrange("g (k p) -> (g k) p", p=P), post[:, :]).then_inc(s["g_stored"], 16)
            sp.wait_ge(s["a_ones"], 6)
            for u in ("A", "B"):
                load_v(sp, s, l, io, att, u, 0)
            sp.wait_ge(s["g_chain"], 1)
            for d, name in enumerate(("new_state_c_fwd", "new_state_c_bwd")):
                for h in range(C_HEADS):
                    sp.dma_start(io[name][bass.ds(l, 1), h, :, :].rearrange("a x y -> (a x) y"),
                                 st[h * C_DK:(h + 1) * C_DK, d, S_SLOTS - 1, h * C_DV:(h + 1) * C_DV]).then_inc(s["g_new"], 16)
            sp.wait_ge(s["g_new"], 16 * 2 * C_HEADS)

        @block.tensor
        def _(pe):
            pe.transpose(tr_ps[0:2 * KD, 0:P], per["post"][:, :, :].rearrange("p g k -> p (g k)"), per["ident"][:, :]).then_inc(s["g_postT"], 1)
            for i in range(T // 2):
                if i >= 2:
                    pe.wait_ge(s["g_min"], i - 1)
                for t in (2 * i, 2 * i + 1):
                    mm = pe.matmul(cum_ps[i % 2][:, (t % 2) * 2 * CD:(t % 2 + 1) * 2 * CD], per["lrT"][:, tile_rows(t)],
                                   per["gate_w"][:, :], start=True, stop=True)
                mm.then_inc(s["g_pre"], 1)
            pe.wait_ge(s["g_gate"], 1)

            def running_sums(t):
                if t == 2:
                    pe.wait_ge(s["g_gate"], 2)
                if t >= 2:
                    pe.wait_ge(s["g_exp"], t - 1)
                for d in range(2):
                    mm = pe.matmul(cum_ps[t % 2][:, d * P:(d + 1) * P], gate[:, t, d * CD:(d + 1) * CD], per["tri"][:, d, :],
                                   start=True, stop=True)
                mm.then_inc(s["g_cum"], 1)

            running_sums(0)
            running_sums(1)
            for t in range(T):
                b = t % 2
                pe.wait_ge(s["g_mul"], t + 1)
                if t == 0:
                    pe.wait_ge(s["g_post"], 1)
                if t:
                    pe.wait_ge(s["g_k2t"], t)
                for d in range(2):
                    mm = pe.transpose(tr_ps[:, d * P:(d + 1) * P], kt[:, b, 1, d, :], per["ident"][:, :])
                mm.then_inc(s["g_tr"], 1)
                for d in range(2):
                    if t:
                        pe.wait_ge(s["g_am"], 2 * t + d - 1)
                    if d == 0:
                        pe.wait_ge(s["g_qbd"], t + 1)
                    pe.matmul(at_ps[d][:, :], kt[:, b, 0, d, :], qbd[:, b, d, :, :].rearrange("p h i -> p (h i)"),
                              start=True, stop=True).then_inc(s["g_at"], 1)
                if t + 2 < T:
                    running_sums(t + 2)
                pe.wait_ge(s["g_k2t"], t + 1)
                if t:
                    pe.wait_ge(s["g_dsm"], t)
                for c in range(2):
                    rows = slice(c * CHUNK, (c + 1) * CHUNK)
                    for d in range(2):
                        mm = pe.matmul(ds_ps[c][:, d * CV:(d + 1) * CV], k2t[rows, b, d, :], per["cv"][rows, t, :],
                                       start=True, stop=True)
                mm.then_inc(s["g_ds"], 1)
                pe.wait_ge(s["g_am"], 2 * t + 2)
                if t:
                    pe.wait_ge(s["g_oi"], t)
                for h in range(C_HEADS):
                    cols = slice(h * C_DV, (h + 1) * C_DV)
                    for d in range(2):
                        mm = pe.matmul(o_ps[:, cols], am[:, b, d, h, :], per["cv"][:, t, cols], start=(d == 0), stop=(d == 1))
                mm.then_inc(s["g_o"], 1)
            for n, t in enumerate(backward):
                if n == 0:
                    pe.wait_ge(s["g_oi"], T)
                pe.wait_ge(s["g_bwd"], n + 1)
                if n >= 2:
                    pe.wait_ge(s["g_oc"], n - 1)
                for c in range(2):
                    for d in range(2):
                        mm = pe.matmul(cum_ps[n % 2][c * CHUNK:(c + 1) * CHUNK, 0:CV], qt[:, t, d, c * CHUNK:(c + 1) * CHUNK],
                                       st[:, d, slot0(t) + step_of(d, t, c), :], start=(d == 0), stop=(d == 1))
                mm.then_inc(s["g_inter"], 1)

        @block.gpsimd
        def _(pool):
            def blockdiag(t):
                b = t % 2
                pool.wait_ge(s["g_qt"], t + 1)
                if t >= 2:
                    pool.wait_ge(s["g_at"], 2 * t - 2)
                for d in range(2):
                    ins = pool.tensor_tensor(qbd[:, b, d, :, :], qt[:, t, d, :].unsqueeze(1).broadcast_to([P, C_HEADS, P]),
                                             per["bdmask"][:, :].unsqueeze(2).broadcast_to([P, C_HEADS, P]), ALU.mult)
                ins.then_inc(s["g_qbd"], 1)

            pool.wait_ge(s["a_ones"], 6)
            split(pool, s, per, att, "A", 0, 0)
            for t in range(T):
                blockdiag(t)
            split(pool, s, per, att, "B", 0, SPLIT_CHAIN["A"])

        @block.scalar
        def _(act):
            do = Chain(act, s["g_act"])
            act.wait_ge(s["g_postT"], 1)
            act.copy(post[:, :], tr_ps[0:2 * KD, 0:P]).then_inc(s["g_post"], 1)
            for i in range(T // 2):
                act.wait_ge(s["g_pre"], i + 1)
                act.activation(soft[:, 2 * i:2 * i + 2, :], cum_ps[i % 2][:, :].rearrange("p (t c) -> p t c", t=2),
                               ACT.Abs).then_inc(s["g_abs"], 1)
                act.wait_ge(s["g_abs"], i + 1)
                act.activation(soft[:, 2 * i:2 * i + 2, :], soft[:, 2 * i:2 * i + 2, :], ACT.Exp, scale=-1.0).then_inc(s["g_sx"], 1)
            act.wait_ge(s["g_sx"], T // 2)
            for part in (slice(0, 2), slice(2, T)):
                act.activation(soft[:, part, :], soft[:, part, :], ACT.Ln, bias=per["one"][:, :]).then_inc(s["g_ln"], 1)

            def exps(t):
                b = t % 2
                act.wait_ge(s["g_cum"], t + 1)
                if t >= 2:
                    act.wait_ge(s["g_mul"], t - 1)
                cum = cum_ps[b][:, 0:2 * P].rearrange("p (d i) -> p d i", d=2)
                act.activation(ex[:, b, 0, :, :], cum, ACT.Exp, scale=1.0 / TAU)
                act.activation(ex[:, b, 1, :, :], cum, ACT.Exp, scale=-1.0 / TAU)
                do(act.mul(lc[:, b, 0, :], cum[:, 0, CHUNK - 1::CHUNK], 1.0 / TAU))
                do(act.mul(lc[:, b, 1, :], cum[:, 1, 0::CHUNK], 1.0 / TAU))
                act.activation(el[:, t, :, :], lc[:, b, :, :], ACT.Exp)
                for d in range(2):
                    for c in range(2):
                        cols = slice(c * CHUNK, (c + 1) * CHUNK)
                        ins = act.activation(ex[:, b, 2, d, cols], cum[:, d, cols], ACT.Exp, scale=-1.0 / TAU,
                                             bias=lc[:, b, d, c:c + 1])
                ins.then_inc(s["g_exp"], 1)

            exps(0)
            for t in range(T):
                b = t % 2
                act.wait_ge(s["g_tr"], t + 1)
                if t >= 2:
                    act.wait_ge(s["g_ds"], t - 1)
                act.copy(k2t[:, b, :, :], tr_ps[:, 0:2 * P].rearrange("p (d f) -> p d f", d=2)).then_inc(s["g_k2t"], 1)
                if t + 1 < T:
                    exps(t + 1)
                act.wait_ge(s["g_o"], t + 1)
                act.copy(oi[:, t, :], o_ps[:, 0:CV]).then_inc(s["g_oi"], 1)

        @block.vector
        def _(dve):
            do = Chain(dve, s["g_dve"])
            kst, qst, qst2, v = att["kst"], att["qst"], att["qst2"], att["v"]
            ones0, ones1 = 3 * B_QK, 3 * B_QK + 2
            for ap, value in ((kst["B"][:, :, ones0:ones1].bitcast(F32), 1.0), (kst["B"][:, :, ones1:].bitcast(F32), 0.0),
                              (qst["B"][:, :, ones0:].bitcast(F32), 0.0), (qst2[:, :, HEAD_DIM:].bitcast(F32), 0.0),
                              (v["A"][:, :, HEAD_DIM:], 1.0), (v["B"][:, :, HEAD_DIM:], 1.0)):
                dve.memset(ap, value).then_inc(s["a_ones"], 1)
            dve.memset(st[:, :, 0, :], 0.0).then_inc(s["g_zero"], 1)
            dve.memset(st[:, :, NC_S + 1, :], 0.0).then_inc(s["g_zero"], 1)
            for i in range(T // 2):
                dve.wait_ge(s["g_abs"], i + 1)
                dve.tensor_scalar(gate[:, 2 * i:2 * i + 2, :], cum_ps[i % 2][:, :].rearrange("p (t c) -> p t c", t=2),
                                  0.0, None, ALU.min).then_inc(s["g_min"], 1)
            dve.wait_ge(s["g_min"], T // 2)
            for i, part in enumerate((slice(0, 2), slice(2, T))):
                dve.wait_ge(s["g_ln"], i + 1)
                dve.tensor_tensor(gate[:, part, :], gate[:, part, :], soft[:, part, :], ALU.subtract).then_inc(s["g_gate"], 1)

            def both(ap):
                return ap.unsqueeze(1).broadcast_to([P, 2, P])

            def scale_qk(t):
                b = t % 2
                dve.wait_ge(s["g_exp"], t + 1)
                if t >= 2:
                    dve.wait_ge(s["g_at"], 2 * t - 2)
                q, k = both(per["cqT"][:, tile_rows(t)]), both(per["ckT"][:, tile_rows(t)])
                dve.scalar_tensor_tensor(out=qt[:, t, :, :], in0=q, scalar=float(C_DK) ** -0.5, in1=ex[:, b, 0, :, :],
                                         op0=ALU.mult, op1=ALU.mult).then_inc(s["g_qt"], 1)
                dve.tensor_tensor(kt[:, b, 0, :, :], k, ex[:, b, 1, :, :], ALU.mult)
                dve.tensor_tensor(kt[:, b, 1, :, :], k, ex[:, b, 2, :, :], ALU.mult).then_inc(s["g_mul"], 1)

            def advance(d, t, c):
                n = slot0(t) + step_of(d, t, c)
                do(dve.scalar_tensor_tensor(out=st[:, d, n + 1, :], in0=st[:, d, n, :], scalar=el[:, t, d, c:c + 1],
                                            in1=st[:, d, n + 1, :], op0=ALU.mult, op1=ALU.add))

            scale_qk(0)
            for t in range(T):
                b = t % 2
                for d in range(2):
                    dve.wait_ge(s["g_at"], 2 * t + d + 1)
                    if t >= 2:
                        dve.wait_ge(s["g_o"], t - 1)
                    dve.tensor_tensor(am[:, b, d, :, :], at_ps[d][:, :].rearrange("p (h i) -> p h i", h=C_HEADS),
                                      per["tri"][:, d, :].unsqueeze(1).broadcast_to([P, C_HEADS, P]),
                                      ALU.mult).then_inc(s["g_am"], 1)
                if t + 1 < T:
                    scale_qk(t + 1)
                dve.wait_ge(s["g_ds"], t + 1)
                for c in range(2):
                    for d in range(2):
                        dst = st[:, d, slot0(t) + step_of(d, t, c) + 1, :].rearrange("p (h e) -> p h e", h=C_HEADS)
                        ins = dve.tensor_tensor(dst, ds_ps[c][:, d * CV:(d + 1) * CV].rearrange("p (h e) -> p h e", h=C_HEADS),
                                                per["bdmask"][:, :].unsqueeze(2).broadcast_to([P, C_HEADS, C_DV]), ALU.mult)
                ins.then_inc(s["g_dsm"], 1)
                dve.wait_ge(s["g_dsm"], t + 1)
                if t == 0:
                    dve.wait_ge(s["g_st0"], 16 * 2 * C_HEADS)
                for c in range(2):
                    advance(0, t, c)

            def join(n):
                t = backward[n]
                dve.wait_ge(s["g_inter"], n + 1)
                dve.tensor_tensor(oc[:, t, :], cum_ps[n % 2][:, 0:CV], oi[:, t, :], ALU.add).then_inc(s["g_oc"], 1)

            dve.wait_ge(s["g_oi"], T)
            for n, t in enumerate(backward):
                advance(1, t, 1)
                advance(1, t, 0)
                dve.sem_inc(s["g_bwd"], 1)
                if n == TP - 1:
                    dve.sem_inc(s["g_chain"], 1)
                if n >= 2:
                    join(n - 2)
            join(T - 2)
            join(T - 1)


KT = (PAST + DEC_SEQ + SEQ) // P
KT_S = (PAST + DEC_SEQ) // P
KEYS = KT * P
ATT_STEPS = KT_S + 1
PREP = 30
PREP_AT = (3, 3, 4, 4, 4, 3, 3, 3, 3, 0, 0)
PREP_Q, PREP_MAX, PREP_LAST = 3, 6, 27
HALF = 5


QK_W = {"A": HEAD_DIM, "B": B_QK}
SPLIT_CHAIN = {"A": 4, "B": 5}


def attention_front(nc, ctx):
    def sb(name, shape, dt=F32):
        return ctx.enter_context(nc.sbuf_tensor(name, shape, dt))

    return {
        "kraw": {u: sb(f"k_raw{u}", [P, KT, QK_W[u]]) for u in "AB"},
        "qraw": {u: sb(f"q_raw{u}", [P, T, QK_W[u]]) for u in "AB"},
        "v": {u: sb(f"v{u}", [P, KT, HEAD_DIM + 1]) for u in "AB"},
        "kst": {u: sb(f"k_stack{u}", [P, KT, P], F32R) for u in "AB"},
        "qst": {u: sb(f"q_stack{u}", [P, T, P], F32R) for u in "AB"},
        "qst2": sb("q_stackA2", [P, T, P], F32R)}


def load_part(sp, s, l, io, u, dst, h, what, sem):
    w = HEAD_DIM if what == "v" else QK_W[u]
    if u == "A":
        kv = h // (A_HEADS // A_KV)
        c = {"q": h * HEAD_DIM, "k": A_HEADS * HEAD_DIM + kv * HEAD_DIM,
             "v": (A_HEADS + A_KV) * HEAD_DIM + kv * HEAD_DIM}[what]
    else:
        base, nb = (A_HEADS + 2 * A_KV) * HEAD_DIM, B_HEADS * 2 * B_QK
        c = {"q": base + h * B_QK, "k": base + nb + h * B_QK, "v": base + 2 * nb + (h // 2) * B_V}[what]
    src = io["Zs"][:, bass.ds(c, w)].rearrange("(t p) d -> p t d", p=P)
    first = 0 if what == "q" else PAST // P
    sp.dma_start(dst[:, first:, 0:w], src).then_inc(s[sem], 16)
    if what != "q":
        cache = io[f"cache_{u.lower()}_{what}"]
        head = h // (A_HEADS // A_KV) if u == "A" else h // 2
        c0 = (h % 2) * B_QK if (u == "B" and what == "k") else 0
        src = cache[bass.ds(l, 1), bass.ds(head, 1), :, bass.ds(c0, w)].rearrange("a b (t p) d -> p (a b t) d", p=P)
        sp.dma_start(dst[:, 0:first, 0:w], src).then_inc(s[sem], 16)


def load_qk(sp, s, l, io, att, u, h):
    load_part(sp, s, l, io, u, att["kraw"][u], h, "k", f"a_raw{u}")
    load_part(sp, s, l, io, u, att["qraw"][u], h, "q", f"a_raw{u}")


def load_v(sp, s, l, io, att, u, h):
    load_part(sp, s, l, io, u, att["v"][u], h, "v", f"a_v{u}")


def split(pool, s, per, att, u, h, chain0):
    n = [0]

    def do(ins):
        n[0] += 1
        ins.then_inc(s["a_pool"], 1)
        pool.wait_ge(s["a_pool"], chain0 + n[0])

    def copy(dst, src):
        one = per["one"][:, :].unsqueeze(2).broadcast_to(list(src.shape))
        return pool.tensor_tensor(dst, src, one, ALU.mult)

    w = QK_W[u]
    k, q, ks, qs = att["kraw"][u][:, :, :], att["qraw"][u][:, :, :], att["kst"][u], att["qst"][u]
    pool.wait_ge(s[f"a_raw{u}"], 48 * (h + 1))
    do(copy(ks[:, :, 0:w], k))
    do(copy(qs[:, :, 0:w], q))
    if u == "A":
        do(pool.tensor_tensor(ks[:, :, w:2 * w], k, ks[:, :, 0:w].bitcast(F32), ALU.subtract))
        do(copy(qs[:, :, w:2 * w], qs[:, :, 0:w].bitcast(F32)))
        ins = pool.tensor_tensor(att["qst2"][:, :, 0:w], q, qs[:, :, 0:w].bitcast(F32), ALU.subtract)
    else:
        do(pool.tensor_tensor(ks[:, :, 2 * w:3 * w], k, ks[:, :, 0:w].bitcast(F32), ALU.subtract))
        do(copy(ks[:, :, w:2 * w], ks[:, :, 0:w].bitcast(F32)))
        do(copy(qs[:, :, 2 * w:3 * w], qs[:, :, 0:w].bitcast(F32)))
        ins = pool.tensor_tensor(qs[:, :, w:2 * w], q, qs[:, :, 0:w].bitcast(F32), ALU.subtract)
    ins.then_inc(s[f"a_split{u}"], 1)


def attention_block(nc, l, io, per, mid, att, s):
    A, B = "A", "B"
    W = {A: HEAD_DIM, B: B_QK}
    KR = {A: P, B: 3 * B_QK + 2}
    SCALE = {A: float(HEAD_DIM) ** -0.5, B: float(B_QK) ** -0.5}
    with ExitStack() as ctx:
        def sb(name, shape, dt=F32):
            return ctx.enter_context(nc.sbuf_tensor(name, shape, dt))

        v, kst, qst, qst2 = att["v"], att["kst"], att["qst"], att["qst2"]
        kT = {u: sb(f"kT{u}", [P, KEYS], F32R) for u in (A, B)}
        kT2 = sb("kTA2", [P, KEYS], F32R)
        qT = {u: sb(f"qT{u}", [P, TOK], F32R) for u in (A, B)}
        qT2 = {u: sb(f"qT2{u}", [P, TOK], F32R) for u in (A, B)}
        pr = sb("probs", [P, 2, DEC_SEQ])
        nmx = sb("neg_max_parts", [P, T, 3])
        nm = sb("neg_max", [P, T])
        rs = sb("recip_sums", [P, 2, HALF])
        csq = sb("c_squares", [P, T, C_HEADS * C_DV])
        stats = sb("c_stats", [P, 3, T, C_HEADS])
        sc = [ctx.enter_context(nc.psum_tensor(f"scores{i}", [P, 2, NB], F32)) for i in range(2)]
        ob = ctx.enter_context(nc.psum_tensor("att_out", [P, 2, NB], F32))
        wk = [ctx.enter_context(nc.psum_tensor(f"work{i}", [P, NB], F32)) for i in range(2)]
        block = ctx.enter_context(nc.Block())
        m_cols = {A: qst2[:, :, HEAD_DIM:HEAD_DIM + 2], B: qst[B][:, :, 3 * B_QK:KR[B]]}
        TURNS = A_HEADS

        def step0(u, h):
            return h * 2 * ATT_STEPS + (0 if u == A else ATT_STEPS)

        def unit(u, h):
            return 2 * h + (0 if u == A else 1)

        @block.sync
        def _(sp):
            su, wst = output_front(per)
            for t in range(2):
                load_su(sp, s, io, su, t)
            for k in range(2):
                load_wo(sp, s, l, io, wst, k)
            with sp.Fori(0, TURNS - 1) as h:
                for u in (A, B):
                    sp.wait_ge(s[f"a_split{u}"], h + 1)
                    load_qk(sp, s, l, io, att, u, h + 1)
                    sp.wait_ge(s["a_pv"], step0(u, h) + ATT_STEPS)
                    load_v(sp, s, l, io, att, u, h + 1)

        @block.gpsimd
        def _(pool):
            nA, nB = SPLIT_CHAIN[A], SPLIT_CHAIN[B]
            with pool.Fori(0, TURNS - 1) as h:
                pool.wait_ge(s["a_work"], PREP * (unit(A, h) + 1))
                split(pool, s, per, att, A, h + 1, (h + 1) * (nA + nB))
                pool.wait_ge(s["a_work"], PREP * (unit(B, h) + 1))
                split(pool, s, per, att, B, h + 1, (h + 1) * (nA + nB) + nA)

        @block.tensor
        def _(pe):
            def prep(u, h, i):
                p = unit(u, h)
                bank = wk[i % 2]
                first_unit = isinstance(h, int) and h == 0 and u == A
                if i < 2:
                    if not first_unit:
                        pe.wait_ge(s["a_wkdve"], (PREP - PREP_MAX) * p - 1 + i)
                elif i < PREP_MAX:
                    pe.wait_ge(s["a_wkact"], PREP_MAX * p + i - 1)
                elif i < PREP_MAX + 2:
                    pe.wait_ge(s["a_wkact"], PREP_MAX * p + PREP_MAX)
                else:
                    pe.wait_ge(s["a_wkdve"], (PREP - PREP_MAX) * p + i - 1 - PREP_MAX)
                if i == 0:
                    pe.wait_ge(s[f"a_split{u}"], h + 1)
                if i == PREP_LAST:
                    pe.wait_ge(s["a_nm"], p + 1)
                if i < PREP_Q:
                    for j in range(4):
                        mm = pe.matmul(bank[:, j * P:(j + 1) * P], kst[u][:, 4 * i + j, :], per["ident_r"][:, :],
                                       start=True, stop=True)
                elif i < PREP_MAX or i >= PREP_LAST:
                    g = i - (PREP_Q if i < PREP_MAX else PREP_LAST)
                    src = qst2 if u == A and i >= PREP_LAST else qst[u]
                    for t in range(4 * g, min(4 * g + 4, T)):
                        mm = pe.matmul(bank[:, (t - 4 * g) * P:(t - 4 * g + 1) * P], src[:, t, :], per["ident_r"][:, :],
                                       start=True, stop=True)
                else:
                    m, rows = i - PREP_MAX, P if u == A else 3 * B_QK
                    if m < 2 * TS:
                        parts = [(m // 2, (m % 2) * NB, NB)]
                    else:
                        q0 = 2 * (m - 2 * TS)
                        keys0 = 2 * NB if q0 < TS else KT_S * P
                        parts = [(q0, keys0, SEQ), (q0 + 1, keys0, SEQ)]
                    for x, (t, k0, n) in enumerate(parts):
                        mm = pe.matmul(bank[:, x * SEQ:x * SEQ + n], qT[u][0:rows, tile_rows(t)], kT[u][0:rows, k0:k0 + n],
                                       start=True, stop=True)
                mm.then_inc(s["a_work"], 1)

            def scores(u, h, j):
                n = step0(u, h) + j
                if not (isinstance(h, int) and h == 0 and u == A and j < 2):
                    pe.wait_ge(s["a_exp"], n - 1)
                if j == 0:
                    pe.wait_ge(s["a_wkdve"], (PREP - PREP_MAX) * (unit(u, h) + 1))
                slot = sc[(j + (0 if u == A else ATT_STEPS)) % 2]
                for c in range(2):
                    if j < KT_S:
                        keys, q, out = tile_rows(j), slice(c * NB, (c + 1) * NB), slot[:, c, :]
                    else:
                        keys, q, out = tile_rows(KT_S + c), slice(DEC_SEQ, TOK), slot[:, c, 0:SEQ]
                    if u == A:
                        pe.matmul(out, kT[u][:, keys], qT[u][:, q], start=True, stop=False)
                        mm = pe.matmul(out, kT2[:, keys], qT2[u][:, q], start=False, stop=True)
                    else:
                        mm = pe.matmul(out, kT[u][:, keys], qT2[u][:, q], start=True, stop=True)
                mm.then_inc(s["a_scores"], 1)

            def weigh(u, h, j, part):
                n = step0(u, h) + j
                pb = pr[:, (j + (0 if u == A else ATT_STEPS)) % 2, :]
                if part == 0:
                    pe.wait_ge(s["a_exp"], n + 1)
                    if j == 0:
                        pe.wait_ge(s[f"a_v{u}"], 32 * (h + 1))
                        pe.wait_ge(s["a_out"], unit(u, h) + 1)
                if j < KT_S:
                    work = [(t, pb[:, tile_rows(t)], j) for t in range(part * 4, part * 4 + 4)]
                else:
                    t = TS + part
                    work = [(t, pb[:, c * NB + part * P:c * NB + (part + 1) * P], KT_S + c) for c in range(2)]
                for t, probs, key in work:
                    o = ob[:, t // HALF, (t % HALF) * (HEAD_DIM + 1):(t % HALF + 1) * (HEAD_DIM + 1)]
                    mm = pe.matmul(o, probs, v[u][:, key, :], start=(j == 0 and t % HALF == 0),
                                   stop=(j == KT_S - 1 or (j == KT_S and key == KT - 1)), skip_group_check=True)
                if part == 1:
                    mm.then_inc(s["a_pv"], 1)

            def run_unit(u, h, nxt):
                def prep_uses(first, n):
                    for i in range(first, first + n):
                        prep(*nxt, i)

                def scores_ahead(j):
                    if j + 2 < ATT_STEPS:
                        scores(u, h, j + 2)
                    elif nxt:
                        scores(*nxt, j + 2 - ATT_STEPS)

                done = 0
                for j in range(ATT_STEPS):
                    n = PREP_AT[j] if nxt else 0
                    if j == 0:
                        prep_uses(done, min(n, 2))
                        scores_ahead(j)
                        weigh(u, h, j, 0)
                        prep_uses(done + 2, n - 2)
                        weigh(u, h, j, 1)
                    elif done < PREP_LAST:
                        prep_uses(done, (n + 1) // 2)
                        weigh(u, h, j, 0)
                        prep_uses(done + (n + 1) // 2, n // 2)
                        weigh(u, h, j, 1)
                        scores_ahead(j)
                    else:
                        weigh(u, h, j, 0)
                        prep_uses(done, (n + 1) // 2)
                        weigh(u, h, j, 1)
                        prep_uses(done + (n + 1) // 2, n // 2)
                        scores_ahead(j)
                    done += n

            for i in range(PREP_MAX):
                prep(A, 0, i)
            pe.wait_ge(s["a_wkact"], PREP_MAX)
            for t in range(TS):
                if t >= 2:
                    pe.wait_ge(s["a_wkdve"], 2 * (t - 1))
                for c in range(2):
                    mm = pe.matmul(sc[t % 2][:, c, :], qT[A][:, tile_rows(t)], kT[A][:, c * NB:(c + 1) * NB],
                                   start=True, stop=True)
                mm.then_inc(s["a_work"], 2)
            for i in range(PREP_MAX + 2 * TS, PREP):
                prep(A, 0, i)
            scores(A, 0, 0)
            scores(A, 0, 1)
            with pe.Fori(0, TURNS - 1) as h:
                run_unit(A, h, (B, h))
                run_unit(B, h, (A, h + 1))
            run_unit(A, TURNS - 1, (B, TURNS - 1))
            run_unit(B, TURNS - 1, None)

        @block.scalar
        def _(act):
            def stand(u, h, i):
                p = unit(u, h)
                act.wait_ge(s["a_work"], PREP * p + i + 1)
                bank = wk[i % 2]
                if i < PREP_Q:
                    cols = slice(i * NB, (i + 1) * NB)
                    ins = act.copy(kT[u][:, cols], bank[:, :])
                    if u == A:
                        ins = act.copy(kT2[0:HEAD_DIM, cols], bank[0:HEAD_DIM, :])
                else:
                    cols = slice((i - PREP_Q) * NB, min((i - PREP_Q + 1) * NB, TOK))
                    ins = act.copy(qT[u][:, cols], bank[:, 0:cols.stop - cols.start])
                ins.then_inc(s["a_wkact"], 1)

            def exps(u, h, j):
                n = step0(u, h) + j
                b = (j + (0 if u == A else ATT_STEPS)) % 2
                act.wait_ge(s["a_scores"], n + 1)
                if j == 2:
                    act.wait_ge(s["a_pv"], n - 1)
                if j < KT_S:
                    act.activation(pr[:, b, :], sc[b][:, :, :].rearrange("p c n -> p (c n)"), ACT.Exp,
                                   scale=SCALE[u]).then_inc(s["a_exp"], 1)
                else:
                    act.activation(pr[:, b, :].rearrange("p (c n) -> p c n", c=2)[:, :, 0:SEQ], sc[b][:, :, 0:SEQ], ACT.Exp,
                                   scale=SCALE[u]).then_inc(s["a_exp"], 1)

            def run_unit(u, h, nxt):
                for j in range(ATT_STEPS):
                    exps(u, h, j)
                    if nxt and j < 2:
                        for i in range(3 * j, 3 * j + 3):
                            stand(*nxt, i)
                    if not nxt and j == ATT_STEPS // 2:
                        act.wait_ge(s["g_css"], 1)
                        act.activation(stats[:, 1, :, :], stats[:, 0, :, :], ACT.Sqrt, bias=per["eps"][:, :],
                                       scale=1.0 / C_DV).then_inc(s["g_cstd"], 1)

            for i in range(PREP_MAX):
                stand(A, 0, i)
            with act.Fori(0, TURNS - 1) as h:
                run_unit(A, h, (B, h))
                run_unit(B, h, (A, h + 1))
            run_unit(A, TURNS - 1, (B, TURNS - 1))
            run_unit(B, TURNS - 1, None)

        @block.vector
        def _(dve):
            def own(u, h, n):
                return 2 * unit(u, h) + n

            def maxima(u, h):
                p = unit(u, h)
                first = isinstance(h, int) and h == 0 and u == A
                for t in range(TS if first else 0):
                    dve.wait_ge(s["a_work"], PREP_MAX + 2 * (t + 1))
                    dve.tensor_reduce(nmx[:, t, 0:2], sc[t % 2][:, :, :], AX_X, ALU.max, negate=True).then_inc(s["a_wkdve"], 2)
                for i in range(PREP_MAX + (2 * TS if first else 0), PREP_LAST):
                    m = i - PREP_MAX
                    dve.wait_ge(s["a_work"], PREP * p + i + 1)
                    if m < 2 * TS:
                        dst, src = nmx[:, m // 2, m % 2:m % 2 + 1], wk[i % 2][:, :]
                    else:
                        q0 = 2 * (m - 2 * TS)
                        dst = nmx[:, q0:q0 + 2, 2] if q0 < TS else nm[:, TS:T]
                        src = wk[i % 2][:, :].rearrange("p (t n) -> p t n", t=2)
                    dve.tensor_reduce(dst, src, AX_X, ALU.max, negate=True).then_inc(s["a_wkdve"], 1)
                dve.wait_ge(s["a_wkdve"], (PREP - PREP_MAX) * p + PREP_LAST - PREP_MAX)
                dve.tensor_reduce(nm[:, 0:TS], nmx[:, 0:TS, :], AX_X, ALU.min).then_inc(s["a_own"], 1)
                dve.wait_ge(s["a_own"], own(u, h, 1))
                mc = m_cols[u]
                dve.tensor_copy(mc[:, :, 0], nm[:, :]).then_inc(s["a_own"], 1)
                dve.wait_ge(s["a_own"], own(u, h, 2))
                dve.tensor_tensor(mc[:, :, 1], nm[:, :], mc[:, :, 0].bitcast(F32), ALU.subtract).then_inc(s["a_nm"], 1)
                for i in range(PREP_LAST, PREP):
                    cols = slice((i - PREP_LAST) * NB, min((i - PREP_LAST + 1) * NB, TOK))
                    dve.wait_ge(s["a_work"], PREP * p + i + 1)
                    dve.tensor_copy(qT2[u][:, cols], wk[i % 2][:, 0:cols.stop - cols.start]).then_inc(s["a_wkdve"], 1)

            def output(u, h):
                p = unit(u, h)
                o = ob[:, :, 0:HALF * (HEAD_DIM + 1)].rearrange("p b (t e) -> p b t e", e=HEAD_DIM + 1)
                dve.wait_ge(s["a_pv"], step0(u, h) + ATT_STEPS)
                dve.reciprocal(rs[:, :, :], o[:, :, :, HEAD_DIM]).then_inc(s["a_rs"], 1)
                dve.wait_ge(s["a_rs"], p + 1)
                if u == A:
                    dst = mid["oa"][:, :, bass.ds(h * HEAD_DIM, HEAD_DIM)].rearrange("p (b t) e -> p b t e", b=2)
                else:
                    dst = mid["ob"][:, bass.ds(h, 1), :, :].rearrange("p a (b t) e -> p (a b) t e", b=2)
                r = rs[:, :, :].unsqueeze(3).broadcast_to([P, 2, HALF, HEAD_DIM])
                dve.tensor_tensor(dst, o[:, :, :, 0:HEAD_DIM], r, ALU.mult).then_inc(s["a_out"], 1)

            def gla_norm():
                do = Chain(dve, s["g_norm"])
                oc = mid["oc"]
                do(dve.tensor_tensor(csq[:, :, :], oc[:, :, :], oc[:, :, :], ALU.mult))
                dve.tensor_reduce(stats[:, 0, :, :], csq[:, :, :].rearrange("p t (h e) -> p t h e", h=C_HEADS), AX_X,
                                  ALU.add).then_inc(s["g_css"], 1)
                dve.wait_ge(s["g_cstd"], 1)
                do(dve.reciprocal(stats[:, 2, :, :], stats[:, 1, :, :]))
                o4 = oc[:, :, :].rearrange("p t (h e) -> p (t h) e", h=C_HEADS)
                r3 = stats[:, 2, :, :].rearrange("p t h -> p (t h)").unsqueeze(2).broadcast_to([P, T * C_HEADS, C_DV])
                do(dve.tensor_tensor(o4, o4, r3, ALU.mult))
                do(dve.tensor_tensor(o4, o4, per["gains"][:, 3, :].unsqueeze(1).broadcast_to([P, T * C_HEADS, C_DV]), ALU.mult))

            dve.memset(kT2[HEAD_DIM:, :].bitcast(F32), 0.0).then_inc(s["a_out"], 1)
            dve.wait_ge(s["a_out"], 1)
            dve.memset(kT2[HEAD_DIM:HEAD_DIM + 2, :].bitcast(F32), 1.0)
            maxima(A, 0)
            with dve.Fori(0, TURNS - 1) as h:
                maxima(B, h)
                output(A, h)
                maxima(A, h + 1)
                output(B, h)
            maxima(B, TURNS - 1)
            output(A, TURNS - 1)
            gla_norm()
            output(B, TURNS - 1)


def output_front(per):
    su = per["cv"][:, :, :].rearrange("p t c -> p (t c)")[:, 0:2 * D_MODEL].rearrange("p (b c) -> p b c", b=2)
    return su, [per["cqT"], per["ckT"]]


def load_su(sp, s, io, su, t):
    sp.dma_start(su[:, t % 2, :], io["Us"][tile_rows(t), :]).then_inc(s[f"o_su{t % 2}"], 16)


def load_wo(sp, s, l, io, wst, k):
    sp.dma_start(wst[k % 4][:, 0:D_MODEL], io["w_out"][bass.ds(l, 1), k * P:(k + 1) * P, :].rearrange("a p n -> (a p) n")
                 ).then_inc(s[f"o_w{k % 4}"], 16)


def output_block(nc, l, io, per, mid, s):
    BV = B_HEADS * B_V
    AW = A_HEADS * HEAD_DIM
    with ExitStack() as ctx:
        def sb(name, shape, dt=F32):
            return ctx.enter_context(nc.sbuf_tensor(name, shape, dt))

        w_hi = sb("wo_hi", [P, KD, D_MODEL], F32R)
        w_lo = sb("wo_lo", [P, KD, D_MODEL], F32R)
        gp = sb("post_rows", [P, 2, D_MODEL])
        su, wst = output_front(per)
        wst += [sb(f"wo_stage{i}", [P, D_MODEL]) for i in (2, 3)]
        xt = sb("xo_tiles", [P, 2, D_MODEL])
        yt = sb("y_tiles", [P, 2, D_MODEL])
        mx = sb("mixed", [P, D_MODEL])
        bo = sb("b_out", [P, 2, B_HEADS, B_V])
        bsq = sb("b_sq", [P, B_HEADS, B_V])
        bst = sb("b_stats", [P, 2, 3, B_HEADS])
        yst = sb("y_stats", [P, 3, T])
        m_hi = sb("mT_hi", [P, 2, KD, P], F32R)
        m_lo = sb("mT_lo", [P, 2, KD, P], F32R)
        tp = [ctx.enter_context(nc.psum_tensor(f"m_tr{i}", [P, KD, P], F32)) for i in range(2)]
        yp = [ctx.enter_context(nc.psum_tensor(f"y_acc{i}", [P, D_MODEL], F32)) for i in range(2)]
        block = ctx.enter_context(nc.Block())

        def group(t):
            return 0 if t < TS else 1

        BY_VECTOR = (2, 5)

        def wait_lo(eng, k):
            if k in BY_VECTOR:
                eng.wait_ge(s["o_wlo_dve"], BY_VECTOR.index(k) + 1)
            else:
                eng.wait_ge(s["o_wlo"], len([j for j in range(k + 1) if j not in BY_VECTOR]))

        def lo_part(eng, k):
            eng.wait_ge(s["o_whi"], k + 1)
            eng.tensor_tensor(w_lo[:, k, :], wst[k % 4][:, 0:D_MODEL], w_hi[:, k, :].bitcast(F32),
                              ALU.subtract).then_inc(s["o_wlo_dve" if k in BY_VECTOR else "o_wlo"], 1)

        @block.sync
        def _(sp):
            def next_su(t):
                sp.wait_ge(s["o_mix"], t - 1)
                load_su(sp, s, io, su, t)

            def load_x(t):
                if t >= 2:
                    sp.wait_ge(s["o_y"], t - 1)
                new, old, r = ((io["y_sample"], io["x_sample"], t * P) if t < TS
                               else (io["y_prompt"], io["x_prompt"], (t - TS) * P))
                with sp.If(l < 1):
                    sp.dma_start(xt[:, t % 2, :], old[r:r + P, :]).then_inc(s[f"o_x{t % 2}"], 16)
                with sp.Else():
                    sp.dma_start(xt[:, t % 2, :], new[r:r + P, :]).then_inc(s[f"o_x{t % 2}"], 16)

            def store(t):
                dst, r = (io["y_sample"], t * P) if t < TS else (io["y_prompt"], (t - TS) * P)
                sp.wait_ge(s["o_y"], t + 1)
                sp.dma_start(dst[r:r + P, :], yt[:, t % 2, :]).then_inc(s[f"o_st{t % 2}"], 16)

            for k in range(2, KD):
                if k >= 4:
                    wait_lo(sp, k - 4)
                load_wo(sp, s, l, io, wst, k)
                if k == 3:
                    load_x(0)
                    load_x(1)
            sp.wait_ge(s["g_stored"], 16)
            for g in range(2):
                sp.dma_start(gp[:, g, :], io["Gs"][g:g + 1, :].broadcast_to([P, D_MODEL])).then_inc(s["o_gp"], 16)
            next_su(2)
            for t in range(T):
                if t + 3 < T:
                    next_su(t + 3)
                if t + 2 < T:
                    load_x(t + 2)
                store(t)
            for i in range(2):
                sp.wait_ge(s[f"o_st{i}"], 16 * T // 2)

        @block.tensor
        def _(pe):
            def turn(t):
                pe.wait_ge(s["o_mix"], t + 1)
                if t >= 2:
                    pe.wait_ge(s["o_mlo"], t - 1)
                for k in range(KD):
                    mm = pe.transpose(tp[t % 2][:, k, :], mx[:, k * P:(k + 1) * P], per["ident"][:, :])
                mm.then_inc(s["o_turned"], 1)

            turn(0)
            for t in range(T):
                pe.wait_ge(s["o_mlo"], t + 1)
                if t >= 2:
                    pe.wait_ge(s["o_y1"], t - 1)
                for c in range(2):
                    cols = slice(c * NB, (c + 1) * NB)
                    for k in range(KD):
                        if t == 0 and c == 0:
                            wait_lo(pe, k)
                        for q, (mm_, ww) in enumerate(((m_hi, w_hi), (m_hi, w_lo), (m_lo, w_hi))):
                            mm = pe.matmul(yp[t % 2][:, cols], mm_[:, t % 2, k, :], ww[:, k, cols],
                                           start=(k == 0 and q == 0), stop=(k == KD - 1 and q == 2))
                    if t == 0 and c == 0:
                        turn(1)
                mm.then_inc(s["o_acc"], 1)
                if t + 2 < T:
                    turn(t + 2)

        @block.scalar
        def _(act):
            def b_std(t):
                act.wait_ge(s["o_bss"], t + 1)
                act.activation(bst[:, t % 2, 1, :], bst[:, t % 2, 0, :], ACT.Sqrt, bias=per["eps"][:, :],
                               scale=1.0 / B_V).then_inc(s["o_bstd"], 1)

            def hi(t):
                act.wait_ge(s["o_turned"], t + 1)
                if t >= 2:
                    act.wait_ge(s["o_acc"], t - 1)
                act.copy(m_hi[:, t % 2, :, :], tp[t % 2][:, :, :]).then_inc(s["o_mhi"], 1)

            def w_split(k):
                act.wait_ge(s[f"o_w{k % 4}"], 16 * (k // 4 + 1))
                act.copy(w_hi[:, k, :], wst[k % 4][:, 0:D_MODEL]).then_inc(s["o_whi"], 1)

            w_split(0)
            b_std(0)
            w_split(1)
            b_std(1)
            w_split(2)
            w_split(3)
            hi(0)
            w_split(4)
            b_std(2)
            for k in range(5, KD):
                w_split(k)
            hi(1)
            for t in range(T):
                if t + 3 < T:
                    b_std(t + 3)
                act.wait_ge(s["o_acc"], t + 1)
                if t >= 2:
                    act.wait_ge(s[f"o_st{t % 2}"], 16 * (t // 2))
                act.activation(yt[:, t % 2, :], yp[t % 2][:, :], ACT.Square, accum_out=yst[:, 0, t:t + 1]).then_inc(s["o_sq"], 1)
                act.wait_ge(s["o_sq"], t + 1)
                act.activation(yst[:, 1, t:t + 1], yst[:, 0, t:t + 1], ACT.Sqrt, bias=per["eps"][:, :],
                               scale=1.0 / D_MODEL).then_inc(s["o_std"], 1)
                if t + 2 < T:
                    hi(t + 2)

        @block.gpsimd
        def _(pool):
            for k in range(KD):
                if k not in BY_VECTOR:
                    lo_part(pool, k)

        @block.vector
        def _(dve):
            do = Chain(dve, s["o_dve"])
            def b_diff(t):
                o = mid["ob"]
                if t >= 2:
                    dve.wait_ge(s["o_mix"], t - 1)
                do(dve.scalar_tensor_tensor(out=bo[:, t % 2, :, :], in0=o[:, 1::2, t, :], scalar=per["neg_lam"][:, 0:1],
                                            in1=o[:, 0::2, t, :], op0=ALU.mult, op1=ALU.add))
                do(dve.tensor_tensor(bsq[:, :, :], bo[:, t % 2, :, :], bo[:, t % 2, :, :], ALU.mult))
                dve.tensor_reduce(bst[:, t % 2, 0, :], bsq[:, :, :], AX_X, ALU.add).then_inc(s["o_bss"], 1)

            def mix(t):
                b = t % 2
                dve.wait_ge(s["o_bstd"], t + 1)
                do(dve.reciprocal(bst[:, b, 2, :], bst[:, b, 1, :]))
                do(dve.tensor_tensor(bo[:, b, :, :], bo[:, b, :, :], bst[:, b, 2, :].unsqueeze(2).broadcast_to([P, B_HEADS, B_V]), ALU.mult))
                do(dve.tensor_tensor(bo[:, b, :, :], bo[:, b, :, :],
                                     per["gains"][:, 2, :].unsqueeze(1).broadcast_to([P, B_HEADS, B_V]), ALU.mult))
                dve.wait_ge(s[f"o_su{b}"], 16 * (t // 2 + 1))
                if t:
                    dve.wait_ge(s["o_turned"], t)
                dve.tensor_tensor(mx[:, 0:AW], mid["oa"][:, t, :], su[:, b, 0:AW], ALU.mult)
                dve.tensor_tensor(mx[:, AW:AW + BV], bo[:, b, :, :].rearrange("p h e -> p (h e)"), su[:, b, AW:AW + BV], ALU.mult)
                dve.tensor_tensor(mx[:, AW + BV:], mid["oc"][:, t, :], su[:, b, AW + BV:], ALU.mult).then_inc(s["o_mix"], 1)

            def lo(t):
                dve.wait_ge(s["o_mhi"], t + 1)
                dve.tensor_tensor(m_lo[:, t % 2, :, :], tp[t % 2][:, :, :], m_hi[:, t % 2, :, :].bitcast(F32),
                                  ALU.subtract).then_inc(s["o_mlo"], 1)

            def finish(t):
                b, g = t % 2, group(t)
                dve.wait_ge(s["o_std"], t + 1)
                do(dve.reciprocal(yst[:, 2, t:t + 1], yst[:, 1, t:t + 1]))
                dve.wait_ge(s["o_gp"], 16 * 2)
                dve.scalar_tensor_tensor(out=yt[:, b, :], in0=yp[b][:, :], scalar=yst[:, 2, t:t + 1], in1=gp[:, g, :],
                                         op0=ALU.mult, op1=ALU.mult).then_inc(s["o_y1"], 1)
                dve.wait_ge(s["o_y1"], t + 1)
                dve.wait_ge(s[f"o_x{b}"], 16 * (t // 2 + 1))
                dve.tensor_tensor(yt[:, b, :], yt[:, b, :], xt[:, b, :], ALU.add).then_inc(s["o_y"], 1)

            b_diff(0)
            b_diff(1)
            mix(0)
            lo_part(dve, BY_VECTOR[0])
            lo(0)
            b_diff(2)
            mix(1)
            lo_part(dve, BY_VECTOR[1])
            lo(1)
            for t in range(T):
                if t + 3 < T:
                    b_diff(t + 3)
                if t + 2 < T:
                    mix(t + 2)
                finish(t)
                if t + 2 < T:
                    lo(t + 2)


def prologue_block(nc, io, per, s):
    with ExitStack() as ctx:
        crow = ctx.enter_context(nc.sbuf_tensor("cond_rows", [2 * KD, P], F32))
        tr = ctx.enter_context(nc.psum_tensor("cond_tr", [P, NB], F32))
        block = ctx.enter_context(nc.Block())
        loads = [(per["ident"][:, :], io["ident"]), (crow[0:KD, :], io["c"].rearrange("b (k p) -> (b k) p", p=P)),
                 (crow[KD:, :], io["c_ctx"].rearrange("(k p) -> k p", p=P)),
                 (per["tri"][:, :, :], io["tri"]), (per["bdmask"][:, :], io["bdmask"]),
                 (per["cosA"][:, :, :], io["ropeA"][0].rearrange("(t p) d -> p t d", p=P)),
                 (per["sinA"][:, :, :], io["ropeA"][1].rearrange("(t p) d -> p t d", p=P)),
                 (per["cosB"][:, :, :], io["ropeB"][0].rearrange("(t p) d -> p t d", p=P)),
                 (per["sinB"][:, :, :], io["ropeB"][1].rearrange("(t p) d -> p t d", p=P))]

        @block.sync
        def _(sp):
            for dst, src in loads:
                sp.dma_start(dst, src).then_inc(s["c_load"], 16)

        @block.vector
        def _(dve):
            dve.memset(per["eps"][:, :], EPS).then_inc(s["c_set"], 1)
            dve.memset(per["gate_w"][:, :], 0.0).then_inc(s["c_set"], 1)
            dve.memset(per["lrT"][2 * RANK:2 * RANK + 1, :], 1.0).then_inc(s["c_set"], 1)
            dve.memset(per["one"][:, :], 1.0).then_inc(s["c_set"], 1)
            dve.wait_ge(s["c_load"], 16 * len(loads))
            dve.tensor_copy(per["ident_r"][:, :], per["ident"][:, :]).then_inc(s["c_set"], 1)
            dve.wait_ge(s["c_set"], 5)

        @block.tensor
        def _(pe):
            pe.wait_ge(s["c_load"], 16 * len(loads))
            pe.transpose(tr[:, 0:2 * KD], crow[:, :], per["ident"][0:2 * KD, 0:2 * KD]).then_inc(s["c_tr"], 1)

        @block.scalar
        def _(act):
            act.wait_ge(s["c_tr"], 1)
            act.activation(per["cond"][:, :, :].rearrange("p k g -> p g k"), tr[:, 0:2 * KD].rearrange("p (g k) -> p g k", g=2),
                           ACT.Silu).then_inc(s["c_silu"], 1)
            act.wait_ge(s["c_silu"], 1)


SEMS = (["c_load", "c_set", "c_tr", "c_silu"]
        + ["m_small", "m_used", "m_tr", "m_dot", "m_exp", "m_dve"] + ["m_hi", "m_lo", "m_evac", "m_turned", "m_cond", "g_post", "g_postT", "g_stored"] + [f"m_w{i}" for i in range(4)]
        + ["p_x0", "p_x1", "p_xn", "p_wlo", "p_whi", "p_zo", "p_ev", "p_turned", "p_h32", "p_hhi", "p_h", "p_acc", "p_wfree",
           "p_sq", "p_std", "p_hss", "p_hstd", "p_rstd", "p_dve"]
        + ["g_zero", "g_st0", "g_chain", "g_new", "g_min", "g_pre", "g_gate", "g_exp", "g_cum", "g_mul", "g_k2t", "g_tr", "g_am",
           "g_at", "g_dsm", "g_ds", "g_oi", "g_o", "g_oc", "g_inter", "g_act", "g_abs", "g_sx", "g_ln", "g_css", "g_cstd", "g_dve", "g_norm", "g_qbd", "g_qt", "g_bwd"]
        + ["a_ones", "a_rawA", "a_rawB", "a_vA", "a_vB", "a_splitA", "a_splitB", "a_pv", "a_pool", "a_work", "a_wkdve", "a_wkact",
           "a_nm", "a_exp", "a_scores", "a_out", "a_own", "a_rs"]
        + ["o_mix", "o_su0", "o_su1", "o_y", "o_x0", "o_x1", "o_st0", "o_st1", "o_wlo", "o_wlo_dve", "o_w0", "o_w1", "o_w2", "o_w3", "o_gp", "o_mlo",
           "o_turned", "o_y1", "o_acc", "o_bss", "o_bstd", "o_mhi", "o_whi", "o_sq", "o_std", "o_dve"]
        + [f"p_w{i}" for i in range(STAGES)] + [f"p_out{i}" for i in range(3)] + [f"p_new{i}" for i in range(3)])


def program(nc, io):
    with ExitStack() as ctx:
        def sb(name, shape, dt=F32):
            return ctx.enter_context(nc.sbuf_tensor(name, shape, dt))

        s = {n: ctx.enter_context(nc.semaphore(n)) for n in SEMS}
        per = {
            "ident": sb("ident", [P, P]), "ident_r": sb("ident_r", [P, P], F32R), "tri": sb("tri", [P, 2, P]), "bdmask": sb("bdmask", [P, C_HEADS]),
            "cosA": sb("cosA", [P, TS, HEAD_DIM]), "sinA": sb("sinA", [P, TS, HEAD_DIM]),
            "cosB": sb("cosB", [P, TS, B_QK]), "sinB": sb("sinB", [P, TS, B_QK]),
            "cond": sb("cond", [P, KD, 2]), "eps": sb("eps", [P, 1]), "one": sb("one", [P, 1]),
            "gains": sb("gains", [P, 4, HEAD_DIM]), "neg_lam": sb("neg_lam", [P, 1]),
            "h_scale": sb("h_scale", [P, 2, KD]), "h_shift": sb("h_shift", [P, 2, KD]), "post": sb("post", [P, 2, KD]),
            "gate_w": sb("gate_w", [2 * RANK + 1, 2 * C_HEADS * C_DK]), "lrT": sb("lrT", [2 * RANK + 1, TOK]),
            "cqT": sb("cqT", [P, TOK]), "ckT": sb("ckT", [P, TOK]), "cv": sb("cv", [P, T, C_HEADS * C_DV]),
        }
        io["Zs"] = nc.dram_tensor("z_scratch", [TOK, Z_COLS], F32).ap()
        io["Us"] = nc.dram_tensor("u_scratch", [TOK, D_MODEL], F32).ap()
        io["Gs"] = nc.dram_tensor("post_scratch", [2, D_MODEL], F32).ap()
        prologue_block(nc, io, per, s)
        with nc.Fori(0, DEPTH) as l:
            with ExitStack() as start:
                f = ProjectionFront(nc, start, l, io, per, s)
                modulation_block(nc, l, io, per, f, s)
                projection_block(nc, l, io, per, f, s)
            with ExitStack() as branch:
                mid = {n: branch.enter_context(nc.sbuf_tensor(n, shape, F32)) for n, shape in (
                    ("oa", [P, T, A_HEADS * HEAD_DIM]), ("ob", [P, 2 * B_HEADS, T, B_V]), ("oc", [P, T, C_HEADS * C_DV]))}
                with ExitStack() as front:
                    att = attention_front(nc, front)
                    gla_block(nc, l, io, per, mid, att, s)
                    attention_block(nc, l, io, per, mid, att, s)
                output_block(nc, l, io, per, mid, s)
            nc.all_engine_barrier(sems_to_clear=range(s[SEMS[4]].num, s[SEMS[-1]].num + 1))


_OUTS = {"y_prompt": (1, SEQ, D_MODEL), "y_sample": (1, DEC_SEQ, D_MODEL),
         "new_a_k": (1, DEPTH, A_KV, SEQ, HEAD_DIM), "new_a_v": (1, DEPTH, A_KV, SEQ, HEAD_DIM),
         "new_b_k": (1, DEPTH, B_HEADS, SEQ, 2 * B_QK), "new_b_v": (1, DEPTH, B_HEADS, SEQ, B_V),
         "new_state_c_fwd": (1, DEPTH, C_HEADS, C_DK, C_DV), "new_state_c_bwd": (1, DEPTH, C_HEADS, C_DK, C_DV)}


def shape_constants():
    import numpy as np

    f = np.float32
    j, i = np.arange(P)[:, None], np.arange(P)[None, :]
    same = j // 64 == i // 64
    tri = np.stack([same & (j <= i), same & (j >= i)], 1).astype(f)
    bd = (np.arange(P)[:, None] // C_DK == np.arange(C_HEADS)[None, :]).astype(f)
    t = np.arange(DEC_SEQ)

    def rope(d):
        half = d // 4
        freq = (f(ROPE_THETA) ** (-np.arange(half, dtype=f) / f(half))).astype(f)
        cos, sin = [], []
        for pos in (t // GRID_W, t % GRID_W):
            ang = pos.astype(f)[:, None] * freq[None, :]
            cos += [np.cos(ang), np.cos(ang)]
            sin += [-np.sin(ang), np.sin(ang)]
        return np.stack([np.concatenate(cos, 1), np.concatenate(sin, 1)]).astype(f)

    lam = np.array([[0.8 - 0.6 * np.exp(-0.3 * l), 0.2 + 0.6 * np.exp(-0.3 * l)] for l in range(DEPTH)], f)
    return {"ident": np.eye(P, dtype=f), "tri": tri, "bdmask": bd, "ropeA": rope(HEAD_DIM), "ropeB": rope(B_QK),
            "lam_consts": lam}


def kernel(**inputs):
    import numpy as np
    import concourse.bacc as bacc
    from concourse.bass_utils import run_bass_kernel_spmd

    nc = bacc.Bacc("TRN2", target_bir_lowering=False, num_devices=1)
    arrays, io = {}, {}
    for name, a in {**inputs, **shape_constants()}.items():
        a = np.ascontiguousarray(a)
        arrays[f"in_{name}"] = a
        io[name] = nc.dram_tensor(f"in_{name}", a.shape, mybir.dt.from_np(a.dtype), kind="ExternalInput").ap()
    for name, shape in _OUTS.items():
        io[name] = nc.dram_tensor(f"out_{name}", shape, F32, kind="ExternalOutput").ap()
    for name in ("x_prompt", "x_sample", "y_prompt", "y_sample"):
        io[name] = io[name].rearrange("b t d -> (b t) d")
    for name in ("new_a_k", "new_a_v", "new_b_k", "new_b_v", "new_state_c_fwd", "new_state_c_bwd",
                 "cache_a_k", "cache_a_v", "cache_b_k", "cache_b_v", "state_c_fwd", "state_c_bwd"):
        io[name] = io[name].rearrange("b l h x y -> (b l) h x y")
    program(nc, io)
    r = run_bass_kernel_spmd(nc, [arrays], core_ids=[0])
    return tuple(r.results[0][f"out_{name}"] for name in _OUTS)
```
